# Optimizing a Trainium2 kernel written in Bass

```python
import math
import jax, jax.numpy as jnp
from jax import lax
import numpy as np

D_MODEL = 1024
BATCH = 1
SEQ = 512
DEPTH = 2

CHUNK = 64
N_A_LAYERS = DEPTH // 2
N_B_LAYERS = DEPTH - N_A_LAYERS
SSM_GROUP = 16
SSM_GROUPS = D_MODEL // SSM_GROUP
SSM_STATE = 64
N_HEADS = 16
HEAD_DIM = D_MODEL // N_HEADS
Q_BLOCK = 128
PEER_HEADS = 8
PEER_NKEYS = 128
PEER_EXPERTS = PEER_NKEYS * PEER_NKEYS
PEER_TOPK = 16
PEER_QDIM = 256
PEER_TOK_BLOCK = 128
PLE_DIM = 256
ALPHA = (2 * DEPTH) ** 0.25
BETA = (8 * DEPTH) ** -0.25
LN_EPS = 1e-5

kernel_name = "yoco_s5_stickbreak_peer_trunk"

def layer_norm(h, g, b):
    hf = h.astype(jnp.float32)
    mu = jnp.mean(hf, axis=-1, keepdims=True)
    var = jnp.mean(jnp.square(hf - mu), axis=-1, keepdims=True)
    y = (hf - mu) * lax.rsqrt(var + LN_EPS)
    return (y * g.astype(jnp.float32) + b.astype(jnp.float32)).astype(h.dtype)

def s5_mixer(h, w_in, lam_re, lam_im, log_dt, b_re, b_im, c_re, c_im, d_skip, w_glu):
    bsz, seq, _ = h.shape
    f32 = jnp.float32
    u = (h @ w_in).astype(f32)
    ug = u.reshape(bsz, seq, SSM_GROUPS, SSM_GROUP)
    lam = lax.complex(lam_re.astype(f32), lam_im.astype(f32))
    dt = jnp.exp(log_dt.astype(f32))[:, None]
    a_bar = jnp.exp(lam * dt)
    b_cplx = lax.complex(b_re.astype(f32), b_im.astype(f32))
    b_bar = ((a_bar - 1.0) / lam)[..., None] * b_cplx
    bu = lax.complex(jnp.einsum('bsgc,gpc->bsgp', ug, jnp.real(b_bar)),
                     jnp.einsum('bsgc,gpc->bsgp', ug, jnp.imag(b_bar)))
    a_seq = jnp.broadcast_to(a_bar[None, None], (1, seq, SSM_GROUPS, SSM_STATE))

    def combine(left, right):
        a_l, b_l = left
        a_r, b_r = right
        return a_l * a_r, a_r * b_l + b_r

    _, states = lax.associative_scan(combine, (a_seq, bu), axis=1)
    y = (jnp.einsum('bsgp,gcp->bsgc', jnp.real(states), c_re.astype(f32))
         - jnp.einsum('bsgp,gcp->bsgc', jnp.imag(states), c_im.astype(f32)))
    y = y.reshape(bsz, seq, D_MODEL) + d_skip.astype(f32) * u
    y = jax.nn.gelu(y).astype(h.dtype)
    val, gate = jnp.split(y @ w_glu, 2, axis=-1)
    return val * jax.nn.sigmoid(gate)

def shared_kv(h, g, b, w_kv):
    bsz, seq, _ = h.shape
    k, v = jnp.split(layer_norm(h, g, b) @ w_kv, 2, axis=-1)
    return (k.reshape(bsz, seq, N_HEADS, HEAD_DIM), v.reshape(bsz, seq, N_HEADS, HEAD_DIM))

def stick_breaking_mixer(h, w_q, w_o, k, v):
    bsz, seq, _ = h.shape
    q = (h @ w_q).reshape(bsz, seq, N_HEADS, HEAD_DIM)
    scale = HEAD_DIM ** -0.5
    outs = []
    for blk in range(seq // Q_BLOCK):
        t0 = blk * Q_BLOCK
        t1 = t0 + Q_BLOCK
        qb, kb, vb = q[:, t0:t1], k[:, :t1], v[:, :t1]
        z = jnp.einsum('bqhd,bkhd->bhqk', qb, kb).astype(jnp.float32) * scale
        mask = jnp.arange(t1)[None, :] < jnp.arange(t0, t1)[:, None]
        log_keep = jnp.where(mask, jax.nn.log_sigmoid(-z), 0.0)
        later = lax.cumsum(log_keep, axis=3, reverse=True) - log_keep
        w = jnp.where(mask, jnp.exp(jax.nn.log_sigmoid(z) + later), 0.0)
        outs.append(jnp.einsum('bhqk,bkhd->bqhd', w.astype(vb.dtype), vb))
    o = jnp.concatenate(outs, axis=1).reshape(bsz, seq, D_MODEL)
    return o @ w_o

def peer_ffn(h, w_q, k1, k2, u_tab, v_tab):
    bsz, seq, _ = h.shape
    n_tok = bsz * seq
    xt = h.reshape(n_tok, D_MODEL)
    q = (xt @ w_q).reshape(n_tok, PEER_HEADS, PEER_QDIM).astype(jnp.float32)
    q1, q2 = jnp.split(q, 2, axis=-1)
    s1 = jnp.einsum('thd,nd->thn', q1, k1.astype(jnp.float32))
    s2 = jnp.einsum('thd,nd->thn', q2, k2.astype(jnp.float32))
    v1, i1 = lax.top_k(s1, PEER_TOPK)
    v2, i2 = lax.top_k(s2, PEER_TOPK)
    cand = (v1[..., :, None] + v2[..., None, :]).reshape(n_tok, PEER_HEADS, PEER_TOPK * PEER_TOPK)
    sc, ci = lax.top_k(cand, PEER_TOPK)
    e1 = jnp.take_along_axis(i1, ci // PEER_TOPK, axis=-1)
    e2 = jnp.take_along_axis(i2, ci % PEER_TOPK, axis=-1)
    idx = e1 * PEER_NKEYS + e2
    gates = jax.nn.softmax(sc, axis=-1)
    n_blk = n_tok // PEER_TOK_BLOCK

    def block(args):
        xb, ib, gb = args
        act = jnp.einsum('td,thkd->thk', xb, u_tab[ib]).astype(jnp.float32)
        wgt = (gb * jax.nn.gelu(act)).astype(xb.dtype)
        return jnp.einsum('thk,thkd->td', wgt, v_tab[ib])

    out = lax.map(block, (xt.reshape(n_blk, PEER_TOK_BLOCK, D_MODEL),
                          idx.reshape(n_blk, PEER_TOK_BLOCK, PEER_HEADS, PEER_TOPK),
                          gates.reshape(n_blk, PEER_TOK_BLOCK, PEER_HEADS, PEER_TOPK)))
    return out.reshape(bsz, seq, D_MODEL).astype(h.dtype)

def setup_inputs(seed: int = 0) -> dict:
    key = jax.random.key(seed)
    ks = jax.random.split(key, 32)
    f32 = jnp.float32

    def nrm(k, shape, std):
        return std * jax.random.normal(k, shape, f32)

    D, G, P = D_MODEL, SSM_GROUPS, SSM_STATE
    x = nrm(ks[0], (BATCH, SEQ, D), 1.0)
    p = nrm(ks[1], (DEPTH, BATCH, SEQ, PLE_DIM), 1.0)
    ln_mix_g = 1.0 + nrm(ks[2], (DEPTH, D), 0.02)
    ln_mix_b = nrm(ks[3], (DEPTH, D), 0.02)
    ln_ffn_g = 1.0 + nrm(ks[4], (DEPTH, D), 0.02)
    ln_ffn_b = nrm(ks[5], (DEPTH, D), 0.02)
    ssm_w_in = nrm(ks[6], (N_A_LAYERS, D, D), D ** -0.5)
    ssm_lam_re = -0.5 * jnp.exp(nrm(ks[7], (N_A_LAYERS, G, P), 0.01))
    ssm_lam_im = math.pi * jnp.arange(P, dtype=f32)[None, None, :] + nrm(ks[8], (N_A_LAYERS, G, P), 0.01)
    ssm_log_dt = jax.random.uniform(ks[9], (N_A_LAYERS, G), f32, math.log(1e-3), math.log(1e-1))
    ssm_b_re = nrm(ks[10], (N_A_LAYERS, G, P, SSM_GROUP), (2 * SSM_GROUP) ** -0.5)
    ssm_b_im = nrm(ks[11], (N_A_LAYERS, G, P, SSM_GROUP), (2 * SSM_GROUP) ** -0.5)
    ssm_c_re = nrm(ks[12], (N_A_LAYERS, G, SSM_GROUP, P), P ** -0.5)
    ssm_c_im = nrm(ks[13], (N_A_LAYERS, G, SSM_GROUP, P), P ** -0.5)
    ssm_d = nrm(ks[14], (N_A_LAYERS, D), 1.0)
    ssm_w_glu = jnp.concatenate([nrm(ks[15], (N_A_LAYERS, D, D), BETA * D ** -0.5),
                                 nrm(ks[16], (N_A_LAYERS, D, D), D ** -0.5)], axis=-1)
    kv_ln_g = 1.0 + nrm(ks[17], (D,), 0.02)
    kv_ln_b = nrm(ks[18], (D,), 0.02)
    w_kv = jnp.concatenate([nrm(ks[19], (D, D), D ** -0.5),
                            nrm(ks[20], (D, D), BETA * D ** -0.5)], axis=-1)
    sb_w_q = nrm(ks[21], (N_B_LAYERS, D, D), D ** -0.5)
    sb_w_o = nrm(ks[22], (N_B_LAYERS, D, D), BETA * D ** -0.5)
    peer_w_q = nrm(ks[23], (DEPTH, D, PEER_HEADS * PEER_QDIM), D ** -0.5)
    peer_k1 = nrm(ks[24], (DEPTH, PEER_NKEYS, PEER_QDIM // 2), (PEER_QDIM // 2) ** -0.5)
    peer_k2 = nrm(ks[25], (DEPTH, PEER_NKEYS, PEER_QDIM // 2), (PEER_QDIM // 2) ** -0.5)
    peer_u = nrm(ks[26], (DEPTH, PEER_EXPERTS, D), D ** -0.5)
    peer_v = nrm(ks[27], (DEPTH, PEER_EXPERTS, D), BETA)
    ple_w = nrm(ks[28], (DEPTH, PLE_DIM, D), PLE_DIM ** -0.5)
    ple_gate = nrm(ks[29], (DEPTH, D, D), D ** -0.5)
    return {"x": x, "p": p, "ln_mix_g": ln_mix_g, "ln_mix_b": ln_mix_b,
            "ln_ffn_g": ln_ffn_g, "ln_ffn_b": ln_ffn_b, "ssm_w_in": ssm_w_in,
            "ssm_lam_re": ssm_lam_re, "ssm_lam_im": ssm_lam_im, "ssm_log_dt": ssm_log_dt,
            "ssm_b_re": ssm_b_re, "ssm_b_im": ssm_b_im, "ssm_c_re": ssm_c_re,
            "ssm_c_im": ssm_c_im, "ssm_d": ssm_d, "ssm_w_glu": ssm_w_glu,
            "kv_ln_g": kv_ln_g, "kv_ln_b": kv_ln_b, "w_kv": w_kv,
            "sb_w_q": sb_w_q, "sb_w_o": sb_w_o, "peer_w_q": peer_w_q,
            "peer_k1": peer_k1, "peer_k2": peer_k2, "peer_u": peer_u, "peer_v": peer_v,
            "ple_w": ple_w, "ple_gate": ple_gate}

def reference(x, p, ln_mix_g, ln_mix_b, ln_ffn_g, ln_ffn_b, ssm_w_in, ssm_lam_re, ssm_lam_im,
              ssm_log_dt, ssm_b_re, ssm_b_im, ssm_c_re, ssm_c_im, ssm_d, ssm_w_glu,
              kv_ln_g, kv_ln_b, w_kv, sb_w_q, sb_w_o, peer_w_q, peer_k1, peer_k2,
              peer_u, peer_v, ple_w, ple_gate):
    h = x
    k_sh = None
    v_sh = None
    for i in range(DEPTH):
        if i < N_A_LAYERS:
            mix = s5_mixer(h, ssm_w_in[i], ssm_lam_re[i], ssm_lam_im[i], ssm_log_dt[i],
                           ssm_b_re[i], ssm_b_im[i], ssm_c_re[i], ssm_c_im[i],
                           ssm_d[i], ssm_w_glu[i])
        else:
            if i == N_A_LAYERS:
                k_sh, v_sh = shared_kv(h, kv_ln_g, kv_ln_b, w_kv)
            j = i - N_A_LAYERS
            mix = stick_breaking_mixer(h, sb_w_q[j], sb_w_o[j], k_sh, v_sh)
        h = layer_norm(ALPHA * h + mix, ln_mix_g[i], ln_mix_b[i])
        ffn = peer_ffn(h, peer_w_q[i], peer_k1[i], peer_k2[i], peer_u[i], peer_v[i])
        h = layer_norm(ALPHA * h + ffn, ln_ffn_g[i], ln_ffn_b[i])
        h = h + jax.nn.sigmoid(h @ ple_gate[i]) * (p[i] @ ple_w[i])
    return h


_drawn_inputs = setup_inputs


def setup_inputs(seed=0):
    import zlib

    import numpy as np

    out = dict(_drawn_inputs(seed))
    spreads = {}
    factors = {'ssm_lam_re': 8.0, 'kv_ln_g': 6.69, 'kv_ln_b': 6.206}
    for name, (base, spread) in spreads.items():
        noise = np.random.default_rng([zlib.crc32(name.encode()), seed]).standard_normal(out[name].shape)
        drawn = base * np.exp(spread * noise) if base else spread * noise
        out[name] = __import__('jax').numpy.asarray(drawn.astype(out[name].dtype))
    for name, factor in factors.items():
        out[name] = (out[name] * factor).astype(out[name].dtype)
    return out
```

```python
import math
from contextlib import ExitStack, contextmanager

import numpy as np
import concourse.bass as bass
from concourse import mybir

ALU = mybir.AluOpType
ACT = mybir.ActivationFunctionType
AX_X = mybir.AxisListType.X
F32 = mybir.dt.float32
U32 = mybir.dt.uint32

P = 128
D = 1024
T = 512
DEPTH = 2
KC = D // P
TB = T // P
HALF = 512
CHB = 4
GROUP = 16
PAIRS = D // (2 * GROUP)
LEVELS = 9
HEADS = 16
HD = D // HEADS
PH = 8
NKEYS = 128
EXPERTS = NKEYS * NKEYS
TOPK = 16
SLOTS = PH * TOPK
RING = 8
TURN = 2 * RING
PLE = 256
ALPHA = (2 * DEPTH) ** 0.25
LN_EPS = 1e-5
LOWEST = -3.0e38
MASKED = -1.0e30
ARENA = 29500
WSLOTS = 3
ROUND = 1.5 * 2.0 ** 23
TWO_PI_HI = 6.28125
TWO_PI_LO = 2 * math.pi - TWO_PI_HI
PI_BELOW = 3.1415925
STATE_ORDER = ("x", "xT", "lam_re", "lam_im", "log_dt", "b_re", "b_im", "c_re", "c_im", "d_skip")


class Steps:

    def __init__(self, eng, sem):
        self.eng, self.sem, self.base, self.n = eng, sem, 0, 0

    def did(self, ins):
        ins.then_inc(self.sem, 1)
        self.n += 1

    def settle(self):
        self.eng.wait_ge(self.sem, self.base + self.n)

    @contextmanager
    def loop(self, trips, per_trip):
        with self.eng.Fori(0, trips) as i:
            start = self.base + self.n
            self.base, self.n = i * per_trip + start, 0
            yield i
            assert self.n == per_trip, (self.n, per_trip)
        self.base, self.n = start + trips * per_trip, 0


def first(n):
    return isinstance(n, int) and n == 0


def build(nc, a, out):
    ctx = ExitStack()
    with ctx:
        def sb(name, cols, dt=F32):
            return ctx.enter_context(nc.sbuf_tensor(name, [P, cols], dt))

        def sem(name):
            return ctx.enter_context(nc.semaphore(name))

        ps = ctx.enter_context(nc.psum_tensor("ps", [P, 8, HALF], F32))

        def bank(n):
            return ps[:, n, :]

        h = sb("h", TB * D)
        hT = sb("hT", KC * T)
        wring = sb("wring", WSLOTS * KC * HALF)
        ident = sb("ident", P)
        lnp = sb("lnp", 2 * D)
        stat = sb("stat", TB * 12)
        mv = sb("mv", TB * 2)
        rstd = sb("rstd", TB)
        arena = sb("arena", ARENA)
        here = [0]

        def reg_wait(eng, semaphore, value):
            value = eng.to_reg(value)
            eng.wait_ge(s["const_set"], 9)
            eng.wait_ge(semaphore, value)

        def place(cols, at=None):
            if at is not None:
                here[0] = at
            v = arena[:, here[0]:here[0] + cols]
            here[0] += cols
            assert here[0] <= ARENA, here[0]
            return v

        def hb(tb, n0=None):
            return h[:, tb * D:(tb + 1) * D] if n0 is None else h[:, tb * D + n0 * HALF:tb * D + (n0 + 1) * HALF]

        def hT_at(k, tb=None):
            return hT[:, k * T:(k + 1) * T] if tb is None else hT[:, k * T + tb * P:k * T + (tb + 1) * P]

        def w_at(slot, k, c0=0, c1=HALF):
            o = (slot * KC + k) * HALF
            return wring[:, o + c0:o + c1]

        yT = place(KC * T, 0)
        tab = [[place(CHB * T) for _ in range(2)] for _ in range(2)]
        ptmp = [place(CHB * T // 2) for _ in range(2)]
        rot = [place(T) for _ in range(4)]
        vin = [place(T) for _ in range(2)]
        sc_r = [place(T) for _ in range(2)]
        prod = [[place(T) for _ in range(4)] for _ in range(2)]
        ub = [place(T) for _ in range(2)]
        win = [place(D) for _ in range(2)]
        braw = [[place(CHB * GROUP) for _ in range(2)] for _ in range(2)]
        bmul = [place(CHB * GROUP) for _ in range(4)]
        bbd = [[place(P) for _ in range(2)] for _ in range(2)]
        bT = [[place(P) for _ in range(2)] for _ in range(2)]
        cbd = [[place(P) for _ in range(2)] for _ in range(2)]
        dgD = [place(P) for _ in range(2)]
        dsk = place(KC)
        par = {n: place(PAIRS) for n in ("lr", "li", "dt", "t0", "t1", "t2", "rho", "th", "c", "s", "fr", "fi")}
        wc = place(LEVELS * PAIRS)
        ws = place(LEVELS * PAIRS)
        e0 = [place(PAIRS) for _ in range(2)]
        sgm = [place(HALF, KC * T + 2048 * q) for q in range(2)]

        s = {n: sem(n) for n in (
            "const_set", "dve_step", "pool_step", "act_step", "xT_in", "h_in", "par_in", "win_in0", "win_in1",
            "u_full", "u_copied", "bbar_set", "bt_full", "bt_copied", "tables_set", "bu_full", "bu_read",
            "prods_set", "pair_done", "y_taken", "sin_done", "trig_set",
            "w_in0", "w_in1", "w_in2", "w_used", "lin_full", "lin_free", "gate_sig", "ln_in", "ln_used",
            "var_set", "std_set", "h_set", "hT_copied", "out_done")}

        for n in ("tri_set", "lnp_free", "ffn_read", "k_in", "ple_in", "scores_full", "scores_read", "cand_gap", "gap_exp", "idx_set",
                  "u_used", "v_used", "gelu_set", "diag_set", "ffn_full", "z_full", "z_exp", "soft_set",
                  "sum_full", "weights_set", "o_full", "o_copied", "ple_free", "q_copied", "pool_staged", "gates_set", "act_seen"):
            s[n] = sem(n)
        u_in = [sem(f"u_in{r}") for r in range(RING)]
        v_in = [sem(f"v_in{r}") for r in range(RING)]

        idx = place(TB * SLOTS, 0).bitcast(U32)
        gates = place(TB * SLOTS)
        stage_idx = place(2 * RING).bitcast(U32)
        actv = place(TURN)
        gelu = place(TURN)
        gg = place(TURN)
        diag = [place(P) for _ in range(RING)]
        zrow = place(HALF)
        plw = place(2 * D)
        pTs = place(2 * T)
        rings_at = here[0]
        u_ring = [place(D) for _ in range(RING)]
        v_ring = [place(D) for _ in range(RING)]
        q_sb = [place(T, rings_at + n * T if n == 0 else None) for n in range(8)]
        k12 = [place(NKEYS) for _ in range(2)]
        val = [place(TB * TOPK) for _ in range(2)]
        key = [place(TB * SLOTS) for _ in range(2)]
        rest = [place(NKEYS) for _ in range(2 * TB)]
        cand = [place(TOPK * TOPK) for _ in range(TB)]
        cand2 = [place(TOPK * TOPK) for _ in range(TB)]
        best = place(TB * SLOTS)
        bpos = place(TB * SLOTS)
        ksel = [place(TB * SLOTS) for _ in range(2)]
        iota16 = place(TOPK)
        eq = [place(SLOTS * TOPK) for _ in range(2)]
        esel = [place(SLOTS) for _ in range(2)]
        rsum = place(TB * PH)
        rinv = place(TB * PH)
        sgp = [place(HALF, rings_at + q * HALF) for q in range(2)]

        hk = place(TB * D, 0)
        hkT = place(KC * T)
        KT = place(KC * T)
        QT = place(KC * T)
        V = hk
        oT = place(KC * T)
        ZW = 1280
        ez = [place(ZW) for _ in range(2)]
        sp_ = [place(ZW) for _ in range(2)]
        wT = [place(ZW) for _ in range(2)]
        ntri = place(P)
        nones = place(P)
        seen = place(2 * P)
        hide = place(P)
        STRIP = {0: 0, 3: 512, 1: 640, 2: 1024}

        block = ctx.enter_context(nc.Block())
        w_plan = []
        loads = {}

        def piece(name, ap, c0):
            w_plan.append(ap[:, c0:c0 + HALF].rearrange("(k p) n -> p k n", p=P))
            return len(w_plan) - 1

        glu = [piece("val", a["w_glu"], n0 * HALF) if g == 0 else piece("gate", a["w_glu"], D + n0 * HALF)
               for n0 in range(2) for g in range(2)]
        w_q1 = [[], []]
        w_pg = [[], []]
        w_k = w_v = w_qq = w_oo = None
        for l in range(DEPTH):
            if l == 1:
                w_k = [piece("k", a["w_kv"], n0 * HALF) for n0 in range(2)]
                w_v = [piece("v", a["w_kv"], D + n0 * HALF) for n0 in range(2)]
                w_qq = [piece("q", a["w_q"], n0 * HALF) for n0 in range(2)]
                w_oo = [piece("o", a["w_o"], n0 * HALF) for n0 in range(2)]
            w_q1[l] = [piece("pq", a["peer_w_q"][l * D:(l + 1) * D, :], c * HALF) for c in range(4)]
            w_pg[l] = [piece("pg", a["ple_gate"][l * D:(l + 1) * D, :], n0 * HALF) for n0 in range(2)]
        H_AFTER = [TB, 2 * TB, 4 * TB, 5 * TB, 6 * TB]
        LN_ORDER = [("ln_mix", 0), ("ln_ffn", 0), ("kv", 0), ("ln_mix", 1), ("ln_ffn", 1)]

        @block.sync
        def _(sp):
            sp.dma_start(hT[:, :].rearrange("p (k t) -> p k t", k=KC),
                         a["xT"].rearrange("(k p) t -> p k t", p=P)).then_inc(s["xT_in"], 16)
            for n, key in (("lr", "lam_re"), ("li", "lam_im")):
                sp.dma_start(par[n], a[key]).then_inc(s["par_in"], 16)
            for g in range(2):
                sp.dma_start(par["dt"][64 * g:64 * g + 64, :],
                             a["log_dt"][g:g + 1, :].to_broadcast([64, PAIRS])).then_inc(s["par_in"], 16)
            sp.dma_start(dsk, a["d_skip"]).then_inc(s["par_in"], 16)

            def pre(b, q, turn):
                if not first(turn):
                    sp.wait_ge(s["pair_done"], (b - 1) * CHB)
                sp.dma_start(win[q].rearrange("p (k n) -> p k n", k=KC),
                             a["w_in"][:, bass.ds(b * P, P)].rearrange("(k p) n -> p k n", p=P)).then_inc(s[f"win_in{q}"], 16)
                for r, (bn, cn) in enumerate((("b_re", "c_re"), ("b_im", "c_im"))):
                    sp.dma_start(braw[q][r], a[bn][:, bass.ds(b * CHB * GROUP, CHB * GROUP)]).then_inc(s[f"win_in{q}"], 16)
                    for g in range(2):
                        sp.dma_start(cbd[q][r][64 * g:64 * g + 64, :].rearrange("p (j c) -> p j c", j=CHB)[:, :, GROUP * g:GROUP * g + GROUP],
                                     a[cn][64 * g:64 * g + 64, bass.ds(b * CHB * GROUP, CHB * GROUP)].rearrange(
                                         "p (j c) -> p j c", j=CHB)).then_inc(s[f"win_in{q}"], 16)

            sp.wait_ge(s["const_set"], 9)
            pre(0, 0, 0)
            pre(1, 1, 0)
            sp.dma_start(h[:, :].rearrange("p (b d) -> p b d", b=TB),
                         a["x"].rearrange("(b p) d -> p b d", p=P)).then_inc(s["h_in"], 16)
            for n in range(2):
                sp.dma_start(lnp[:, n * D:(n + 1) * D], a[("ln_mix_g", "ln_mix_b")[n]][0:1, :].to_broadcast([P, D])).then_inc(s["ln_in"], 16)

            def load_piece(n, src):
                slot = n % WSLOTS
                sp.dma_start(wring[:, slot * KC * HALF:(slot + 1) * KC * HALF].rearrange("p (k n) -> p k n", k=KC),
                             src).then_inc(s[f"w_in{slot}"], 16)

            for n in range(WSLOTS):
                load_piece(n, w_plan[n])
            with sp.Fori(0, KC // 2 - 1) as it:
                pre(2 * it + 2, 0, it + 1)
                pre(2 * it + 3, 1, it + 1)
            def load_ln(n):
                name, l = LN_ORDER[n]
                sp.wait_ge(s["lnp_free"], n)
                for m, x in enumerate("gb"):
                    sp.dma_start(lnp[:, m * D:(m + 1) * D],
                                 a[f"{name}_{x}"][l:l + 1, :].to_broadcast([P, D])).then_inc(s["ln_in"], 16)

            for n in range(WSLOTS, len(w_plan)):
                sp.wait_ge(s["w_used"], n - WSLOTS + 1)
                load_piece(n, w_plan[n])
                for l in range(DEPTH):
                    if n == w_q1[l][0]:
                        sp.wait_ge(s["h_set"], (1 if l == 0 else 5) * TB)
                        for m, x in enumerate(("k1T", "k2T")):
                            sp.dma_start(k12[m], a[x][l * P:(l + 1) * P, :]).then_inc(s["k_in"], 16)
                        sp.dma_start(plw.rearrange("p (k n) -> p k n", k=2),
                                     a["ple_w"][l * PLE:(l + 1) * PLE, :].rearrange("(k p) n -> p k n", p=P)).then_inc(s["ple_in"], 16)
                        sp.dma_start(pTs.rearrange("p (k n) -> p k n", k=2),
                                     a["pT"][l].rearrange("(k p) n -> p k n", p=P)).then_inc(s["ple_in"], 16)
                        load_ln(1 if l == 0 else 4)
                if n == w_pg[0][1]:
                    load_ln(2)
                if n == w_qq[0]:
                    load_ln(3)

        @block.gpsimd
        def _(pool):
            step = Steps(pool, s["pool_step"])
            step.did(pool.memset(ident[:, :], 0.0))
            for q in range(2):
                for r in range(2):
                    pool.memset(bbd[q][r], 0.0).then_inc(s["const_set"], 1)
                    pool.memset(cbd[q][r], 0.0).then_inc(s["const_set"], 1)
            step.settle()
            pool.affine_select(out=ident[:, :], in_=ident[:, :], compare_op=ALU.not_equal, fill=1.0, base=0,
                               pattern=[[-1, P]], channel_multiplier=1).then_inc(s["const_set"], 1)

            def tables(b, q, turn):
                if not first(turn):
                    pool.wait_ge(s["prods_set"], (b - 1) * CHB)
                if not first(b):
                    pool.wait_ge(s["tables_set"], 2 * b)
                c, sn = (tab[q][r].rearrange("p (j t) -> p j t", j=CHB) for r in range(2))
                tm = [ptmp[r].rearrange("p (j t) -> p j t", j=CHB) for r in range(2)]
                for lv in range(LEVELS):
                    n = 1 << lv
                    wcb = wc[:, bass.ds(lv * PAIRS + b * CHB, CHB)].unsqueeze(2).to_broadcast([P, CHB, n])
                    wsb = ws[:, bass.ds(lv * PAIRS + b * CHB, CHB)].unsqueeze(2).to_broadcast([P, CHB, n])
                    step.settle()
                    step.did(pool.tensor_tensor(c[:, :, n:2 * n], c[:, :, 0:n], wcb, ALU.mult))
                    step.did(pool.tensor_tensor(tm[0][:, :, 0:n], sn[:, :, 0:n], wsb, ALU.mult))
                    step.did(pool.tensor_tensor(sn[:, :, n:2 * n], sn[:, :, 0:n], wcb, ALU.mult))
                    step.did(pool.tensor_tensor(tm[1][:, :, 0:n], c[:, :, 0:n], wsb, ALU.mult))
                    step.settle()
                    i0 = pool.tensor_tensor(c[:, :, n:2 * n], c[:, :, n:2 * n], tm[0][:, :, 0:n], ALU.subtract)
                    i1 = pool.tensor_tensor(sn[:, :, n:2 * n], sn[:, :, n:2 * n], tm[1][:, :, 0:n], ALU.add)
                    if lv < LEVELS - 1:
                        step.did(i0)
                        step.did(i1)
                    else:
                        i0.then_inc(s["tables_set"], 1)
                        i1.then_inc(s["tables_set"], 1)

            for q in range(2):
                for r in range(2):
                    step.did(pool.memset(tab[q][r].rearrange("p (j t) -> p j t", j=CHB)[:, :, 0:1], 1.0 - r))
            pool.wait_ge(s["trig_set"], 1)
            tables(0, 0, 0)
            tables(1, 1, 0)
            with step.loop(KC // 2 - 1, 2 * (6 * LEVELS - 2)) as it:
                tables(2 * it + 2, 0, it + 1)
                tables(2 * it + 3, 1, it + 1)

            def gather(l, tb):
                done = (l * TB + tb) * SLOTS
                pool.wait_ge(s["idx_set"], l + 1)
                with step.loop(SLOTS // TURN, 2) as j:
                    for half in range(2):
                        mine = stage_idx[:, half * RING:(half + 1) * RING]
                        step.did(pool.tensor_copy(mine, idx[:, bass.ds(j * TURN + (tb * SLOTS + half * RING), RING)]))
                        reg_wait(pool, s["pool_step"], step.base + step.n)
                        for g in range(2):
                            n = done + half * RING + 4 * g + 4
                            reg_wait(pool, s["u_used"], j * TURN + n)
                            for r in range(4 * g, 4 * g + 4):
                                pool.indirect_dma_start(u_ring[r], None, a["peer_u"][:, :],
                                                        bass.IndirectOffsetOnAxis(mine[:, r:r + 1], 0)).then_inc(u_in[r], 16)
                            reg_wait(pool, s["v_used"], j * TURN + n)
                            for r in range(4 * g, 4 * g + 4):
                                pool.indirect_dma_start(v_ring[r], None, a["peer_v"][:, :],
                                                        bass.IndirectOffsetOnAxis(mine[:, r:r + 1], 0)).then_inc(v_in[r], 16)

            for l in range(DEPTH):
                if l == 0:
                    pool.wait_ge(s["h_set"], TB)
                    pool.iota(iota16.bitcast(U32), pattern=[[1, TOPK]], base=0, channel_multiplier=0).then_inc(s["tri_set"], 1)
                    pool.memset(zrow, 0.0).then_inc(s["tri_set"], 1)
                else:
                    pool.wait_ge(s["h_set"], 3 * TB)
                    pool.memset(ntri, -1.0).then_inc(s["tri_set"], 1)
                    pool.memset(nones, -1.0).then_inc(s["tri_set"], 1)
                    pool.memset(seen, 1.0).then_inc(s["tri_set"], 1)
                    pool.memset(hide, 0.0).then_inc(s["tri_set"], 1)
                    pool.wait_ge(s["tri_set"], 6)
                    pool.affine_select(out=ntri, in_=ntri, compare_op=ALU.is_ge, fill=0.0, base=0,
                                       pattern=[[-1, P]], channel_multiplier=1).then_inc(s["tri_set"], 1)
                    sv = seen.rearrange("p (e q) -> p e q", e=2)
                    pool.affine_select(out=sv, in_=sv, compare_op=ALU.is_gt, fill=0.0, base=0,
                                       pattern=[[0, 2], [1, P]], channel_multiplier=-1).then_inc(s["tri_set"], 1)
                    pool.affine_select(out=hide, in_=hide, compare_op=ALU.is_gt, fill=MASKED, base=0,
                                       pattern=[[1, P]], channel_multiplier=-1).then_inc(s["tri_set"], 1)
                    pool.wait_ge(s["h_set"], 5 * TB)
                    pool.iota(iota16.bitcast(U32), pattern=[[1, TOPK]], base=0, channel_multiplier=0).then_inc(s["tri_set"], 1)
                    pool.memset(zrow, 0.0).then_inc(s["tri_set"], 1)
                for tb in range(TB):
                    gather(l, tb)

        @block.scalar
        def _(act):
            step = Steps(act, s["act_step"])
            act.wait_ge(s["par_in"], 80)
            act.sem_inc(s["y_taken"], 1)
            act.activation(par["dt"], par["dt"], ACT.Exp).then_inc(s["sin_done"], 1)
            act.wait_ge(s["dve_step"], 1)
            act.activation(par["rho"], par["t0"], ACT.Exp).then_inc(s["sin_done"], 1)
            act.wait_ge(s["dve_step"], 7)
            act.activation(par["s"], par["th"], ACT.Sin).then_inc(s["sin_done"], 1)
            act.activation(par["t1"], par["th"], ACT.Sin, scale=0.5).then_inc(s["sin_done"], 1)

            def pre(b, q, turn):
                act.wait_ge(s["u_full"], b + 1)
                if not first(turn):
                    act.wait_ge(s["pair_done"], (b - 1) * CHB)
                act.copy(ub[q], bank(6 + q)).then_inc(s["u_copied"], 1)
                act.wait_ge(s["bt_full"], b + 1)
                for r in range(2):
                    act.copy(bT[q][r], ps[:, 6 + q, r * P:(r + 1) * P]).then_inc(s["bt_copied"], 1)

            def main(b, q):
                act.wait_ge(s["pair_done"], b * CHB + CHB)
                act.activation(yT[:, bass.ds(b * T, T)], bank(4 + q), ACT.Gelu_apprx_tanh).then_inc(s["y_taken"], 1)

            pre(0, 0, 0)
            pre(1, 1, 0)
            main(0, 0)
            with act.Fori(0, KC // 2 - 1) as it:
                pre(2 * it + 2, 0, it + 1)
                main(2 * it + 1, 1)
                pre(2 * it + 3, 1, it + 1)
                main(2 * it + 2, 0)
            main(KC - 1, 1)

            for n in range(2 * TB):
                act.wait_ge(s["lin_full"], 2 * (n + 1))
                if n >= 2:
                    act.wait_ge(s["lin_free"], 2 * (n - 1))
                act.activation(sgm[n % 2], bank((2 * n + 1) % 4), ACT.Sigmoid).then_inc(s["gate_sig"], 1)
            lin = [4 * TB]
            lns = [0]

            def root():
                lns[0] += 1
                act.wait_ge(s["var_set"], lns[0])
                act.activation(rstd[:, :], rstd[:, :], ACT.Sqrt).then_inc(s["std_set"], 1)

            def evacuate(dst, scale=None, **more):
                lin[0] += 1
                act.wait_ge(s["lin_full"], lin[0])
                n = (lin[0] - 1) % 4
                src = bank(n)
                if more:
                    src = src.rearrange("p (k t) -> p k t", k=4)
                if scale is None:
                    act.copy(dst, src).then_inc(s["lin_free"], 1)
                else:
                    act.mul(dst, src, scale).then_inc(s["lin_free"], 1)

            def turned(dst):
                for tb in range(TB):
                    for q in range(2):
                        evacuate(dst[:, q * 4 * T:(q + 1) * 4 * T].rearrange("p (k t) -> p k t", k=4)[:, :, tb * P:(tb + 1) * P],
                                 strided=True)

            def route(l):
                for n in range(4 * 4):
                    evacuate(q_sb[n % 8])
                act.wait_ge(s["cand_gap"], l + 1)
                act.activation(gates, gates, ACT.Exp).then_inc(s["gap_exp"], 1)

            def experts(l, tb):
                done = (l * TB + tb) * SLOTS
                with step.loop(SLOTS // TURN, TURN // 4 * 5) as j:
                    for g in range(0, TURN, 4):
                        act.wait_ge(s["u_used"], j * TURN + (done + RING + g + 4))
                        step.did(act.activation(gelu[:, g:g + 4], actv[:, g:g + 4], ACT.Gelu_apprx_tanh))
                        reg_wait(act, s["act_step"], step.base + step.n)
                        for r in range(g, g + 4):
                            step.did(act.activation(gg[:, r:r + 1], gates[:, bass.ds(j * TURN + (tb * SLOTS + r), 1)], ACT.Copy,
                                                    scale=gelu[:, r:r + 1]))
                        step.settle()
                        act.wait_ge(s["v_used"], j * TURN + (done + g + 4))
                        for r in range(g, g + 4):
                            act.activation(diag[r % RING], ident[:, :], ACT.Copy, scale=gg[:, r:r + 1]).then_inc(s["diag_set"], 1)

            def ple(l):
                for n in range(2 * TB):
                    lin[0] += 2
                    act.wait_ge(s["lin_full"], lin[0])
                    if n >= 2:
                        act.wait_ge(s["lin_free"], lin[0] - 4)
                    act.activation(sgp[n % 2], bank((lin[0] - 2) % 4), ACT.Sigmoid).then_inc(s["gate_sig"], 1)

            def strips(hd):
                return ps[:, 4 * (hd % 2):4 * (hd % 2) + 3, :].rearrange("p b n -> p (b n)")[:, 0:ZW]

            def soft(hd):
                m = hd % 2
                act.wait_ge(s["z_full"], hd + 1)
                act.activation(ez[m], strips(hd), ACT.Abs).then_inc(s["z_exp"], 1)
                act.wait_ge(s["z_exp"], 3 * hd + 1)
                act.activation(ez[m], ez[m], ACT.Exp, scale=-1.0).then_inc(s["z_exp"], 1)
                act.wait_ge(s["z_exp"], 3 * hd + 2)
                act.activation(ez[m], ez[m], ACT.Ln, bias=1.0).then_inc(s["z_exp"], 1)

            def attend():
                soft(0)
                soft(1)
                for hd in range(HEADS):
                    act.wait_ge(s["sum_full"], hd + 1)
                    act.activation(wT[hd % 2], strips(hd), ACT.Exp).then_inc(s["weights_set"], 1)
                    if hd > 0:
                        o_out(hd - 1)
                    if hd + 2 < HEADS:
                        soft(hd + 2)
                o_out(HEADS - 1)

            def o_out(hd):
                rows = slice(64 * (hd % 2), 64 * (hd % 2) + 64)
                act.wait_ge(s["o_full"], hd + 1)
                act.copy(oT[rows, (hd // 2) * T:(hd // 2 + 1) * T], ps[rows, 4 * (hd % 2) + 3, :]).then_inc(s["o_copied"], 1)

            def peer_layer(l):
                turned(hT)
                route(l)
                for tb in range(TB):
                    experts(l, tb)
                root()
                turned(hT)
                ple(l)

            act.sem_inc(s["diag_set"], TURN)
            root()
            peer_layer(0)
            root()
            turned(hkT)
            for n in range(KC):
                evacuate(KT[:, n * T:(n + 1) * T])
            for n0 in range(2):
                for tb in range(TB):
                    evacuate(V[:, tb * D + n0 * HALF:tb * D + (n0 + 1) * HALF])
            turned(hT)
            for n in range(KC):
                evacuate(QT[:, n * T:(n + 1) * T], scale=HD ** -0.5)
            attend()
            lin[0] += 2 * TB
            root()
            peer_layer(1)

            act.wait_ge(s["h_set"], 7 * TB)
            act.dma_start(out.rearrange("(b p) d -> p b d", p=P),
                          h[:, :].rearrange("p (b d) -> p b d", b=TB)).then_inc(s["out_done"], 16)
            act.wait_ge(s["out_done"], 16)

        @block.vector
        def _(dve):
            step = Steps(dve, s["dve_step"])

            def tt(o_, x, y, op):
                step.did(dve.tensor_tensor(o_, x, y, op))

            def ts(o_, x, c1, c2, op0, op1=None):
                step.did(dve.tensor_scalar(o_, x, c1, c2, op0, op1) if op1 is not None else dve.tensor_scalar(o_, x, c1, None, op0))

            def stt(o_, x, c, y, op0, op1):
                step.did(dve.scalar_tensor_tensor(out=o_, in0=x, scalar=c, in1=y, op0=op0, op1=op1))

            lr, li, dt, t0, t1, t2, rho, th, c, sn, fr, fi = (par[n] for n in (
                "lr", "li", "dt", "t0", "t1", "t2", "rho", "th", "c", "s", "fr", "fi"))
            dve.wait_ge(s["sin_done"], 1)
            tt(t0, lr, dt, ALU.mult)
            tt(th, li, dt, ALU.mult)
            step.settle()
            ts(t2, th, 1.0 / (2 * math.pi), ROUND, ALU.mult, ALU.add)
            step.settle()
            ts(t2, t2, ROUND, None, ALU.subtract)
            step.settle()
            stt(th, t2, -TWO_PI_HI, th, ALU.mult, ALU.add)
            step.settle()
            stt(th, t2, -TWO_PI_LO, th, ALU.mult, ALU.add)
            step.settle()
            ts(th, th, PI_BELOW, -PI_BELOW, ALU.min, ALU.max)
            dve.wait_ge(s["sin_done"], 4)
            tt(c, t1, t1, ALU.mult)
            step.settle()
            ts(c, c, -2.0, 1.0, ALU.mult, ALU.add)
            step.settle()

            def normalise(cc, ss):
                tt(t0, cc, cc, ALU.mult)
                tt(t1, ss, ss, ALU.mult)
                step.settle()
                tt(t0, t0, t1, ALU.add)
                step.settle()
                ts(t0, t0, -0.5, 1.5, ALU.mult, ALU.add)
                step.settle()
                tt(cc, cc, t0, ALU.mult)
                tt(ss, ss, t0, ALU.mult)
                step.settle()

            normalise(c, sn)
            W = [(wc[:, lv * PAIRS:(lv + 1) * PAIRS], ws[:, lv * PAIRS:(lv + 1) * PAIRS]) for lv in range(LEVELS)]
            step.did(dve.tensor_copy(W[0][0], c))
            step.did(dve.tensor_copy(W[0][1], sn))
            step.settle()
            for lv in range(1, LEVELS):
                (pc, ps_), (qc, qs) = W[lv - 1], W[lv]
                tt(t0, pc, pc, ALU.mult)
                tt(t1, ps_, ps_, ALU.mult)
                stt(qs, pc, 2.0, ps_, ALU.mult, ALU.mult)
                step.settle()
                tt(qc, t0, t1, ALU.subtract)
                step.settle()
                normalise(qc, qs)
            tt(t0, rho, c, ALU.mult)
            tt(t1, rho, sn, ALU.mult)
            tt(t2, lr, lr, ALU.mult)
            tt(th, li, li, ALU.mult)
            step.settle()
            ts(t0, t0, -1.0, None, ALU.add)
            tt(t2, t2, th, ALU.add)
            step.settle()
            step.did(dve.reciprocal(t2, t2))
            tt(fr, t0, lr, ALU.mult)
            tt(th, t1, li, ALU.mult)
            tt(fi, t1, lr, ALU.mult)
            tt(c, t0, li, ALU.mult)
            step.settle()
            tt(fr, fr, th, ALU.add)
            tt(fi, fi, c, ALU.subtract)
            step.settle()
            tt(fr, fr, t2, ALU.mult)
            step.settle()
            dve.tensor_tensor(fi, fi, t2, ALU.mult).then_inc(s["trig_set"], 1)
            dve.wait_ge(s["trig_set"], 1)
            dve.wait_ge(s["const_set"], 9)

            def pre(b, q, turn):
                dve.wait_ge(s[f"win_in{q}"], turn * 112 + 112)
                if not first(turn):
                    dve.wait_ge(s["pair_done"], (b - 1) * CHB)
                br, bi = (braw[q][r].rearrange("p (j c) -> p j c", j=CHB) for r in range(2))
                m = [bmul[k].rearrange("p (j c) -> p j c", j=CHB) for k in range(4)]
                frb = fr[:, bass.ds(b * CHB, CHB)].unsqueeze(2).to_broadcast([P, CHB, GROUP])
                fib = fi[:, bass.ds(b * CHB, CHB)].unsqueeze(2).to_broadcast([P, CHB, GROUP])
                tt(m[0], br, frb, ALU.mult)
                tt(m[1], bi, fib, ALU.mult)
                tt(m[2], br, fib, ALU.mult)
                tt(m[3], bi, frb, ALU.mult)
                step.settle()
                for r, op in ((0, ALU.subtract), (1, ALU.add)):
                    o4 = bbd[q][r].rearrange("p (j c) -> p j c", j=CHB)
                    for g in range(2):
                        pp = slice(64 * g, 64 * g + 64)
                        dve.tensor_tensor(o4[pp, :, GROUP * g:GROUP * g + GROUP], m[2 * r][pp], m[2 * r + 1][pp],
                                          op).then_inc(s["bbar_set"], 1)
                ts(cbd[q][1], cbd[q][1], -1.0, None, ALU.mult)
                dve.tensor_scalar(dgD[q], ident[:, :], dsk[:, bass.ds(b, 1)], None, ALU.mult).then_inc(s["bbar_set"], 1)
                step.settle()

            def main(b, q):
                dve.wait_ge(s["tables_set"], 2 * (b + 1))
                for j in range(CHB):
                    cj, sj = (tab[q][r][:, j * T:(j + 1) * T] for r in range(2))
                    k = 2 * (j % 2)
                    dve.wait_ge(s["bu_full"], b * CHB + (j + 1))
                    tt(rot[0], bank(k), cj, ALU.mult)
                    tt(rot[1], bank(k + 1), sj, ALU.mult)
                    tt(rot[2], bank(k + 1), cj, ALU.mult)
                    dve.tensor_tensor(rot[3], bank(k), sj, ALU.mult).then_inc(s["bu_read"], 1)
                    step.settle()
                    dve.wait_ge(s["bu_read"], b * CHB + (j + 1))
                    tt(vin[0], rot[0], rot[1], ALU.add)
                    tt(vin[1], rot[2], rot[3], ALU.subtract)
                    step.settle()
                    decay = rho[:, bass.ds(b * CHB + j, 1)].to_broadcast([P, T])
                    for r in range(2):
                        step.did(dve.tensor_tensor_scan(sc_r[r], decay, vin[r], 0.0, ALU.mult, ALU.add))
                    step.settle()
                    if not (first(b) and j < 2):
                        dve.wait_ge(s["pair_done"], b * CHB + (j - 1))
                    pr = prod[j % 2]
                    tt(pr[0], sc_r[0], cj, ALU.mult)
                    stt(pr[1], sc_r[1], -1.0, sj, ALU.mult, ALU.mult)
                    tt(pr[2], sc_r[0], sj, ALU.mult)
                    i = dve.tensor_tensor(pr[3], sc_r[1], cj, ALU.mult)
                    i.then_inc(s["prods_set"], 1)
                    step.settle()

            pre(0, 0, 0)
            pre(1, 1, 0)
            main(0, 0)
            per_pre, per_main = 5, 3 + 2 + 2 + 3
            with step.loop(KC // 2 - 1, 2 * (per_pre + CHB * per_main)) as it:
                pre(2 * it + 2, 0, it + 1)
                main(2 * it + 1, 1)
                pre(2 * it + 3, 1, it + 1)
                main(2 * it + 2, 0)
            main(KC - 1, 1)

            dve.wait_ge(s["h_in"], 16)
            n = 0
            for n0 in range(2):
                for tb in range(TB):
                    dve.wait_ge(s["gate_sig"], n + 1)
                    tt(sgm[n % 2], sgm[n % 2], bank((2 * n) % 4), ALU.mult)
                    step.settle()
                    dve.scalar_tensor_tensor(out=hb(tb, n0), in0=hb(tb, n0), scalar=ALPHA, in1=sgm[n % 2], op0=ALU.mult,
                                             op1=ALU.add).then_inc(s["lin_free"], 2)
                    n += 1
            dve.wait_ge(s["lin_free"], 2 * n)

            lns = [0]
            lin = [4 * TB]
            gate_n = [2 * TB]

            def layer_norm(src, dst):
                which = lns[0]
                lns[0] += 1
                for tb in range(TB):
                    for n0 in range(2):
                        step.did(dve.bn_stats(stat[:, (2 * tb + n0) * 6:(2 * tb + n0 + 1) * 6], hb(tb, n0)))
                step.settle()
                for tb in range(TB):
                    step.did(dve.bn_aggr(mv[:, 2 * tb:2 * tb + 2], stat[:, 12 * tb:12 * tb + 12]))
                step.settle()
                dve.tensor_scalar(rstd[:, :], mv[:, :].rearrange("p (b m) -> p b m", m=2)[:, :, 1], LN_EPS, None,
                                  ALU.add).then_inc(s["var_set"], 1)
                dve.wait_ge(s["std_set"], which + 1)
                step.did(dve.reciprocal(rstd[:, :], rstd[:, :]))
                step.settle()
                dve.wait_ge(s["ln_in"], 32 * (which + 1))
                for tb in range(TB):
                    ts(dst[:, tb * D:(tb + 1) * D], hb(tb), mv[:, 2 * tb:2 * tb + 1], rstd[:, tb:tb + 1], ALU.subtract, ALU.mult)
                step.settle()
                for tb in range(TB):
                    d = dst[:, tb * D:(tb + 1) * D]
                    i = dve.tensor_tensor(d, d, lnp[:, 0:D], ALU.mult)
                    step.did(i)
                step.settle()
                for tb in range(TB):
                    d = dst[:, tb * D:(tb + 1) * D]
                    dve.tensor_tensor(d, d, lnp[:, D:2 * D], ALU.add).then_inc(s["h_set"], 1)
                dve.wait_ge(s["h_set"], H_AFTER[which])
                dve.sem_inc(s["lnp_free"], 1)

            def route(l):
                step.settle()
                dve.wait_ge(s["tri_set"], 2 if l == 0 else 11)
                step.did(dve.tensor_copy(iota16, iota16.bitcast(U32)))
                for hh in range(PH):
                    e = hh % 2
                    dve.wait_ge(s["scores_full"], l * PH + hh + 1)
                    todo = [(tb, sd) for tb in range(TB) for sd in range(2)]

                    def S(tb, sd):
                        return ps[:, 4 + 2 * e + sd, tb * P:(tb + 1) * P]

                    def kv8(tb, sd, c):
                        return val[sd][:, tb * TOPK + 8 * c:tb * TOPK + 8 * c + 8]

                    def ki8(tb, sd, c):
                        o = tb * SLOTS + hh * TOPK + 8 * c
                        return key[sd][:, o:o + 8].bitcast(U32)

                    def bv8(t, tb, c):
                        o = tb * SLOTS + hh * TOPK + 8 * c
                        return t[:, o:o + 8]

                    for tb, sd in todo:
                        step.did(dve.max(kv8(tb, sd, 0), S(tb, sd)))
                    step.settle()
                    for tb, sd in todo:
                        step.did(dve.max_index(ki8(tb, sd, 0), kv8(tb, sd, 0), S(tb, sd)))
                    for tb, sd in todo:
                        i = dve.match_replace(rest[2 * tb + sd], kv8(tb, sd, 0), S(tb, sd), LOWEST)
                        if (tb, sd) != todo[-1]:
                            step.did(i)
                    i.then_inc(s["scores_read"], 1)
                    step.settle()
                    dve.wait_ge(s["scores_read"], l * PH + hh + 1)
                    for tb, sd in todo:
                        step.did(dve.max(kv8(tb, sd, 1), rest[2 * tb + sd]))
                    step.settle()
                    for tb, sd in todo:
                        step.did(dve.max_index(ki8(tb, sd, 1), kv8(tb, sd, 1), rest[2 * tb + sd]))
                    for tb in range(TB):
                        v1 = val[0][:, tb * TOPK:(tb + 1) * TOPK].unsqueeze(2).to_broadcast([P, TOPK, TOPK])
                        v2 = val[1][:, tb * TOPK:(tb + 1) * TOPK].unsqueeze(1).to_broadcast([P, TOPK, TOPK])
                        tt(cand[tb].rearrange("p (i j) -> p i j", i=TOPK), v1, v2, ALU.add)
                    step.settle()
                    for tb in range(TB):
                        step.did(dve.max(bv8(best, tb, 0), cand[tb]))
                    step.settle()
                    for tb in range(TB):
                        step.did(dve.max_index(bv8(bpos, tb, 0).bitcast(U32), bv8(best, tb, 0), cand[tb]))
                        step.did(dve.match_replace(cand2[tb], bv8(best, tb, 0), cand[tb], LOWEST))
                    step.settle()
                    for tb in range(TB):
                        step.did(dve.max(bv8(best, tb, 1), cand2[tb]))
                    step.settle()
                    for tb in range(TB):
                        step.did(dve.max_index(bv8(bpos, tb, 1).bitcast(U32), bv8(best, tb, 1), cand2[tb]))
                step.settle()
                b3 = best.rearrange("p (n k) -> p n k", k=TOPK)
                g3 = gates.rearrange("p (n k) -> p n k", k=TOPK)
                dve.tensor_tensor(g3, b3, b3[:, :, 0:1].to_broadcast([P, TB * PH, TOPK]), ALU.subtract).then_inc(s["cand_gap"], 1)
                bu = bpos.bitcast(U32)
                step.did(dve.tensor_scalar(ksel[0].bitcast(U32), bu, 4, None, ALU.logical_shift_right))
                step.did(dve.tensor_scalar(ksel[1].bitcast(U32), bu, 15, None, ALU.bitwise_and))
                for sd in range(2):
                    step.did(dve.tensor_copy(key[sd], key[sd].bitcast(U32)))
                step.settle()
                for sd in range(2):
                    step.did(dve.tensor_copy(ksel[sd], ksel[sd].bitcast(U32)))
                step.settle()
                for tb in range(TB):
                    cols = slice(tb * SLOTS, (tb + 1) * SLOTS)
                    for sd in range(2):
                        tt(eq[sd].rearrange("p (n j) -> p n j", j=TOPK), ksel[sd][:, cols].unsqueeze(2).to_broadcast([P, SLOTS, TOPK]),
                           iota16.unsqueeze(1).to_broadcast([P, SLOTS, TOPK]), ALU.is_equal)
                    step.settle()
                    for sd in range(2):
                        e4 = eq[sd].rearrange("p (h k j) -> p h k j", h=PH, k=TOPK)
                        k4 = key[sd][:, cols].rearrange("p (h j) -> p h j", h=PH).unsqueeze(2).to_broadcast([P, PH, TOPK, TOPK])
                        tt(e4, e4, k4, ALU.mult)
                    step.settle()
                    for sd in range(2):
                        step.did(dve.tensor_reduce(esel[sd], eq[sd].rearrange("p (n j) -> p n j", j=TOPK), AX_X, ALU.add))
                    step.settle()
                    stt(esel[0], esel[0], float(NKEYS), esel[1], ALU.mult, ALU.add)
                    step.settle()
                    ts(idx[:, cols], esel[0], float(l * EXPERTS), None, ALU.add)
                dve.wait_ge(s["gap_exp"], l + 1)
                step.did(dve.tensor_reduce(rsum, g3, AX_X, ALU.add))
                step.settle()
                step.did(dve.reciprocal(rinv, rsum))
                step.settle()
                dve.tensor_tensor(g3, g3, rinv.unsqueeze(2).to_broadcast([P, TB * PH, TOPK]), ALU.mult).then_inc(s["idx_set"], 1)

            def experts(l, tb):
                done = (l * TB + tb) * SLOTS
                dve.wait_ge(s["idx_set"], l + 1)
                with dve.Fori(0, SLOTS // TURN) as j:
                    for r in range(TURN):
                        if r % 4 == 0:
                            dve.wait_ge(s["diag_set"], j * TURN + (done + r + 4))
                        dve.wait_ge(u_in[r % RING], j * 32 + (16 * (done // RING) + 16 * (r // RING) + 16))
                        u = u_ring[r % RING]
                        dve.tensor_tensor_reduce(u, u, hb(tb), 1.0, 0.0, ALU.mult, ALU.add,
                                                 actv[:, r:r + 1]).then_inc(s["u_used"], 1)

            def ffn_sum(l, tb):
                k = 4 + 2 * (tb % 2)
                dve.wait_ge(s["ffn_full"], l * TB + tb + 1)
                dve.scalar_tensor_tensor(out=hb(tb), in0=hb(tb), scalar=ALPHA, in1=ps[:, k:k + 2, :].rearrange("p b n -> p (b n)"),
                                         op0=ALU.mult, op1=ALU.add).then_inc(s["ffn_read"], 1)
                dve.wait_ge(s["ffn_read"], l * TB + tb + 1)

            def gated(sg, keep):
                n = 0
                for n0 in range(2):
                    for tb in range(TB):
                        dve.wait_ge(s["gate_sig"], gate_n[0] + n + 1)
                        tt(sg[n % 2], sg[n % 2], bank((lin[0] + 1) % 4), ALU.mult)
                        step.settle()
                        dve.scalar_tensor_tensor(out=hb(tb, n0), in0=hb(tb, n0), scalar=keep, in1=sg[n % 2], op0=ALU.mult,
                                                 op1=ALU.add).then_inc(s["lin_free"], 2)
                        n += 1
                        lin[0] += 2
                gate_n[0] += n
                dve.wait_ge(s["lin_free"], lin[0])

            def peer_layer(l):
                lin[0] += 2 * TB + 16
                route(l)
                for tb in range(TB):
                    experts(l, tb)
                    if tb > 0:
                        ffn_sum(l, tb - 1)
                ffn_sum(l, TB - 1)
                step.settle()
                layer_norm(h, h)
                lin[0] += 2 * TB
                gated(sgp, 1.0)
                dve.sem_inc(s["h_set"], TB)

            dve.sem_inc(s["u_used"], RING)
            layer_norm(h, h)
            peer_layer(0)
            layer_norm(h, hk)
            lin[0] += 2 * TB + KC + 2 * TB + 2 * TB + KC
            dve.wait_ge(s["tri_set"], 9)
            for hd in range(HEADS):
                b0, m = 4 * (hd % 2), hd % 2
                zf = ps[:, b0:b0 + 3, :].rearrange("p b n -> p (b n)")[:, 0:ZW]
                dve.wait_ge(s["z_full"], hd + 1)
                dve.wait_ge(s["z_exp"], 3 * hd + 3)
                stt(sp_[m], zf, 0.0, ez[m], ALU.max, ALU.add)
                step.settle()
                for o, w in ((0, 1), (512, 2), (1024, 1)):
                    v = sp_[m][:, o:o + w * P]
                    dve.tensor_tensor(v, v, seen[:, 0:w * P], ALU.mult).then_inc(s["soft_set"], 1)
            for n0 in range(2):
                for tb in range(TB):
                    dve.wait_ge(s["lin_full"], lin[0] + 1)
                    dve.scalar_tensor_tensor(out=hb(tb, n0), in0=hb(tb, n0), scalar=ALPHA, in1=bank(lin[0] % 4), op0=ALU.mult,
                                             op1=ALU.add).then_inc(s["lin_free"], 1)
                    lin[0] += 1
            dve.wait_ge(s["lin_free"], lin[0])
            layer_norm(h, h)
            peer_layer(1)

        @block.tensor
        def _(pe):
            pe.wait_ge(s["xT_in"], 16)
            pe.wait_ge(s["const_set"], 9)

            def pre(b, q, turn):
                pe.wait_ge(s[f"win_in{q}"], turn * 112 + 112)
                if not first(turn):
                    pe.wait_ge(s["bt_copied"], 2 * (b - 1))
                for k in range(KC):
                    i = pe.matmul(bank(6 + q), win[q][:, k * P:(k + 1) * P], hT_at(k), start=(k == 0), stop=(k == KC - 1))
                i.then_inc(s["u_full"], 1)
                pe.wait_ge(s["u_copied"], b + 1)
                pe.wait_ge(s["bbar_set"], b * 5 + 5)
                for r in range(2):
                    i = pe.transpose(ps[:, 6 + q, r * P:(r + 1) * P], bbd[q][r], ident[:, :])
                i.then_inc(s["bt_full"], 1)

            def y_of(b, q, j):
                pe.wait_ge(s["prods_set"], b * CHB + (j + 1))
                rows = slice(32 * j, 32 * j + 32)
                for k in range(4):
                    i = pe.matmul(ps[rows, 4 + q, :], cbd[q][k // 2][:, 32 * j:32 * j + 32], prod[j % 2][k],
                                  start=False, stop=(k == 3), skip_group_check=True)
                i.then_inc(s["pair_done"], 1)

            def main(b, q):
                pe.wait_ge(s["bt_copied"], 2 * b + 2)
                if not first(b):
                    pe.wait_ge(s["y_taken"], b)
                pe.matmul(bank(4 + q), dgD[q], ub[q], start=True, stop=False, skip_group_check=True)
                for j in range(CHB):
                    rows = slice(32 * j, 32 * j + 32)
                    if not (first(b) and j < 2):
                        pe.wait_ge(s["bu_read"], b * CHB + (j - 1))
                    for r in range(2):
                        i = pe.matmul(bank(2 * (j % 2) + r), bT[q][r][rows, :], ub[q][rows, :], start=True, stop=True)
                    i.then_inc(s["bu_full"], 1)
                    if j >= 1:
                        y_of(b, q, j - 1)
                y_of(b, q, CHB - 1)

            pre(0, 0, 0)
            pre(1, 1, 0)
            main(0, 0)
            with pe.Fori(0, KC // 2 - 1) as it:
                pre(2 * it + 2, 0, it + 1)
                main(2 * it + 1, 1)
                pre(2 * it + 3, 1, it + 1)
                main(2 * it + 2, 0)
            main(KC - 1, 1)

            count = [0, 0]

            def linear(mats, inc=1):
                t = count[0]
                if t >= 4:
                    pe.wait_ge(s["lin_free"], t - 3)
                for k, (lhs, rhs) in enumerate(mats):
                    i = pe.matmul(bank(t % 4), lhs, rhs, start=(k == 0), stop=(k == len(mats) - 1))
                i.then_inc(s["lin_full"], 1)
                count[0] += 1

            def rows(src, tb, n_piece):
                slot = n_piece % WSLOTS
                linear([(src[:, k * T + tb * P:k * T + (tb + 1) * P], w_at(slot, k)) for k in range(KC)])

            def columns(src, m, n_piece):
                slot = n_piece % WSLOTS
                linear([(w_at(slot, k, m * P, (m + 1) * P), src[:, k * T:(k + 1) * T]) for k in range(KC)])

            def have(n):
                pe.wait_ge(s[f"w_in{n % WSLOTS}"], 16 * (n // WSLOTS + 1))

            def used(n):
                pe.wait_ge(s["lin_full"], count[0])
                pe.sem_inc(s["w_used"], n)

            def copied():
                pe.wait_ge(s["lin_free"], count[0])

            def turn_over(src, version):
                for tb in range(TB):
                    pe.wait_ge(s["h_set"], version * TB + tb + 1)
                    for q in range(2):
                        t = count[0]
                        if t >= 4:
                            pe.wait_ge(s["lin_free"], t - 3)
                        for k in range(4):
                            o = tb * D + (4 * q + k) * P
                            i = pe.transpose(bank(t % 4)[:, k * P:(k + 1) * P], src[:, o:o + P], ident[:, :])
                        i.then_inc(s["lin_full"], 1)
                        count[0] += 1

            pe.wait_ge(s["y_taken"], KC + 1)
            pe.wait_ge(s["bu_read"], PAIRS)
            for n0 in range(2):
                for g in range(2):
                    have(glu[2 * n0 + g])
                for tb in range(TB):
                    for g in range(2):
                        rows(yT, tb, glu[2 * n0 + g])
                used(2)

            def route(l):
                for pc in range(4):
                    have(w_q1[l][pc])
                    for m in range(4):
                        columns(hT, m, w_q1[l][pc])
                    used(1)
                    copied()
                    if pc == 0:
                        pe.wait_ge(s["k_in"], 32 * (l + 1))
                    for e in range(2):
                        hh = 2 * pc + e
                        if hh >= 2:
                            pe.wait_ge(s["scores_read"], l * PH + hh - 1)
                        for sd in range(2):
                            for tb in range(TB):
                                i = pe.matmul(ps[:, 4 + 2 * e + sd, tb * P:(tb + 1) * P],
                                              q_sb[(pc % 2) * 4 + 2 * e + sd][:, tb * P:(tb + 1) * P], k12[sd],
                                              start=True, stop=True)
                        i.then_inc(s["scores_full"], 1)

            def experts(l, tb):
                done = (l * TB + tb) * SLOTS
                k = 4 + 2 * (tb % 2)
                if tb >= 2:
                    pe.wait_ge(s["ffn_read"], l * TB + tb - 1)
                else:
                    pe.wait_ge(s["scores_read"], (l + 1) * PH)
                for n0 in range(2):
                    pe.matmul(bank(k + n0), zrow[0:1, 0:P], zrow[0:1, :], start=True, stop=False, skip_group_check=True)
                with pe.Fori(0, SLOTS // TURN) as j:
                    for r in range(TURN):
                        if r % 4 == 0:
                            pe.wait_ge(s["diag_set"], j * TURN + (done + TURN + r + 4))
                        pe.wait_ge(v_in[r % RING], j * 32 + (16 * (done // RING) + 16 * (r // RING) + 16))
                        for n0 in range(2):
                            i = pe.matmul(bank(k + n0), diag[r % RING], v_ring[r % RING][:, n0 * HALF:(n0 + 1) * HALF],
                                          start=False, stop=False, skip_group_check=True)
                        i.then_inc(s["v_used"], 1)
                for n0 in range(2):
                    i = pe.matmul(bank(k + n0), zrow[0:1, 0:P], zrow[0:1, :], start=False, stop=True, skip_group_check=True)
                i.then_inc(s["ffn_full"], 1)

            def peer_layer(l):
                turn_over(h, 0 if l == 0 else 4)
                copied()
                route(l)
                pe.wait_ge(s["tri_set"], 2 if l == 0 else 11)
                for tb in range(TB):
                    experts(l, tb)
                turn_over(h, 1 if l == 0 else 5)
                copied()
                pe.wait_ge(s["ple_in"], 32 * (l + 1))
                for n0 in range(2):
                    have(w_pg[l][n0])
                    for tb in range(TB):
                        rows(hT, tb, w_pg[l][n0])
                        linear([(pTs[:, k * T + tb * P:k * T + (tb + 1) * P], plw[:, k * D + n0 * HALF:k * D + (n0 + 1) * HALF])
                                for k in range(2)])
                    used(1)

            pe.sem_inc(s["v_used"], RING)
            peer_layer(0)

            turn_over(hk, 3)
            copied()
            for n0 in range(2):
                have(w_k[n0])
                for m in range(4):
                    columns(hkT, m, w_k[n0])
                used(1)
            for n0 in range(2):
                have(w_v[n0])
                for tb in range(TB):
                    rows(hkT, tb, w_v[n0])
                used(1)
            turn_over(h, 2)
            copied()
            for n0 in range(2):
                have(w_qq[n0])
                for m in range(4):
                    columns(hT, m, w_qq[n0])
                used(1)
            copied()
            pe.wait_ge(s["tri_set"], 9)

            def strip(hd, kb, c0=0, c1=None):
                w = T - kb * P
                o = STRIP[kb] + c0
                return ps[:, 4 * (hd % 2) + STRIP[kb] // HALF, :][:, o % HALF:o % HALF + (w if c1 is None else c1) - c0]

            def scores(hd):
                rw = slice(64 * (hd % 2), 64 * (hd % 2) + 64)
                c = (hd // 2) * T
                if hd >= 2:
                    pe.wait_ge(s["weights_set"], hd - 1)
                for kb in (0, 3, 1, 2):
                    i = pe.matmul(strip(hd, kb), KT[rw, c + kb * P:c + (kb + 1) * P], QT[rw, c + kb * P:c + T],
                                  start=(kb != 1), stop=True, skip_group_check=True)
                i.then_inc(s["z_full"], 1)

            def log_weights(hd):
                pe.wait_ge(s["soft_set"], 3 * hd + 3)
                x = sp_[hd % 2]
                for kb in range(TB):
                    for jb in range(kb, TB):
                        i = pe.matmul(strip(hd, kb, (jb - kb) * P), ntri if jb == kb else nones,
                                      x[:, STRIP[jb]:STRIP[jb] + T - jb * P], start=False, stop=True, skip_group_check=True)
                    i = pe.matmul(strip(hd, kb, 0, P), ident[:, :], hide, start=False, stop=True, skip_group_check=True)
                i.then_inc(s["sum_full"], 1)

            def values(hd):
                rw = slice(64 * (hd % 2), 64 * (hd % 2) + 64)
                pe.wait_ge(s["weights_set"], hd + 1)
                if hd >= 2:
                    pe.wait_ge(s["o_copied"], hd - 1)
                for kb in range(TB):
                    i = pe.matmul(ps[rw, 4 * (hd % 2) + 3, kb * P:T], V[:, kb * D + hd * HD:kb * D + (hd + 1) * HD],
                                  wT[hd % 2][:, STRIP[kb]:STRIP[kb] + T - kb * P], start=(kb == 0), stop=(kb == TB - 1),
                                  skip_group_check=True)
                i.then_inc(s["o_full"], 1)

            scores(0)
            scores(1)
            for hd in range(HEADS):
                log_weights(hd)
                values(hd)
                if hd + 2 < HEADS:
                    scores(hd + 2)
            pe.wait_ge(s["o_copied"], HEADS)
            for n0 in range(2):
                have(w_oo[n0])
                for tb in range(TB):
                    rows(oT, tb, w_oo[n0])
                used(1)
            peer_layer(1)


def kernel(**inputs):
    import numpy as _np
    import concourse.bacc as _bacc
    from concourse import mybir as _mybir
    from concourse.bass_utils import run_bass_kernel_spmd as _run

    v = {k: _np.asarray(x) for k, x in inputs.items()}

    def by_state(x):
        x = x.reshape((PAIRS, 2, 64) + x.shape[2:])
        x = _np.moveaxis(x, 0, 2)
        return x.reshape(P, -1)

    arrays = {
        "x": v["x"][0], "xT": v["x"][0].T, "pT": v["p"][:, 0].transpose(0, 2, 1),
        "lam_re": by_state(v["ssm_lam_re"][0]), "lam_im": by_state(v["ssm_lam_im"][0]),
        "log_dt": v["ssm_log_dt"][0].reshape(PAIRS, 2).T,
        "b_re": by_state(v["ssm_b_re"][0]), "b_im": by_state(v["ssm_b_im"][0]),
        "c_re": by_state(v["ssm_c_re"][0].transpose(0, 2, 1)), "c_im": by_state(v["ssm_c_im"][0].transpose(0, 2, 1)),
        "d_skip": v["ssm_d"][0].reshape(KC, P).T, "w_in": v["ssm_w_in"][0], "w_glu": v["ssm_w_glu"][0],
        "ln_mix_g": v["ln_mix_g"], "ln_mix_b": v["ln_mix_b"], "ln_ffn_g": v["ln_ffn_g"], "ln_ffn_b": v["ln_ffn_b"],
        "kv_g": v["kv_ln_g"][None], "kv_b": v["kv_ln_b"][None],
        "w_kv": v["w_kv"], "w_q": v["sb_w_q"][0], "w_o": v["sb_w_o"][0],
        "peer_w_q": v["peer_w_q"].reshape(DEPTH * D, PH * 256),
        "k1T": v["peer_k1"].transpose(0, 2, 1).reshape(DEPTH * P, NKEYS),
        "k2T": v["peer_k2"].transpose(0, 2, 1).reshape(DEPTH * P, NKEYS),
        "peer_u": v["peer_u"].reshape(DEPTH * EXPERTS, D), "peer_v": v["peer_v"].reshape(DEPTH * EXPERTS, D),
        "ple_w": v["ple_w"].reshape(DEPTH * PLE, D), "ple_gate": v["ple_gate"].reshape(DEPTH * D, D),
    }
    nc = _bacc.Bacc("TRN2", target_bir_lowering=False, num_devices=1)
    feeds, aps = {}, {}
    for name, x in arrays.items():
        x = _np.ascontiguousarray(x)
        feeds[f"in_{name}"] = x
        aps[name] = nc.dram_tensor(f"in_{name}", x.shape, _mybir.dt.from_np(x.dtype), kind="ExternalInput").ap()
    out = nc.dram_tensor("out", (T, D), _mybir.dt.float32, kind="ExternalOutput").ap()
    build(nc, aps, out)
    r = _run(nc, [feeds], core_ids=[0])
    return r.results[0]["out"].reshape(1, T, D)
```

```python
import math
from contextlib import ExitStack, contextmanager

import numpy as np
import concourse.bass as bass
from concourse import mybir

ALU = mybir.AluOpType
ACT = mybir.ActivationFunctionType
AX_X = mybir.AxisListType.X
F32 = mybir.dt.float32
U32 = mybir.dt.uint32

P = 128
D = 1024
T = 512
DEPTH = 2
KC = D // P
TB = T // P
HALF = 512
CHB = 4
GROUP = 16
PAIRS = D // (2 * GROUP)
LEVELS = 9
HEADS = 16
HD = D // HEADS
PH = 8
NKEYS = 128
EXPERTS = NKEYS * NKEYS
TOPK = 16
SLOTS = PH * TOPK
RING = 8
TURN = 2 * RING
PLE = 256
ALPHA = (2 * DEPTH) ** 0.25
LN_EPS = 1e-5
LOWEST = -3.0e38
MASKED = -1.0e30
ARENA = 36900
WSLOTS = 2
ROUND = 1.5 * 2.0 ** 23
TWO_PI_HI = 6.28125
TWO_PI_LO = 2 * math.pi - TWO_PI_HI
PI_BELOW = 3.1415925
HB = TB // 2
TH = T // 2
GROUPS = SLOTS // 4


class Steps:

    def __init__(self, eng, sem):
        self.eng, self.sem, self.base, self.n = eng, sem, 0, 0

    def did(self, ins):
        ins.then_inc(self.sem, 1)
        self.n += 1

    def settle(self):
        self.eng.wait_ge(self.sem, self.base + self.n)

    @contextmanager
    def loop(self, trips, per_trip):
        with self.eng.Fori(0, trips) as i:
            start = self.base + self.n
            self.base, self.n = i * per_trip + start, 0
            yield i
            assert self.n == per_trip, (self.n, per_trip)
        self.base, self.n = start + trips * per_trip, 0


def first(n):
    return isinstance(n, int) and n == 0


def build(nc, a, out):
    ctx = ExitStack()
    with ctx:
        def sb(name, cols, dt=F32):
            return ctx.enter_context(nc.sbuf_tensor(name, [P, cols], dt))

        def sem(name):
            return ctx.enter_context(nc.semaphore(name))

        ps = ctx.enter_context(nc.psum_tensor("ps", [P, 8, HALF], F32))

        def bank(n):
            return ps[:, n, :]

        h = sb("h", TB * D)
        wring = sb("wring", WSLOTS * KC * HALF)
        ident = sb("ident", P)
        lnp = sb("lnp", 2 * D)
        stat = sb("stat", TB * 12)
        mv = sb("mv", TB * 2)
        rstd = sb("rstd", TB)
        zrow = sb("zrow", HALF)
        iota16 = sb("iota16", TOPK)
        ntri = sb("ntri", P)
        nones = sb("nones", P)
        seen = sb("seen", P)
        hide = sb("hide", P)
        k12s = sb("k12", 2 * NKEYS)
        arena = sb("arena", ARENA)
        here = [0]

        def reg_wait(eng, semaphore, value):
            value = eng.to_reg(value)
            eng.wait_ge(s["const_set"], 9)
            eng.wait_ge(semaphore, value)

        def place(cols, at=None):
            if at is not None:
                here[0] = at
            v = arena[:, here[0]:here[0] + cols]
            here[0] += cols
            assert here[0] <= ARENA, here[0]
            return v

        def hb(tb, n0=None):
            return h[:, tb * D:(tb + 1) * D] if n0 is None else h[:, tb * D + n0 * HALF:tb * D + (n0 + 1) * HALF]

        def w_at(slot, k, c0=0, c1=HALF):
            o = (slot * KC + k) * HALF
            return wring[:, o + c0:o + c1]

        yT = place(KC * T, 0)
        tab = [[place(CHB * T) for _ in range(2)] for _ in range(2)]
        ptmp = [place(CHB * T // 2) for _ in range(2)]
        rot = [place(T) for _ in range(4)]
        vin = [place(T) for _ in range(2)]
        sc_r = [place(T) for _ in range(2)]
        prod = [[place(T) for _ in range(4)] for _ in range(2)]
        ub = [place(T) for _ in range(2)]
        win = [place(D) for _ in range(2)]
        braw = [[place(CHB * GROUP) for _ in range(2)] for _ in range(2)]
        bmul = [place(CHB * GROUP) for _ in range(4)]
        bbd = [[place(P) for _ in range(2)] for _ in range(2)]
        bT = [[place(P) for _ in range(2)] for _ in range(2)]
        cbd = [[place(P) for _ in range(2)] for _ in range(2)]
        dgD = [place(P) for _ in range(2)]
        dsk = place(KC)
        par = {n: place(PAIRS) for n in ("lr", "li", "dt", "t0", "t1", "t2", "rho", "th", "c", "s", "fr", "fi")}
        wc = place(LEVELS * PAIRS)
        ws = place(LEVELS * PAIRS)
        xT = place(KC * T)
        sgm = [place(HALF, KC * T + HALF * q) for q in range(2)]

        u_ring = [place(D, 0 if r == 0 else None) for r in range(RING)]
        v_ring = [place(D) for _ in range(RING)]
        diag = [place(P) for _ in range(RING)]
        stage_idx = place(TURN).bitcast(U32)
        actv = place(TURN)
        gelu = place(TURN)
        gg = place(TURN)
        idx = place(TB * SLOTS).bitcast(U32)
        gates = place(TB * SLOTS)
        KT = place(KC * T)
        V = place(TB * D)
        QT = place(KC * TH)
        hTh = place(KC * TH)
        dyn = here[0]
        q_sb = [place(TH, dyn if n == 0 else None) for n in range(4)]
        val = [place(HB * TOPK) for _ in range(2)]
        key = [place(HB * SLOTS) for _ in range(2)]
        best = place(HB * SLOTS)
        bpos = place(HB * SLOTS)
        ksel = [place(HB * SLOTS) for _ in range(2)]
        esel = [place(SLOTS) for _ in range(2)]
        rsum = place(HB * PH)
        rinv = place(HB * PH)
        eq_at = here[0]
        rest = [place(NKEYS) for _ in range(2 * HB)]
        cand = [place(TOPK * TOPK) for _ in range(HB)]
        cand2 = [place(TOPK * TOPK) for _ in range(HB)]
        eq = place(SLOTS * TOPK, eq_at)
        plw = place(2 * D, dyn)
        pTs = place(2 * TH)
        sgp = [place(HALF) for _ in range(2)]
        hk = place(HB * D, dyn)
        hkT = place(KC * TH)
        ZW = [384, 896]
        ez = [place(ZW[1], dyn if e == 0 else None) for e in range(2)]
        sp_ = [place(ZW[1]) for _ in range(2)]

        def first_q(hf, kb):
            return max(kb - HB * hf, 0) * P

        def strip_at(hf, kb):
            return kb * TH if hf == 0 or kb < 3 else 3 * TH

        def hk_blocks(hf):
            return range(HB * (hf + 1))

        s = {n: sem(n) for n in (
            "const_set", "dve_step", "pool_step", "act_step", "xT_in", "h_in", "par_in", "win_in0", "win_in1",
            "u_full", "u_copied", "bbar_set", "bt_full", "bt_copied", "tables_set", "bu_full", "bu_read",
            "prods_set", "pair_done", "y_taken", "sin_done", "trig_set", "w_in0", "w_in1", "lin_full", "lin_free",
            "gate_sig", "ln_in", "lnp_free", "var_set", "std_set", "h_set", "out_done", "tri_set", "k_in", "ple_in",
            "scores_full", "scores_read", "gap_set", "gap_exp", "idx_set", "u_used", "v_used", "diag_set",
            "ffn_full", "ffn_read", "z_full", "z_exp", "soft_set", "sum_full", "weights_set", "o_full", "o_copied")}
        u_in = [sem(f"u_in{r}") for r in range(RING)]
        v_in = [sem(f"v_in{r}") for r in range(RING)]

        block = ctx.enter_context(nc.Block())
        w_plan = []

        def piece(ap, c0):
            w_plan.append(ap[:, c0:c0 + HALF].rearrange("(k p) n -> p k n", p=P))
            return len(w_plan) - 1

        def pieces(ap, n, c0=0):
            return [piece(ap, c0 + m * HALF) for m in range(n)]

        W = {"glu": [piece(a["w_glu"], g * D + n0 * HALF) for n0 in range(2) for g in range(2)]}
        for hf in range(2):
            W["pq", 0, hf] = pieces(a["peer_w_q"][0:D, :], 4)
        for hf in range(2):
            W["pg", 0, hf] = pieces(a["ple_gate"][0:D, :], 2)
            W["k", hf] = pieces(a["w_kv"], 2)
            W["v", hf] = pieces(a["w_kv"], 2, D)
            W["q", hf] = pieces(a["w_q"], 2)
            W["o", hf] = pieces(a["w_o"], 2)
            W["pq", 1, hf] = pieces(a["peer_w_q"][D:2 * D, :], 4)
        for hf in range(2):
            W["pg", 1, hf] = pieces(a["ple_gate"][D:2 * D, :], 2)

        H = {}
        for tb in range(TB):
            H["mix", 0, tb] = len(H) + 1
        for hf in range(2):
            for what in (("ffn", 0), ("ple", 0), ("kv", 1), ("mix", 1)):
                for tb in range(HB * hf, HB * hf + HB):
                    H[what + (tb,)] = len(H) + 1
        for hf in range(2):
            for what in (("ffn", 1), ("ple", 1)):
                for tb in range(HB * hf, HB * hf + HB):
                    H[what + (tb,)] = len(H) + 1
        ROUTED = {(0, 0): 1, (0, 1): 2, (1, 0): 3, (1, 1): 4}
        LN_LOADS = [("ln_mix", 0)] + 2 * [("ln_ffn", 0), ("kv", 0), ("ln_mix", 1)] + [("ln_ffn", 1)]
        TILE = {}
        FREE_AT = {}

        STEPS_ROUTE = PH + 1 + 2 * HB + 1
        STEPS_PLE = HB + HB + 4
        STEPS_MID = HB + 2 * HB + 4 + 4 + 4 + (HEADS + 1) + 4 + HB + HB

        def weave(l, tbs, group, steps, filler, lag, block_start=None, block_end=None):
            done, total = 0, len(tbs) * GROUPS
            for n in range(total):
                tb, g = tbs[n // GROUPS], n % GROUPS
                if g == 0 and block_start:
                    block_start(l, tb)
                group(l, tb, (l * TB + tb) * SLOTS + 4 * g, g)
                if g == GROUPS - 1 and block_end:
                    block_end(l, tb)
                while done < min(steps, -(-steps * (n + 1 - lag) // total)):
                    next(filler)
                    done += 1
            while done < steps:
                next(filler)
                done += 1

        def alone(steps, filler):
            for _ in range(steps):
                next(filler)

        @block.tensor
        def _(pe):
            pe.wait_ge(s["xT_in"], 16)
            pe.wait_ge(s["const_set"], 9)

            def pre(b, q, turn):
                pe.wait_ge(s[f"win_in{q}"], turn * 112 + 112)
                if not first(turn):
                    pe.wait_ge(s["bt_copied"], 2 * (b - 1))
                for k in range(KC):
                    i = pe.matmul(bank(6 + q), win[q][:, k * P:(k + 1) * P], xT[:, k * T:(k + 1) * T], start=(k == 0), stop=(k == KC - 1))
                i.then_inc(s["u_full"], 1)
                pe.wait_ge(s["u_copied"], b + 1)
                pe.wait_ge(s["bbar_set"], b * 5 + 5)
                for r in range(2):
                    i = pe.transpose(ps[:, 6 + q, r * P:(r + 1) * P], bbd[q][r], ident[:, :])
                i.then_inc(s["bt_full"], 1)

            def y_of(b, q, j):
                pe.wait_ge(s["prods_set"], b * CHB + (j + 1))
                rows = slice(32 * j, 32 * j + 32)
                for k in range(4):
                    i = pe.matmul(ps[rows, 4 + q, :], cbd[q][k // 2][:, 32 * j:32 * j + 32], prod[j % 2][k],
                                  start=False, stop=(k == 3), skip_group_check=True)
                i.then_inc(s["pair_done"], 1)

            def main(b, q):
                pe.wait_ge(s["bt_copied"], 2 * b + 2)
                if not first(b):
                    pe.wait_ge(s["y_taken"], b)
                pe.matmul(bank(4 + q), dgD[q], ub[q], start=True, stop=False, skip_group_check=True)
                for j in range(CHB):
                    rows = slice(32 * j, 32 * j + 32)
                    if not (first(b) and j < 2):
                        pe.wait_ge(s["bu_read"], b * CHB + (j - 1))
                    for r in range(2):
                        i = pe.matmul(bank(2 * (j % 2) + r), bT[q][r][rows, :], ub[q][rows, :], start=True, stop=True)
                    i.then_inc(s["bu_full"], 1)
                    if j >= 1:
                        y_of(b, q, j - 1)
                y_of(b, q, CHB - 1)

            pre(0, 0, 0)
            pre(1, 1, 0)
            main(0, 0)
            with pe.Fori(0, KC // 2 - 1) as it:
                pre(2 * it + 2, 0, it + 1)
                main(2 * it + 1, 1)
                pre(2 * it + 3, 1, it + 1)
                main(2 * it + 2, 0)
            main(KC - 1, 1)

            def tile(key):
                t = TILE[key] = len(TILE)
                if t >= 4:
                    pe.wait_ge(s["lin_free"], t - 3)
                return bank(t % 4)

            def linear(key, mats, cols=HALF):
                o = tile(key)[:, 0:cols]
                for k, (lhs, rhs) in enumerate(mats):
                    i = pe.matmul(o, lhs, rhs, start=(k == 0), stop=(k == len(mats) - 1))
                i.then_inc(s["lin_full"], 1)

            def rows(key, src, width, at, n):
                linear(key, [(src[:, k * width + at:k * width + at + P], w_at(n % WSLOTS, k)) for k in range(KC)])

            def columns(key, src, m, n):
                linear(key, [(w_at(n % WSLOTS, k, m * P, (m + 1) * P), src[:, k * TH:(k + 1) * TH]) for k in range(KC)], TH)

            def have(n):
                pe.wait_ge(s[f"w_in{n % WSLOTS}"], 16 * (n // WSLOTS + 1))

            def used(n):
                FREE_AT[n] = len(TILE)

            def copied():
                pe.wait_ge(s["lin_free"], len(TILE))

            def turn_over(what, hf, src, base):
                for tb in range(HB * hf, HB * hf + HB):
                    pe.wait_ge(s["h_set"], H[what + (tb,)])
                    for q in range(2):
                        b = tile(("turn", what, tb, q))
                        for k in range(4):
                            o = (tb - base) * D + (4 * q + k) * P
                            i = pe.transpose(b[:, k * P:(k + 1) * P], src[:, o:o + P], ident[:, :])
                        i.then_inc(s["lin_full"], 1)
                    yield

            def column_steps(what, hf, src):
                copied()
                for n0 in range(2):
                    n = W[what, hf][n0]
                    have(n)
                    for m in range(4):
                        columns((what, hf, n0, m), src, m, n)
                        if m == 3:
                            used(n)
                        if m % 2:
                            yield

            def row_steps(what, hf, src):
                copied()
                for n0 in range(2):
                    n = W[what, hf][n0]
                    have(n)
                    for tb in range(HB):
                        rows((what, hf, n0, tb), src, TH, tb * P, n)
                        if tb == HB - 1:
                            used(n)
                        yield

            def route(l, hf):
                copied()
                for hh in range(PH + 1):
                    if hh < PH:
                        n = W["pq", l, hf][hh // 2]
                        have(n)
                        for sd in range(2):
                            columns(("pq", l, hf, hh, sd), hTh, 2 * (hh % 2) + sd, n)
                        if hh % 2:
                            used(n)
                    if hh > 0:
                        g = hh - 1
                        seq = (2 * l + hf) * PH + g
                        pe.wait_ge(s["lin_free"], TILE["pq", l, hf, g, 1] + 1)
                        pe.wait_ge(s["k_in"], 32 * (l + 1))
                        if seq >= 2:
                            pe.wait_ge(s["scores_read"], seq - 1)
                        for sd in range(2):
                            for tb in range(HB):
                                c = (sd * HB + tb) * P
                                i = pe.matmul(ps[:, 4 + g % 2, c:c + P], q_sb[2 * (g % 2) + sd][:, tb * P:(tb + 1) * P],
                                              k12s[:, sd * NKEYS:(sd + 1) * NKEYS], start=True, stop=True)
                        i.then_inc(s["scores_full"], 1)
                    yield
                for _ in range(2 * HB + 1):
                    yield

            def ple(l, hf):
                for _ in range(HB):
                    yield
                yield from turn_over(("ffn", l), hf, h, 0)
                copied()
                pe.wait_ge(s["ple_in"], 32 * (2 * l + hf + 1))
                for n0 in range(2):
                    n = W["pg", l, hf][n0]
                    have(n)
                    for tb in range(HB):
                        rows(("pg", l, hf, n0, tb), hTh, TH, tb * P, n)
                        linear(("pw", l, hf, n0, tb), [(pTs[:, k * TH + tb * P:k * TH + (tb + 1) * P],
                                                        plw[:, k * D + n0 * HALF:k * D + (n0 + 1) * HALF]) for k in range(2)])
                        if tb == HB - 1:
                            used(n)
                        yield

            def strip(hf, hd, kb, c0=0, c1=None):
                w = TH - first_q(hf, kb)
                o = strip_at(hf, kb) + c0
                return ps[:, 2 * (hd % 2) + o // HALF, :][:, o % HALF:o % HALF + (w if c1 is None else c1) - c0]

            def scores(hf, hd):
                rw = slice(64 * (hd % 2), 64 * (hd % 2) + 64)
                c = hd // 2
                if hf * HEADS + hd >= 2:
                    pe.wait_ge(s["weights_set"], hf * HEADS + hd - 1)
                for kb in hk_blocks(hf):
                    i = pe.matmul(strip(hf, hd, kb), KT[rw, c * T + kb * P:c * T + (kb + 1) * P],
                                  QT[rw, c * TH + first_q(hf, kb):(c + 1) * TH], start=(kb % 2 == 0), stop=True,
                                  skip_group_check=True)
                i.then_inc(s["z_full"], 1)

            def log_weights(hf, hd):
                pe.wait_ge(s["soft_set"], 2 * (hf * HEADS + hd) + 2)
                x = sp_[hd % 2]
                for kb in hk_blocks(hf):
                    for jb in hk_blocks(hf):
                        if jb >= kb:
                            o = strip_at(hf, jb)
                            i = pe.matmul(strip(hf, hd, kb, first_q(hf, jb) - first_q(hf, kb)), ntri[:, :] if jb == kb else nones[:, :],
                                          x[:, o:o + TH - first_q(hf, jb)], start=False, stop=True, skip_group_check=True)
                    if kb >= HB * hf:
                        i = pe.matmul(strip(hf, hd, kb, 0, P), ident[:, :], hide[:, :], start=False, stop=True,
                                      skip_group_check=True)
                i.then_inc(s["sum_full"], 1)

            def values(hf, hd):
                rw = slice(64 * (hd % 2), 64 * (hd % 2) + 64)
                seq = hf * HEADS + hd
                pe.wait_ge(s["weights_set"], seq + 1)
                if seq >= 2:
                    pe.wait_ge(s["o_copied"], seq - 1)
                for kb in hk_blocks(hf):
                    o = strip_at(hf, kb)
                    i = pe.matmul(ps[rw, 4, first_q(hf, kb):TH], V[:, kb * D + hd * HD:kb * D + (hd + 1) * HD],
                                  ez[hd % 2][:, o:o + TH - first_q(hf, kb)], start=(kb == 0), stop=True, skip_group_check=True)
                i.then_inc(s["o_full"], 1)

            def attention(hf):
                copied()
                pe.wait_ge(s["scores_read"], (2 * 0 + 2 + hf) * PH)
                for hd in range(0, HEADS, 2):
                    for e in range(2):
                        if hd > 0:
                            values(hf, hd - 2 + e)
                    for e in range(2):
                        scores(hf, hd + e)
                    yield
                    for e in range(2):
                        log_weights(hf, hd + e)
                    yield
                for e in range(2):
                    values(hf, HEADS - 2 + e)
                yield

            def between_layers(hf):
                yield from ple(0, hf)
                for _ in range(HB):
                    yield
                yield from turn_over(("kv", 1), hf, hk, HB * hf)
                yield from turn_over(("ple", 0), hf, h, 0)
                yield from column_steps("k", hf, hkT)
                yield from row_steps("v", hf, hkT)
                yield from column_steps("q", hf, hTh)
                yield from attention(hf)
                pe.wait_ge(s["o_copied"], (hf + 1) * HEADS)
                yield from row_steps("o", hf, QT)
                for _ in range(HB):
                    yield
                yield from turn_over(("mix", 1), hf, h, 0)
                yield from route(1, hf)

            def block_start(l, tb):
                if l * TB + tb > 0:
                    pe.wait_ge(s["ffn_read"], l * TB + tb)
                for n0 in range(2):
                    pe.matmul(bank(6 + n0), zrow[0:1, 0:P], zrow[0:1, :], start=True, stop=False, skip_group_check=True)

            def block_end(l, tb):
                for n0 in range(2):
                    i = pe.matmul(bank(6 + n0), zrow[0:1, 0:P], zrow[0:1, :], start=False, stop=True, skip_group_check=True)
                i.then_inc(s["ffn_full"], 1)

            def group(l, tb, n, g, j=0):
                pe.wait_ge(s["diag_set"], n + (TURN + 4) + j * TURN)
                for r in range(4):
                    q = (4 * g + r) % RING
                    pe.wait_ge(v_in[q], 16 * ((n + r) // RING + 1) + j * 16 * (TURN // RING))
                    for n0 in range(2):
                        i = pe.matmul(bank(6 + n0), diag[q], v_ring[q][:, n0 * HALF:(n0 + 1) * HALF],
                                      start=False, stop=False, skip_group_check=True)
                    i.then_inc(s["v_used"], 1)

            def block_loop(l, tb):
                n = (l * TB + tb) * SLOTS
                block_start(l, tb)
                for g in range(4):
                    group(l, tb, n + 4 * g, g)
                with pe.Fori(1, SLOTS // TURN) as j:
                    for g in range(4):
                        group(l, tb, n + 4 * g, g, j)
                block_end(l, tb)

            pe.wait_ge(s["y_taken"], KC + 1)
            pe.wait_ge(s["bu_read"], PAIRS)
            for n0 in range(2):
                for g in range(2):
                    have(W["glu"][2 * n0 + g])
                for tb in range(TB):
                    for g in range(2):
                        rows(("glu", n0, tb, g), yT, T, tb * P, W["glu"][2 * n0 + g])
                for g in range(2):
                    used(W["glu"][2 * n0 + g])

            def first_route(hf):
                yield from turn_over(("mix", 0), hf, h, 0)
                yield from route(0, hf)

            alone(HB + STEPS_ROUTE, first_route(0))
            pe.sem_inc(s["v_used"], RING)
            weave(0, [0], group, HB + STEPS_ROUTE, first_route(1), 0, block_start, block_end)
            block_loop(0, 1)
            weave(0, [2, 3], group, STEPS_PLE + STEPS_MID + STEPS_ROUTE, between_layers(0), 0, block_start, block_end)
            weave(1, [0, 1], group, STEPS_PLE + STEPS_MID + STEPS_ROUTE, between_layers(1), 0, block_start, block_end)
            weave(1, [2], group, STEPS_PLE, ple(1, 0), 0, block_start, block_end)
            block_loop(1, 3)
            alone(STEPS_PLE, ple(1, 1))

        @block.scalar
        def _(act):
            step = Steps(act, s["act_step"])
            act.wait_ge(s["par_in"], 80)
            act.sem_inc(s["y_taken"], 1)
            act.activation(par["dt"], par["dt"], ACT.Exp).then_inc(s["sin_done"], 1)
            act.wait_ge(s["dve_step"], 1)
            act.activation(par["rho"], par["t0"], ACT.Exp).then_inc(s["sin_done"], 1)
            act.wait_ge(s["dve_step"], 7)
            act.activation(par["s"], par["th"], ACT.Sin).then_inc(s["sin_done"], 1)
            act.activation(par["t1"], par["th"], ACT.Sin, scale=0.5).then_inc(s["sin_done"], 1)

            def pre(b, q, turn):
                act.wait_ge(s["u_full"], b + 1)
                if not first(turn):
                    act.wait_ge(s["pair_done"], (b - 1) * CHB)
                act.copy(ub[q], bank(6 + q)).then_inc(s["u_copied"], 1)
                act.wait_ge(s["bt_full"], b + 1)
                for r in range(2):
                    act.copy(bT[q][r], ps[:, 6 + q, r * P:(r + 1) * P]).then_inc(s["bt_copied"], 1)

            def main(b, q):
                act.wait_ge(s["pair_done"], b * CHB + CHB)
                act.activation(yT[:, bass.ds(b * T, T)], bank(4 + q), ACT.Gelu_apprx_tanh).then_inc(s["y_taken"], 1)

            pre(0, 0, 0)
            pre(1, 1, 0)
            main(0, 0)
            with act.Fori(0, KC // 2 - 1) as it:
                pre(2 * it + 2, 0, it + 1)
                main(2 * it + 1, 1)
                pre(2 * it + 3, 1, it + 1)
                main(2 * it + 2, 0)
            main(KC - 1, 1)

            def store(eng, hf):
                rr = slice(HB * hf * P, HB * (hf + 1) * P)
                eng.dma_start(out[rr, :].rearrange("(b p) d -> p b d", p=P),
                              h[:, HB * hf * D:HB * (hf + 1) * D].rearrange("p (b d) -> p b d", b=HB)).then_inc(s["out_done"], 16)

            def gate(key, dst, n):
                t = TILE[key]
                act.wait_ge(s["lin_full"], t + 2)
                if n >= 2:
                    act.wait_ge(s["lin_free"], t - 2)
                act.activation(dst, bank(t % 4), ACT.Sigmoid).then_inc(s["gate_sig"], 1)

            lns = [0]

            def root(tbs):
                lns[0] += 1
                act.wait_ge(s["var_set"], lns[0])
                act.activation(rstd[:, tbs], rstd[:, tbs], ACT.Sqrt).then_inc(s["std_set"], 1)

            def evacuate(key, dst, cols=HALF, scale=None, tiles=False):
                t = TILE[key]
                act.wait_ge(s["lin_full"], t + 1)
                src = bank(t % 4)[:, 0:cols]
                if tiles:
                    src = src.rearrange("p (k t) -> p k t", k=4)
                if scale is None:
                    act.copy(dst, src).then_inc(s["lin_free"], 1)
                else:
                    act.mul(dst, src, scale).then_inc(s["lin_free"], 1)

            def turn_over(what, hf, dst):
                for tb in range(HB * hf, HB * hf + HB):
                    for q in range(2):
                        o = (tb - HB * hf) * P
                        evacuate(("turn", what, tb, q),
                                 dst[:, q * 4 * TH:(q + 1) * 4 * TH].rearrange("p (k t) -> p k t", k=4)[:, :, o:o + P], tiles=True)
                    yield

            def norm_steps(hf):
                for tb in range(HB * hf, HB * hf + HB):
                    root(slice(tb, tb + 1))
                    yield

            def route(l, hf):
                for hh in range(PH + 1):
                    if hh < PH:
                        for sd in range(2):
                            evacuate(("pq", l, hf, hh, sd), q_sb[2 * (hh % 2) + sd], TH)
                    yield
                for n in range(2 * HB + 1):
                    if n == 0:
                        act.wait_ge(s["gap_set"], 2 * l + hf + 1)
                        g = gates[:, HB * hf * SLOTS:HB * (hf + 1) * SLOTS]
                        act.activation(g, g, ACT.Exp).then_inc(s["gap_exp"], 1)
                    yield

            def ple(l, hf):
                yield from norm_steps(hf)
                yield from turn_over(("ffn", l), hf, hTh)
                for n0 in range(2):
                    for tb in range(HB):
                        n = n0 * HB + tb
                        gate(("pg", l, hf, n0, tb), sgp[n % 2], n)
                        yield

            def column_steps(what, hf, place_of, scale=None):
                for n0 in range(2):
                    for m in range(4):
                        evacuate((what, hf, n0, m), place_of(4 * n0 + m), TH, scale)
                        if m % 2:
                            yield

            def strips(hf, hd):
                return ps[:, 2 * (hd % 2):2 * (hd % 2) + 2, :].rearrange("p b n -> p (b n)")[:, 0:ZW[hf]]

            def soft(hf, hd):
                x = ez[hd % 2][:, 0:ZW[hf]]
                seq = 3 * (hf * HEADS + hd)
                act.wait_ge(s["z_full"], hf * HEADS + hd + 1)
                act.activation(x, strips(hf, hd), ACT.Abs).then_inc(s["z_exp"], 1)
                act.wait_ge(s["z_exp"], seq + 1)
                act.activation(x, x, ACT.Exp, scale=-1.0).then_inc(s["z_exp"], 1)
                act.wait_ge(s["z_exp"], seq + 2)
                act.activation(x, x, ACT.Ln, bias=1.0).then_inc(s["z_exp"], 1)

            def outputs(hf, hd):
                rw = slice(64 * (hd % 2), 64 * (hd % 2) + 64)
                act.wait_ge(s["o_full"], hf * HEADS + hd + 1)
                act.copy(QT[rw, (hd // 2) * TH:(hd // 2 + 1) * TH], ps[rw, 4, 0:TH]).then_inc(s["o_copied"], 1)

            def attention(hf):
                for hd in range(0, HEADS, 2):
                    for e in range(2):
                        if hd > 0:
                            outputs(hf, hd - 2 + e)
                    for e in range(2):
                        soft(hf, hd + e)
                    yield
                    for e in range(2):
                        act.wait_ge(s["sum_full"], hf * HEADS + hd + e + 1)
                        act.activation(ez[e][:, 0:ZW[hf]], strips(hf, hd + e), ACT.Exp).then_inc(s["weights_set"], 1)
                    yield
                for e in range(2):
                    outputs(hf, HEADS - 2 + e)
                yield

            def between_layers(hf):
                yield from ple(0, hf)
                yield from norm_steps(hf)
                yield from turn_over(("kv", 1), hf, hkT)
                yield from turn_over(("ple", 0), hf, hTh)
                yield from column_steps("k", hf, lambda c: KT[:, c * T + hf * TH:c * T + (hf + 1) * TH])
                for n0 in range(2):
                    for tb in range(HB):
                        o = (HB * hf + tb) * D + n0 * HALF
                        evacuate(("v", hf, n0, tb), V[:, o:o + HALF])
                        yield
                yield from column_steps("q", hf, lambda c: QT[:, c * TH:(c + 1) * TH], HD ** -0.5)
                yield from attention(hf)
                for _ in range(4):
                    yield
                yield from norm_steps(hf)
                yield from turn_over(("mix", 1), hf, hTh)
                yield from route(1, hf)

            def group(l, tb, n, g, j=None):
                loop = 0 if j is None else j * TURN
                c = (4 * g) % TURN
                act.wait_ge(s["u_used"], n + (RING + 4) + loop)
                step.did(act.activation(gelu[:, c:c + 4], actv[:, c:c + 4], ACT.Gelu_apprx_tanh))
                if j is None:
                    step.settle()
                else:
                    reg_wait(act, s["act_step"], step.base + step.n)
                for r in range(4):
                    o = tb * SLOTS + 4 * g + r
                    gt = gates[:, o:o + 1] if j is None else gates[:, bass.ds(j * TURN + o, 1)]
                    step.did(act.activation(gg[:, c + r:c + r + 1], gt, ACT.Copy, scale=gelu[:, c + r:c + r + 1]))
                step.settle()
                act.wait_ge(s["v_used"], n + 4 + loop)
                for r in range(4):
                    act.activation(diag[(4 * g + r) % RING], ident[:, :], ACT.Copy,
                                   scale=gg[:, c + r:c + r + 1]).then_inc(s["diag_set"], 1)

            def block_loop(l, tb):
                n = (l * TB + tb) * SLOTS
                for g in range(4):
                    group(l, tb, n + 4 * g, g)
                with step.loop(SLOTS // TURN - 1, 4 * 5) as i:
                    for g in range(4):
                        group(l, tb, n + 4 * g, g, i + 1)

            for n0 in range(2):
                for tb in range(TB):
                    n = n0 * TB + tb
                    t = TILE["glu", n0, tb, 1]
                    act.wait_ge(s["lin_full"], t + 1)
                    if n >= 2:
                        act.wait_ge(s["lin_free"], t - 3)
                    act.activation(sgm[n % 2], bank(t % 4), ACT.Sigmoid).then_inc(s["gate_sig"], 1)
            act.sem_inc(s["diag_set"], TURN)
            root(slice(0, TB))

            def first_route(hf):
                yield from turn_over(("mix", 0), hf, hTh)
                yield from route(0, hf)

            alone(HB + STEPS_ROUTE, first_route(0))
            weave(0, [0], group, HB + STEPS_ROUTE, first_route(1), 1)
            block_loop(0, 1)
            weave(0, [2, 3], group, STEPS_PLE + STEPS_MID + STEPS_ROUTE, between_layers(0), 1)
            weave(1, [0, 1], group, STEPS_PLE + STEPS_MID + STEPS_ROUTE, between_layers(1), 1)
            weave(1, [2], group, STEPS_PLE, ple(1, 0), 1)
            act.wait_ge(s["h_set"], H["ple", 1, 1])
            store(act, 0)
            block_loop(1, 3)
            alone(STEPS_PLE, ple(1, 1))
            act.wait_ge(s["h_set"], H["ple", 1, 3])
            store(act, 1)
            act.wait_ge(s["out_done"], 32)

        @block.vector
        def _(dve):
            step = Steps(dve, s["dve_step"])

            def tt(o_, x, y, op):
                step.did(dve.tensor_tensor(o_, x, y, op))

            def ts(o_, x, c1, c2, op0, op1=None):
                step.did(dve.tensor_scalar(o_, x, c1, c2, op0, op1) if op1 is not None else dve.tensor_scalar(o_, x, c1, None, op0))

            def stt(o_, x, c, y, op0, op1):
                step.did(dve.scalar_tensor_tensor(out=o_, in0=x, scalar=c, in1=y, op0=op0, op1=op1))

            lr, li, dt, t0, t1, t2, rho, th, c, sn, fr, fi = (par[n] for n in (
                "lr", "li", "dt", "t0", "t1", "t2", "rho", "th", "c", "s", "fr", "fi"))
            dve.wait_ge(s["sin_done"], 1)
            tt(t0, lr, dt, ALU.mult)
            tt(th, li, dt, ALU.mult)
            step.settle()
            ts(t2, th, 1.0 / (2 * math.pi), ROUND, ALU.mult, ALU.add)
            step.settle()
            ts(t2, t2, ROUND, None, ALU.subtract)
            step.settle()
            stt(th, t2, -TWO_PI_HI, th, ALU.mult, ALU.add)
            step.settle()
            stt(th, t2, -TWO_PI_LO, th, ALU.mult, ALU.add)
            step.settle()
            ts(th, th, PI_BELOW, -PI_BELOW, ALU.min, ALU.max)
            dve.wait_ge(s["sin_done"], 4)
            tt(c, t1, t1, ALU.mult)
            step.settle()
            ts(c, c, -2.0, 1.0, ALU.mult, ALU.add)
            step.settle()

            def normalise(cc, ss):
                tt(t0, cc, cc, ALU.mult)
                tt(t1, ss, ss, ALU.mult)
                step.settle()
                tt(t0, t0, t1, ALU.add)
                step.settle()
                ts(t0, t0, -0.5, 1.5, ALU.mult, ALU.add)
                step.settle()
                tt(cc, cc, t0, ALU.mult)
                tt(ss, ss, t0, ALU.mult)
                step.settle()

            normalise(c, sn)
            Wp = [(wc[:, lv * PAIRS:(lv + 1) * PAIRS], ws[:, lv * PAIRS:(lv + 1) * PAIRS]) for lv in range(LEVELS)]
            step.did(dve.tensor_copy(Wp[0][0], c))
            step.did(dve.tensor_copy(Wp[0][1], sn))
            step.settle()
            for lv in range(1, LEVELS):
                (pc, ps_), (qc, qs) = Wp[lv - 1], Wp[lv]
                tt(t0, pc, pc, ALU.mult)
                tt(t1, ps_, ps_, ALU.mult)
                stt(qs, pc, 2.0, ps_, ALU.mult, ALU.mult)
                step.settle()
                tt(qc, t0, t1, ALU.subtract)
                step.settle()
                normalise(qc, qs)
            tt(t0, rho, c, ALU.mult)
            tt(t1, rho, sn, ALU.mult)
            tt(t2, lr, lr, ALU.mult)
            tt(th, li, li, ALU.mult)
            step.settle()
            ts(t0, t0, -1.0, None, ALU.add)
            tt(t2, t2, th, ALU.add)
            step.settle()
            step.did(dve.reciprocal(t2, t2))
            tt(fr, t0, lr, ALU.mult)
            tt(th, t1, li, ALU.mult)
            tt(fi, t1, lr, ALU.mult)
            tt(c, t0, li, ALU.mult)
            step.settle()
            tt(fr, fr, th, ALU.add)
            tt(fi, fi, c, ALU.subtract)
            step.settle()
            tt(fr, fr, t2, ALU.mult)
            step.settle()
            dve.tensor_tensor(fi, fi, t2, ALU.mult).then_inc(s["trig_set"], 1)
            dve.wait_ge(s["trig_set"], 1)
            dve.wait_ge(s["const_set"], 9)

            def pre(b, q, turn):
                dve.wait_ge(s[f"win_in{q}"], turn * 112 + 112)
                if not first(turn):
                    dve.wait_ge(s["pair_done"], (b - 1) * CHB)
                br, bi = (braw[q][r].rearrange("p (j c) -> p j c", j=CHB) for r in range(2))
                m = [bmul[k].rearrange("p (j c) -> p j c", j=CHB) for k in range(4)]
                frb = fr[:, bass.ds(b * CHB, CHB)].unsqueeze(2).to_broadcast([P, CHB, GROUP])
                fib = fi[:, bass.ds(b * CHB, CHB)].unsqueeze(2).to_broadcast([P, CHB, GROUP])
                tt(m[0], br, frb, ALU.mult)
                tt(m[1], bi, fib, ALU.mult)
                tt(m[2], br, fib, ALU.mult)
                tt(m[3], bi, frb, ALU.mult)
                step.settle()
                for r, op in ((0, ALU.subtract), (1, ALU.add)):
                    o4 = bbd[q][r].rearrange("p (j c) -> p j c", j=CHB)
                    for g in range(2):
                        pp = slice(64 * g, 64 * g + 64)
                        dve.tensor_tensor(o4[pp, :, GROUP * g:GROUP * g + GROUP], m[2 * r][pp], m[2 * r + 1][pp],
                                          op).then_inc(s["bbar_set"], 1)
                ts(cbd[q][1], cbd[q][1], -1.0, None, ALU.mult)
                dve.tensor_scalar(dgD[q], ident[:, :], dsk[:, bass.ds(b, 1)], None, ALU.mult).then_inc(s["bbar_set"], 1)
                step.settle()

            def main(b, q):
                dve.wait_ge(s["tables_set"], 2 * (b + 1))
                for j in range(CHB):
                    cj, sj = (tab[q][r][:, j * T:(j + 1) * T] for r in range(2))
                    k = 2 * (j % 2)
                    dve.wait_ge(s["bu_full"], b * CHB + (j + 1))
                    tt(rot[0], bank(k), cj, ALU.mult)
                    tt(rot[1], bank(k + 1), sj, ALU.mult)
                    tt(rot[2], bank(k + 1), cj, ALU.mult)
                    dve.tensor_tensor(rot[3], bank(k), sj, ALU.mult).then_inc(s["bu_read"], 1)
                    step.settle()
                    dve.wait_ge(s["bu_read"], b * CHB + (j + 1))
                    tt(vin[0], rot[0], rot[1], ALU.add)
                    tt(vin[1], rot[2], rot[3], ALU.subtract)
                    step.settle()
                    decay = rho[:, bass.ds(b * CHB + j, 1)].to_broadcast([P, T])
                    for r in range(2):
                        step.did(dve.tensor_tensor_scan(sc_r[r], decay, vin[r], 0.0, ALU.mult, ALU.add))
                    step.settle()
                    if not (first(b) and j < 2):
                        dve.wait_ge(s["pair_done"], b * CHB + (j - 1))
                    pr = prod[j % 2]
                    tt(pr[0], sc_r[0], cj, ALU.mult)
                    stt(pr[1], sc_r[1], -1.0, sj, ALU.mult, ALU.mult)
                    tt(pr[2], sc_r[0], sj, ALU.mult)
                    i = dve.tensor_tensor(pr[3], sc_r[1], cj, ALU.mult)
                    i.then_inc(s["prods_set"], 1)
                    step.settle()

            pre(0, 0, 0)
            pre(1, 1, 0)
            main(0, 0)
            per_pre, per_main = 5, 3 + 2 + 2 + 3
            with step.loop(KC // 2 - 1, 2 * (per_pre + CHB * per_main)) as it:
                pre(2 * it + 2, 0, it + 1)
                main(2 * it + 1, 1)
                pre(2 * it + 3, 1, it + 1)
                main(2 * it + 2, 0)
            main(KC - 1, 1)

            dve.wait_ge(s["h_in"], 16)
            gates_seen = [0]

            def gated(key, other, sg, tb, n0, keep):
                gates_seen[0] += 1
                dve.wait_ge(s["gate_sig"], gates_seen[0])
                dve.wait_ge(s["lin_full"], TILE[other] + 1)
                tt(sg, sg, bank(TILE[other] % 4), ALU.mult)
                step.settle()
                dve.scalar_tensor_tensor(out=hb(tb, n0), in0=hb(tb, n0), scalar=keep, in1=sg, op0=ALU.mult,
                                         op1=ALU.add).then_inc(s["lin_free"], 2)

            for n0 in range(2):
                for tb in range(TB):
                    gated(None, ("glu", n0, tb, 0), sgm[tb % 2], tb, n0, ALPHA)
            dve.wait_ge(s["lin_free"], TILE["glu", 1, TB - 1, 1] + 1)

            lns = [0]
            loads = [0]

            def layer_norm(what, tbs, dst, base, last):
                a0, n = tbs[0], len(tbs)
                for tb in tbs:
                    for n0 in range(2):
                        step.did(dve.bn_stats(stat[:, (2 * tb + n0) * 6:(2 * tb + n0 + 1) * 6], hb(tb, n0)))
                step.settle()
                for tb in tbs:
                    step.did(dve.bn_aggr(mv[:, 2 * tb:2 * tb + 2], stat[:, 12 * tb:12 * tb + 12]))
                step.settle()
                rs = rstd[:, a0:a0 + n]
                lns[0] += 1
                dve.tensor_scalar(rs, mv[:, :].rearrange("p (b m) -> p b m", m=2)[:, a0:a0 + n, 1], LN_EPS, None,
                                  ALU.add).then_inc(s["var_set"], 1)
                dve.wait_ge(s["std_set"], lns[0])
                step.did(dve.reciprocal(rs, rs))
                step.settle()
                dve.wait_ge(s["ln_in"], 32 * (loads[0] + 1))

                def d(tb):
                    return dst[:, (tb - base) * D:(tb - base + 1) * D]

                for tb in tbs:
                    ts(d(tb), hb(tb), mv[:, 2 * tb:2 * tb + 1], rstd[:, tb:tb + 1], ALU.subtract, ALU.mult)
                step.settle()
                for tb in tbs:
                    tt(d(tb), d(tb), lnp[:, 0:D], ALU.mult)
                step.settle()
                for tb in tbs:
                    dve.tensor_tensor(d(tb), d(tb), lnp[:, D:2 * D], ALU.add).then_inc(s["h_set"], 1)
                dve.wait_ge(s["h_set"], H[what + (tbs[-1],)])
                if last:
                    loads[0] += 1
                    dve.sem_inc(s["lnp_free"], 1)

            def norm_steps(what, hf, dst, base, last=True):
                for tb in range(HB * hf, HB * hf + HB):
                    layer_norm(what, [tb], dst, base, last and tb % HB == HB - 1)
                    yield

            def nothing(n):
                for _ in range(n):
                    yield

            def route(l, hf):
                seq = 2 * l + hf
                yield
                for hh in range(PH):
                    e = hh % 2
                    dve.wait_ge(s["scores_full"], seq * PH + hh + 1)
                    todo = [(tb, sd) for tb in range(HB) for sd in range(2)]

                    def S(tb, sd):
                        return ps[:, 4 + e, (sd * HB + tb) * P:(sd * HB + tb + 1) * P]

                    def kv8(tb, sd, c):
                        return val[sd][:, tb * TOPK + 8 * c:tb * TOPK + 8 * c + 8]

                    def ki8(tb, sd, c):
                        o = tb * SLOTS + hh * TOPK + 8 * c
                        return key[sd][:, o:o + 8].bitcast(U32)

                    def bv8(t, tb, c):
                        o = tb * SLOTS + hh * TOPK + 8 * c
                        return t[:, o:o + 8]

                    for tb, sd in todo:
                        step.did(dve.max(kv8(tb, sd, 0), S(tb, sd)))
                    step.settle()
                    for tb, sd in todo:
                        step.did(dve.max_index(ki8(tb, sd, 0), kv8(tb, sd, 0), S(tb, sd)))
                    for tb, sd in todo:
                        i = dve.match_replace(rest[2 * tb + sd], kv8(tb, sd, 0), S(tb, sd), LOWEST)
                        if (tb, sd) != todo[-1]:
                            step.did(i)
                    i.then_inc(s["scores_read"], 1)
                    step.settle()
                    dve.wait_ge(s["scores_read"], seq * PH + hh + 1)
                    for tb, sd in todo:
                        step.did(dve.max(kv8(tb, sd, 1), rest[2 * tb + sd]))
                    step.settle()
                    for tb, sd in todo:
                        step.did(dve.max_index(ki8(tb, sd, 1), kv8(tb, sd, 1), rest[2 * tb + sd]))
                    for tb in range(HB):
                        v1 = val[0][:, tb * TOPK:(tb + 1) * TOPK].unsqueeze(2).to_broadcast([P, TOPK, TOPK])
                        v2 = val[1][:, tb * TOPK:(tb + 1) * TOPK].unsqueeze(1).to_broadcast([P, TOPK, TOPK])
                        tt(cand[tb].rearrange("p (i j) -> p i j", i=TOPK), v1, v2, ALU.add)
                    step.settle()
                    for tb in range(HB):
                        step.did(dve.max(bv8(best, tb, 0), cand[tb]))
                    step.settle()
                    for tb in range(HB):
                        step.did(dve.max_index(bv8(bpos, tb, 0).bitcast(U32), bv8(best, tb, 0), cand[tb]))
                        step.did(dve.match_replace(cand2[tb], bv8(best, tb, 0), cand[tb], LOWEST))
                    step.settle()
                    for tb in range(HB):
                        step.did(dve.max(bv8(best, tb, 1), cand2[tb]))
                    step.settle()
                    for tb in range(HB):
                        step.did(dve.max_index(bv8(bpos, tb, 1).bitcast(U32), bv8(best, tb, 1), cand2[tb]))
                    if hh < PH - 1:
                        yield
                step.settle()
                gs = gates[:, HB * hf * SLOTS:HB * (hf + 1) * SLOTS]
                b3 = best.rearrange("p (n k) -> p n k", k=TOPK)
                g3 = gs.rearrange("p (n k) -> p n k", k=TOPK)
                dve.tensor_tensor(g3, b3, b3[:, :, 0:1].to_broadcast([P, HB * PH, TOPK]), ALU.subtract).then_inc(s["gap_set"], 1)
                bu = bpos.bitcast(U32)
                step.did(dve.tensor_scalar(ksel[0].bitcast(U32), bu, 4, None, ALU.logical_shift_right))
                step.did(dve.tensor_scalar(ksel[1].bitcast(U32), bu, 15, None, ALU.bitwise_and))
                for sd in range(2):
                    step.did(dve.tensor_copy(key[sd], key[sd].bitcast(U32)))
                step.settle()
                for sd in range(2):
                    step.did(dve.tensor_copy(ksel[sd], ksel[sd].bitcast(U32)))
                step.settle()
                yield
                for tb in range(HB):
                    cols = slice(tb * SLOTS, (tb + 1) * SLOTS)
                    for sd in range(2):
                        tt(eq.rearrange("p (n j) -> p n j", j=TOPK), ksel[sd][:, cols].unsqueeze(2).to_broadcast([P, SLOTS, TOPK]),
                           iota16[:, :].unsqueeze(1).to_broadcast([P, SLOTS, TOPK]), ALU.is_equal)
                        step.settle()
                        e4 = eq.rearrange("p (h k j) -> p h k j", h=PH, k=TOPK)
                        k4 = key[sd][:, cols].rearrange("p (h j) -> p h j", h=PH).unsqueeze(2).to_broadcast([P, PH, TOPK, TOPK])
                        tt(e4, e4, k4, ALU.mult)
                        step.settle()
                        step.did(dve.tensor_reduce(esel[sd], eq.rearrange("p (n j) -> p n j", j=TOPK), AX_X, ALU.add))
                        step.settle()
                        if sd == 0:
                            yield
                    stt(esel[0], esel[0], float(NKEYS), esel[1], ALU.mult, ALU.add)
                    step.settle()
                    o = (HB * hf + tb) * SLOTS
                    ts(idx[:, o:o + SLOTS], esel[0], float(l * EXPERTS), None, ALU.add)
                    yield
                dve.wait_ge(s["gap_exp"], seq + 1)
                step.did(dve.tensor_reduce(rsum, g3, AX_X, ALU.add))
                step.settle()
                step.did(dve.reciprocal(rinv, rsum))
                step.settle()
                dve.tensor_tensor(g3, g3, rinv.unsqueeze(2).to_broadcast([P, HB * PH, TOPK]), ALU.mult).then_inc(s["idx_set"], 1)
                yield

            def ple(l, hf):
                yield from norm_steps(("ffn", l), hf, h, 0, last=(l == 0 or hf == 1))
                yield from nothing(HB)
                for n0 in range(2):
                    for tb in range(HB):
                        gated(None, ("pw", l, hf, n0, tb), sgp[tb % 2], HB * hf + tb, n0, 1.0)
                        if n0 == 1 and tb == HB - 1:
                            dve.wait_ge(s["lin_free"], TILE["pw", l, hf, 1, tb] + 1)
                            dve.sem_inc(s["h_set"], HB)
                        yield

            def attention(hf):
                for hd in range(0, HEADS, 2):
                    for e in range(2):
                        x, w = sp_[e], ZW[hf]
                        zf = ps[:, 2 * e:2 * e + 2, :].rearrange("p b n -> p (b n)")[:, 0:w]
                        dve.wait_ge(s["z_exp"], 3 * (hf * HEADS + hd + e) + 3)
                        stt(x[:, 0:w], zf, 0.0, ez[e][:, 0:w], ALU.max, ALU.add)
                        step.settle()
                        for kb in range(HB * hf, HB * hf + HB):
                            v = x[:, strip_at(hf, kb):strip_at(hf, kb) + P]
                            dve.tensor_tensor(v, v, seen[:, :], ALU.mult).then_inc(s["soft_set"], 1)
                    yield
                    yield
                yield

            def between_layers(hf):
                yield from ple(0, hf)
                yield from norm_steps(("kv", 1), hf, hk, HB * hf)
                yield from nothing(2 * HB + 4 + 4 + 4)
                yield from attention(hf)
                for n0 in range(2):
                    for tb in range(HB):
                        t = TILE["o", hf, n0, tb]
                        dve.wait_ge(s["lin_full"], t + 1)
                        x = hb(HB * hf + tb, n0)
                        dve.scalar_tensor_tensor(out=x, in0=x, scalar=ALPHA, in1=bank(t % 4), op0=ALU.mult,
                                                 op1=ALU.add).then_inc(s["lin_free"], 1)
                        if n0 == 1 and tb == HB - 1:
                            dve.wait_ge(s["lin_free"], t + 1)
                        yield
                yield from norm_steps(("mix", 1), hf, h, 0)
                yield from nothing(HB)
                yield from route(1, hf)

            def ffn_sum(k):
                dve.wait_ge(s["ffn_full"], k + 1)
                dve.scalar_tensor_tensor(out=hb(k % TB), in0=hb(k % TB), scalar=ALPHA,
                                         in1=ps[:, 6:8, :].rearrange("p b n -> p (b n)"), op0=ALU.mult,
                                         op1=ALU.add).then_inc(s["ffn_read"], 1)
                dve.wait_ge(s["ffn_read"], k + 1)

            def group(l, tb, n, g, j=0):
                dve.wait_ge(s["diag_set"], n + 4 + j * TURN)
                for r in range(4):
                    q = (4 * g + r) % RING
                    dve.wait_ge(u_in[q], 16 * ((n + r) // RING + 1) + j * 16 * (TURN // RING))
                    c = (4 * g + r) % TURN
                    dve.tensor_tensor_reduce(u_ring[q], u_ring[q], hb(tb), 1.0, 0.0, ALU.mult, ALU.add,
                                             actv[:, c:c + 1]).then_inc(s["u_used"], 1)
                if isinstance(j, int) and g == 0 and n > 0:
                    ffn_sum(n // SLOTS - 1)

            def block_loop(l, tb):
                n = (l * TB + tb) * SLOTS
                for g in range(4):
                    group(l, tb, n + 4 * g, g)
                with dve.Fori(1, SLOTS // TURN) as j:
                    for g in range(4):
                        group(l, tb, n + 4 * g, g, j)

            def first_route(hf):
                yield from nothing(HB)
                yield from route(0, hf)

            dve.sem_inc(s["u_used"], RING)
            layer_norm(("mix", 0), list(range(TB)), h, 0, True)
            dve.wait_ge(s["tri_set"], 8)
            step.did(dve.tensor_copy(iota16[:, :], iota16[:, :].bitcast(U32)))
            alone(HB + STEPS_ROUTE, first_route(0))
            weave(0, [0], group, HB + STEPS_ROUTE, first_route(1), 1)
            block_loop(0, 1)
            weave(0, [2, 3], group, STEPS_PLE + STEPS_MID + STEPS_ROUTE, between_layers(0), 1)
            weave(1, [0, 1], group, STEPS_PLE + STEPS_MID + STEPS_ROUTE, between_layers(1), 1)
            weave(1, [2], group, STEPS_PLE, ple(1, 0), 1)
            block_loop(1, 3)
            ffn_sum(DEPTH * TB - 1)
            alone(STEPS_PLE, ple(1, 1))

        @block.gpsimd
        def _(pool):
            step = Steps(pool, s["pool_step"])
            step.did(pool.memset(ident[:, :], 0.0))
            for q in range(2):
                for r in range(2):
                    pool.memset(bbd[q][r], 0.0).then_inc(s["const_set"], 1)
                    pool.memset(cbd[q][r], 0.0).then_inc(s["const_set"], 1)
            step.settle()
            pool.affine_select(out=ident[:, :], in_=ident[:, :], compare_op=ALU.not_equal, fill=1.0, base=0,
                               pattern=[[-1, P]], channel_multiplier=1).then_inc(s["const_set"], 1)

            pool.iota(iota16[:, :].bitcast(U32), pattern=[[1, TOPK]], base=0, channel_multiplier=0).then_inc(s["tri_set"], 1)
            pool.memset(zrow[:, :], 0.0).then_inc(s["tri_set"], 1)
            pool.memset(nones[:, :], -1.0).then_inc(s["tri_set"], 1)
            pool.memset(ntri[:, :], -1.0).then_inc(s["tri_set"], 1)
            pool.memset(hide[:, :], 0.0).then_inc(s["tri_set"], 1)
            pool.memset(seen[:, :], 1.0).then_inc(s["tri_set"], 1)
            pool.wait_ge(s["tri_set"], 6)
            pool.affine_select(out=ntri[:, :], in_=ntri[:, :], compare_op=ALU.is_ge, fill=0.0, base=0,
                               pattern=[[-1, P]], channel_multiplier=1).then_inc(s["tri_set"], 1)
            pool.affine_select(out=seen[:, :], in_=seen[:, :], compare_op=ALU.is_gt, fill=0.0, base=0,
                               pattern=[[1, P]], channel_multiplier=-1).then_inc(s["tri_set"], 1)
            pool.affine_select(out=hide[:, :], in_=hide[:, :], compare_op=ALU.is_gt, fill=MASKED, base=0,
                               pattern=[[1, P]], channel_multiplier=-1).then_inc(s["tri_set"], 1)

            def tables(b, q, turn):
                if not first(turn):
                    pool.wait_ge(s["prods_set"], (b - 1) * CHB)
                if not first(b):
                    pool.wait_ge(s["tables_set"], 2 * b)
                c, sn = (tab[q][r].rearrange("p (j t) -> p j t", j=CHB) for r in range(2))
                tm = [ptmp[r].rearrange("p (j t) -> p j t", j=CHB) for r in range(2)]
                for lv in range(LEVELS):
                    n = 1 << lv
                    wcb = wc[:, bass.ds(lv * PAIRS + b * CHB, CHB)].unsqueeze(2).to_broadcast([P, CHB, n])
                    wsb = ws[:, bass.ds(lv * PAIRS + b * CHB, CHB)].unsqueeze(2).to_broadcast([P, CHB, n])
                    step.settle()
                    step.did(pool.tensor_tensor(c[:, :, n:2 * n], c[:, :, 0:n], wcb, ALU.mult))
                    step.did(pool.tensor_tensor(tm[0][:, :, 0:n], sn[:, :, 0:n], wsb, ALU.mult))
                    step.did(pool.tensor_tensor(sn[:, :, n:2 * n], sn[:, :, 0:n], wcb, ALU.mult))
                    step.did(pool.tensor_tensor(tm[1][:, :, 0:n], c[:, :, 0:n], wsb, ALU.mult))
                    step.settle()
                    i0 = pool.tensor_tensor(c[:, :, n:2 * n], c[:, :, n:2 * n], tm[0][:, :, 0:n], ALU.subtract)
                    i1 = pool.tensor_tensor(sn[:, :, n:2 * n], sn[:, :, n:2 * n], tm[1][:, :, 0:n], ALU.add)
                    if lv < LEVELS - 1:
                        step.did(i0)
                        step.did(i1)
                    else:
                        i0.then_inc(s["tables_set"], 1)
                        i1.then_inc(s["tables_set"], 1)

            for q in range(2):
                for r in range(2):
                    step.did(pool.memset(tab[q][r].rearrange("p (j t) -> p j t", j=CHB)[:, :, 0:1], 1.0 - r))
            pool.wait_ge(s["trig_set"], 1)
            tables(0, 0, 0)
            tables(1, 1, 0)
            with step.loop(KC // 2 - 1, 2 * (6 * LEVELS - 2)) as it:
                tables(2 * it + 2, 0, it + 1)
                tables(2 * it + 3, 1, it + 1)

            def gather(l, tb):
                done = (l * TB + tb) * SLOTS
                pool.wait_ge(s["idx_set"], ROUTED[l, tb // HB])
                with step.loop(SLOTS // TURN, 2) as j:
                    for half in range(2):
                        mine = stage_idx[:, half * RING:(half + 1) * RING]
                        step.did(pool.tensor_copy(mine, idx[:, bass.ds(j * TURN + (tb * SLOTS + half * RING), RING)]))
                        reg_wait(pool, s["pool_step"], step.base + step.n)
                        for g in range(2):
                            n = done + half * RING + 4 * g + 4
                            reg_wait(pool, s["u_used"], j * TURN + n)
                            for r in range(4 * g, 4 * g + 4):
                                pool.indirect_dma_start(u_ring[r], None, a["peer_u"][:, :],
                                                        bass.IndirectOffsetOnAxis(mine[:, r:r + 1], 0)).then_inc(u_in[r], 16)
                            reg_wait(pool, s["v_used"], j * TURN + n)
                            for r in range(4 * g, 4 * g + 4):
                                pool.indirect_dma_start(v_ring[r], None, a["peer_v"][:, :],
                                                        bass.IndirectOffsetOnAxis(mine[:, r:r + 1], 0)).then_inc(v_in[r], 16)

            for l in range(DEPTH):
                for tb in range(TB):
                    gather(l, tb)

        @block.sync
        def _(sp):
            sp.dma_start(xT.rearrange("p (k t) -> p k t", k=KC),
                         a["xT"].rearrange("(k p) t -> p k t", p=P)).then_inc(s["xT_in"], 16)
            for n, key in (("lr", "lam_re"), ("li", "lam_im")):
                sp.dma_start(par[n], a[key]).then_inc(s["par_in"], 16)
            for g in range(2):
                sp.dma_start(par["dt"][64 * g:64 * g + 64, :],
                             a["log_dt"][g:g + 1, :].to_broadcast([64, PAIRS])).then_inc(s["par_in"], 16)
            sp.dma_start(dsk, a["d_skip"]).then_inc(s["par_in"], 16)

            def pre(b, q, turn):
                if not first(turn):
                    sp.wait_ge(s["pair_done"], (b - 1) * CHB)
                sp.dma_start(win[q].rearrange("p (k n) -> p k n", k=KC),
                             a["w_in"][:, bass.ds(b * P, P)].rearrange("(k p) n -> p k n", p=P)).then_inc(s[f"win_in{q}"], 16)
                for r, (bn, cn) in enumerate((("b_re", "c_re"), ("b_im", "c_im"))):
                    sp.dma_start(braw[q][r], a[bn][:, bass.ds(b * CHB * GROUP, CHB * GROUP)]).then_inc(s[f"win_in{q}"], 16)
                    for g in range(2):
                        sp.dma_start(cbd[q][r][64 * g:64 * g + 64, :].rearrange("p (j c) -> p j c", j=CHB)[:, :, GROUP * g:GROUP * g + GROUP],
                                     a[cn][64 * g:64 * g + 64, bass.ds(b * CHB * GROUP, CHB * GROUP)].rearrange(
                                         "p (j c) -> p j c", j=CHB)).then_inc(s[f"win_in{q}"], 16)

            sp.wait_ge(s["const_set"], 9)
            pre(0, 0, 0)
            pre(1, 1, 0)
            sp.dma_start(h[:, :].rearrange("p (b d) -> p b d", b=TB),
                         a["x"].rearrange("(b p) d -> p b d", p=P)).then_inc(s["h_in"], 16)
            for n in range(2):
                sp.dma_start(lnp[:, n * D:(n + 1) * D], a[("ln_mix_g", "ln_mix_b")[n]][0:1, :].to_broadcast([P, D])).then_inc(s["ln_in"], 16)

            def load_piece(n):
                if n >= WSLOTS:
                    sp.wait_ge(s["lin_full"], FREE_AT[n - WSLOTS])
                slot = n % WSLOTS
                sp.dma_start(wring[:, slot * KC * HALF:(slot + 1) * KC * HALF].rearrange("p (k n) -> p k n", k=KC),
                             w_plan[n]).then_inc(s[f"w_in{slot}"], 16)

            def load_ln(n):
                name, l = LN_LOADS[n]
                sp.wait_ge(s["lnp_free"], n)
                for m, x in enumerate("gb"):
                    sp.dma_start(lnp[:, m * D:(m + 1) * D],
                                 a[f"{name}_{x}"][l:l + 1, :].to_broadcast([P, D])).then_inc(s["ln_in"], 16)

            def load_keys(l):
                if l > 0:
                    sp.wait_ge(s["scores_full"], 2 * l * PH)
                for m, x in enumerate(("k1T", "k2T")):
                    sp.dma_start(k12s[:, m * NKEYS:(m + 1) * NKEYS], a[x][l * P:(l + 1) * P, :]).then_inc(s["k_in"], 16)

            def load_embedding(l, hf):
                if (l, hf) == (1, 1):
                    sp.wait_ge(s["h_set"], H["ple", 1, HB - 1])
                else:
                    sp.wait_ge(s["idx_set"], 2 * l + hf + 2)
                sp.dma_start(plw.rearrange("p (k n) -> p k n", k=2),
                             a["ple_w"][l * PLE:(l + 1) * PLE, :].rearrange("(k p) n -> p k n", p=P)).then_inc(s["ple_in"], 16)
                sp.dma_start(pTs.rearrange("p (k n) -> p k n", k=2),
                             a["pT"][l].rearrange("(k p) n -> p k n", p=P)[:, :, hf * TH:(hf + 1) * TH]).then_inc(s["ple_in"], 16)

            for n in range(WSLOTS):
                load_piece(n)
            load_keys(0)
            with sp.Fori(0, KC // 2 - 1) as it:
                pre(2 * it + 2, 0, it + 1)
                pre(2 * it + 3, 1, it + 1)
            also = {W["pq", 0, 0][1]: [(load_ln, 1)]}
            for hf in range(2):
                also[W["pg", 0, hf][1]] = [(load_embedding, 0, hf), (load_ln, 2 + 3 * hf)]
                also[W["v", hf][1]] = [(load_ln, 3 + 3 * hf)]
                also[W["pq", 1, hf][1]] = [(load_keys, 1)] * (1 - hf) + [(load_ln, 4 + 3 * hf)]
                also[W["pg", 1, hf][1]] = [(load_embedding, 1, hf)]
            for n in range(WSLOTS, len(w_plan)):
                load_piece(n)
                for load, *args in also.get(n, ()):
                    load(*args)


def kernel(**inputs):
    import numpy as _np
    import concourse.bacc as _bacc
    from concourse import mybir as _mybir
    from concourse.bass_utils import run_bass_kernel_spmd as _run

    v = {k: _np.asarray(x) for k, x in inputs.items()}

    def by_state(x):
        x = x.reshape((PAIRS, 2, 64) + x.shape[2:])
        x = _np.moveaxis(x, 0, 2)
        return x.reshape(P, -1)

    arrays = {
        "x": v["x"][0], "xT": v["x"][0].T, "pT": v["p"][:, 0].transpose(0, 2, 1),
        "lam_re": by_state(v["ssm_lam_re"][0]), "lam_im": by_state(v["ssm_lam_im"][0]),
        "log_dt": v["ssm_log_dt"][0].reshape(PAIRS, 2).T,
        "b_re": by_state(v["ssm_b_re"][0]), "b_im": by_state(v["ssm_b_im"][0]),
        "c_re": by_state(v["ssm_c_re"][0].transpose(0, 2, 1)), "c_im": by_state(v["ssm_c_im"][0].transpose(0, 2, 1)),
        "d_skip": v["ssm_d"][0].reshape(KC, P).T, "w_in": v["ssm_w_in"][0], "w_glu": v["ssm_w_glu"][0],
        "ln_mix_g": v["ln_mix_g"], "ln_mix_b": v["ln_mix_b"], "ln_ffn_g": v["ln_ffn_g"], "ln_ffn_b": v["ln_ffn_b"],
        "kv_g": v["kv_ln_g"][None], "kv_b": v["kv_ln_b"][None],
        "w_kv": v["w_kv"], "w_q": v["sb_w_q"][0], "w_o": v["sb_w_o"][0],
        "peer_w_q": v["peer_w_q"].reshape(DEPTH * D, PH * 256),
        "k1T": v["peer_k1"].transpose(0, 2, 1).reshape(DEPTH * P, NKEYS),
        "k2T": v["peer_k2"].transpose(0, 2, 1).reshape(DEPTH * P, NKEYS),
        "peer_u": v["peer_u"].reshape(DEPTH * EXPERTS, D), "peer_v": v["peer_v"].reshape(DEPTH * EXPERTS, D),
        "ple_w": v["ple_w"].reshape(DEPTH * PLE, D), "ple_gate": v["ple_gate"].reshape(DEPTH * D, D),
    }
    nc = _bacc.Bacc("TRN2", target_bir_lowering=False, num_devices=1)
    feeds, aps = {}, {}
    for name, x in arrays.items():
        x = _np.ascontiguousarray(x)
        feeds[f"in_{name}"] = x
        aps[name] = nc.dram_tensor(f"in_{name}", x.shape, _mybir.dt.from_np(x.dtype), kind="ExternalInput").ap()
    out = nc.dram_tensor("out", (T, D), _mybir.dt.float32, kind="ExternalOutput").ap()
    build(nc, aps, out)
    r = _run(nc, [feeds], core_ids=[0])
    return r.results[0]["out"].reshape(1, T, D)
```

```python
import math
from contextlib import ExitStack, contextmanager

import numpy as np
import concourse.bass as bass
from concourse import mybir

ALU = mybir.AluOpType
ACT = mybir.ActivationFunctionType
AX_X = mybir.AxisListType.X
F32 = mybir.dt.float32
U32 = mybir.dt.uint32

P = 128
D = 1024
T = 512
DEPTH = 2
KC = D // P
TB = T // P
HALF = 512
CHB = 4
GROUP = 16
PAIRS = D // (2 * GROUP)
SEG = 256
LEVELS = 8
HEADS = 16
HD = D // HEADS
PH = 8
NKEYS = 128
EXPERTS = NKEYS * NKEYS
TOPK = 16
SLOTS = PH * TOPK
RING = 8
TURN = 2 * RING
PLE = 256
ALPHA = (2 * DEPTH) ** 0.25
LN_EPS = 1e-5
LOWEST = -3.0e38
MASKED = -1.0e30
ARENA = 36900
WSLOTS = 2
ROUND = 1.5 * 2.0 ** 23
TWO_PI_HI = 6.28125
TWO_PI_LO = 2 * math.pi - TWO_PI_HI
PI_BELOW = 3.1415925
HB = TB // 2
TH = T // 2
GROUPS = SLOTS // 4


class Steps:

    def __init__(self, eng, sem):
        self.eng, self.sem, self.base, self.n = eng, sem, 0, 0

    def did(self, ins):
        ins.then_inc(self.sem, 1)
        self.n += 1

    def settle(self, behind=0):
        self.eng.wait_ge(self.sem, self.base + self.n - behind)

    @contextmanager
    def loop(self, trips, per_trip):
        with self.eng.Fori(0, trips) as i:
            start = self.base + self.n
            self.base, self.n = i * per_trip + start, 0
            yield i
            assert self.n == per_trip, (self.n, per_trip)
        self.base, self.n = start + trips * per_trip, 0


def first(n):
    return isinstance(n, int) and n == 0


def build(nc, a, out):
    ctx = ExitStack()
    with ctx:
        def sb(name, cols, dt=F32):
            return ctx.enter_context(nc.sbuf_tensor(name, [P, cols], dt))

        def sem(name):
            return ctx.enter_context(nc.semaphore(name))

        ps = ctx.enter_context(nc.psum_tensor("ps", [P, 8, HALF], F32))

        def bank(n):
            return ps[:, n, :]

        h = sb("h", TB * D)
        wring = sb("wring", WSLOTS * KC * HALF)
        ident = sb("ident", P)
        lnp = sb("lnp", 2 * D)
        stat = sb("stat", TB * 12)
        mv = sb("mv", TB * 2)
        rstd = sb("rstd", TB)
        zrow = sb("zrow", HALF)
        iota16 = sb("iota16", TOPK)
        ntri = sb("ntri", P)
        nones = sb("nones", P)
        seen = sb("seen", P)
        hide = sb("hide", P)
        k12s = sb("k12", 2 * NKEYS)
        arena = sb("arena", ARENA)
        here = [0]

        def reg_wait(eng, semaphore, value):
            value = eng.to_reg(value)
            eng.wait_ge(s["const_set"], 9)
            eng.wait_ge(semaphore, value)

        def place(cols, at=None):
            if at is not None:
                here[0] = at
            v = arena[:, here[0]:here[0] + cols]
            here[0] += cols
            assert here[0] <= ARENA, here[0]
            return v

        def hb(tb, n0=None):
            return h[:, tb * D:(tb + 1) * D] if n0 is None else h[:, tb * D + n0 * HALF:tb * D + (n0 + 1) * HALF]

        def w_at(slot, k, c0=0, c1=HALF):
            o = (slot * KC + k) * HALF
            return wring[:, o + c0:o + c1]

        yT = place(KC * T, 0)
        tab = [[place(CHB * SEG) for _ in range(2)] for _ in range(2)]
        ptmp = [place(CHB * SEG // 2) for _ in range(2)]
        rot = [place(T) for _ in range(4)]
        vin = [[place(T) for _ in range(2)] for _ in range(2)]
        sc_r = [place(T) for _ in range(2)]
        prod = [[place(T) for _ in range(4)] for _ in range(2)]
        ub = [place(T) for _ in range(2)]
        win = [place(D) for _ in range(2)]
        braw = [[place(CHB * GROUP) for _ in range(2)] for _ in range(2)]
        bmul = [place(CHB * GROUP) for _ in range(4)]
        bbd = [[place(P) for _ in range(4)] for _ in range(2)]
        bT = [[place(P) for _ in range(4)] for _ in range(2)]
        cbd = [[place(P) for _ in range(4)] for _ in range(2)]
        btmp = [place(P) for _ in range(4)]
        ctmp = [place(P) for _ in range(4)]
        dgD = [place(P) for _ in range(2)]
        dsk = place(KC)
        par = {n: place(PAIRS) for n in ("lr", "li", "dt", "t0", "t1", "t2", "rho", "th", "c", "s", "fr", "fi")}
        wc = place((LEVELS + 1) * PAIRS)
        ws = place((LEVELS + 1) * PAIRS)
        xT = place(KC * T)

        u_ring = [place(D, 0 if r == 0 else None) for r in range(RING)]
        v_ring = [place(D) for _ in range(RING)]
        diag = [place(P) for _ in range(RING)]
        stage_idx = place(TURN).bitcast(U32)
        actv = place(TURN)
        gelu = place(TURN)
        gg = place(TURN)
        idx = place(TB * SLOTS).bitcast(U32)
        gates = place(TB * SLOTS)
        KV_AT = here[0]
        KT = place(KC * T)
        V = place(TB * D)
        sgm = [arena[:, here[0] + HALF * q:here[0] + HALF * (q + 1)] for q in range(2)]
        QT = place(KC * TH)
        hTh = place(KC * TH)
        glu_w = [[arena[:, o + g * KC * HALF:o + (g + 1) * KC * HALF] for g in range(2)] for o in (RING * D, KV_AT)]
        dyn = here[0]
        q_sb = [place(TH, dyn if n == 0 else None) for n in range(4)]
        val = [place(HB * TOPK) for _ in range(2)]
        key = [place(HB * SLOTS) for _ in range(2)]
        best = place(HB * SLOTS)
        bpos = place(HB * SLOTS)
        ksel = [place(HB * SLOTS) for _ in range(2)]
        esel = [place(SLOTS) for _ in range(2)]
        rsum = place(HB * PH)
        rinv = place(HB * PH)
        eq_at = here[0]
        rest = [place(NKEYS) for _ in range(2 * HB)]
        cand = [place(TOPK * TOPK) for _ in range(HB)]
        cand2 = [place(TOPK * TOPK) for _ in range(HB)]
        eq = place(SLOTS * TOPK, eq_at)
        plw = place(2 * D, dyn)
        pTs = place(2 * TH)
        sgp = [place(HALF) for _ in range(2)]
        hk = place(HB * D, dyn)
        hkT = place(KC * TH)
        ZW = [384, 896]
        ez = [place(ZW[1], dyn if e == 0 else None) for e in range(2)]
        sp_ = [place(ZW[1]) for _ in range(2)]

        def first_q(hf, kb):
            return max(kb - HB * hf, 0) * P

        def strip_at(hf, kb):
            return kb * TH if hf == 0 or kb < 3 else 3 * TH

        def hk_blocks(hf):
            return range(HB * (hf + 1))

        s = {n: sem(n) for n in (
            "const_set", "dve_step", "pool_step", "act_step", "xT_in", "h_in", "par_in", "win_in0", "win_in1", "bc_in0", "bc_in1",
            "u_full", "u_copied", "bbar_set", "bt_full", "bt_copied", "tables_set", "bu_full", "bu_read",
            "prods_set", "c_negated", "c_turned", "pair_done", "y_taken", "sin_done", "trig_set", "w_in0", "w_in1", "lin_full", "lin_free",
            "gate_sig", "glu_w_in0", "glu_w_in1", "side_full", "side_sig", "side_free", "ln_in", "lnp_free", "var_set", "std_set", "h_set", "out_done", "tri_set", "k_in", "ple_in",
            "scores_full", "scores_read", "gap_set", "gap_exp", "idx_set", "routed", "u_used", "v_used", "diag_set",
            "ffn_full", "ffn_read", "z_full", "z_exp", "soft_set", "sum_full", "weights_set", "o_full", "o_copied")}
        u_in = [sem(f"u_in{r}") for r in range(RING)]
        v_in = [sem(f"v_in{r}") for r in range(RING)]

        block = ctx.enter_context(nc.Block())
        w_plan = []

        def piece(ap, c0):
            w_plan.append(ap[:, c0:c0 + HALF].rearrange("(k p) n -> p k n", p=P))
            return len(w_plan) - 1

        def pieces(ap, n, c0=0):
            return [piece(ap, c0 + m * HALF) for m in range(n)]

        W = {"glu": [piece(a["w_glu"], g * D) for g in range(2)]}
        for hf in range(2):
            W["pq", 0, hf] = pieces(a["peer_w_q"][0:D, :], 4)
        for hf in range(2):
            W["pg", 0, hf] = pieces(a["ple_gate"][0:D, :], 2)
            W["k", hf] = pieces(a["w_kv"], 2)
            W["v", hf] = pieces(a["w_kv"], 2, D)
            W["q", hf] = pieces(a["w_q"], 2)
            W["o", hf] = pieces(a["w_o"], 2)
            W["pq", 1, hf] = pieces(a["peer_w_q"][D:2 * D, :], 4)
        for hf in range(2):
            W["pg", 1, hf] = pieces(a["ple_gate"][D:2 * D, :], 2)

        H = {}
        for tb in range(TB):
            H["mix", 0, tb] = len(H) + 1
        for hf in range(2):
            for what in (("ffn", 0), ("ple", 0), ("kv", 1), ("mix", 1)):
                for tb in range(HB * hf, HB * hf + HB):
                    H[what + (tb,)] = len(H) + 1
        for tbs in (range(HB), [HB], [HB + 1]):
            for what in (("ffn", 1), ("ple", 1)):
                for tb in tbs:
                    H[what + (tb,)] = len(H) + 1
        LN_LOADS = [("ln_mix", 0)] + 2 * [("ln_ffn", 0), ("kv", 0), ("ln_mix", 1)] + [("ln_ffn", 1)]
        TILE = {}
        FREE_AT = {}

        NORM, TURN_OVER, PRODUCTS = HB, HB, 2 * HB
        ATTENTION = 3 * HEADS // 2 + 1
        STEPS_ROUTE = 2 * (PH + 1) + 2 * HB + 2
        STEPS_PLE = NORM + TURN_OVER + PRODUCTS
        STEPS_PLE_BLOCK = 1 + 1 + 2
        STEPS_FIRST = [TURN_OVER + STEPS_ROUTE, NORM + TURN_OVER + STEPS_ROUTE]
        STEPS_BETWEEN = STEPS_PLE + NORM + 2 * TURN_OVER + 3 * PRODUCTS + ATTENTION + PRODUCTS + NORM + TURN_OVER + STEPS_ROUTE

        def weave(l, tbs, group, steps, filler, lag, block_start=None, block_end=None):
            done, total = 0, len(tbs) * GROUPS
            for n in range(total):
                tb, g = tbs[n // GROUPS], n % GROUPS
                if g == 0 and block_start:
                    block_start(l, tb)
                group(l, tb, (l * TB + tb) * SLOTS + 4 * g, g)
                if g == GROUPS - 1 and block_end:
                    block_end(l, tb)
                while done < min(steps, -(-steps * (n + 1 - lag) // total)):
                    next(filler)
                    done += 1
            while done < steps:
                next(filler)
                done += 1

        def alone(steps, filler, beside=None):
            for n in range(steps):
                next(filler)
                if beside:
                    beside(n)

        SIDE = [(n0, HB + tb) for n0 in range(2) for tb in range(HB)]
        SIDE_STEPS = {HB + 2 * ((1, 4, 8)[p - 1] + g) + 1: (p, g) for p in range(1, len(SIDE)) for g in range(2)}

        @block.tensor
        def _(pe):
            pe.wait_ge(s["xT_in"], 16)
            pe.wait_ge(s["const_set"], 9)

            def feed(b, q, turn, k0, k1):
                if k0 == 0:
                    pe.wait_ge(s[f"win_in{q}"], turn * 16 + 16)
                    if not first(turn):
                        pe.wait_ge(s["bt_copied"], 4 * (b - 1))
                for k in range(k0, k1):
                    i = pe.matmul(bank(6 + q), win[q][:, k * P:(k + 1) * P], xT[:, k * T:(k + 1) * T], start=(k == 0), stop=(k == KC - 1))
                if k1 == KC:
                    i.then_inc(s["u_full"], 1)

            def turn_b(b, q):
                pe.wait_ge(s["u_copied"], b + 1)
                pe.wait_ge(s["bbar_set"], b * 7 + 7)
                for r in range(4):
                    i = pe.transpose(ps[:, 6 + q, r * P:(r + 1) * P], bbd[q][r], ident[:, :])
                i.then_inc(s["bt_full"], 1)

            def bu_of(b, q, j, pair):
                rows = slice(32 * j, 32 * j + 32)
                if j == 0:
                    pe.wait_ge(s["bt_copied"], 4 * b + 4)
                if not (isinstance(pair, int) and pair < 2):
                    pe.wait_ge(s["bu_read"], pair - 1)
                for r in range(2):
                    for g in range(2):
                        i = pe.matmul(ps[:, 2 * (j % 2) + r, g * SEG:(g + 1) * SEG], bT[q][2 * g + r][rows, :],
                                      ub[q][rows, g * SEG:(g + 1) * SEG], start=True, stop=True)
                i.then_inc(s["bu_full"], 1)

            def y_of(b, q, j):
                rows = slice(32 * j, 32 * j + 32)
                if j == 0:
                    if not first(b):
                        pe.wait_ge(s["y_taken"], b)
                    pe.matmul(bank(4 + q), dgD[q], ub[q], start=True, stop=False, skip_group_check=True)
                    pe.wait_ge(s["c_turned"], b * 2 + 2)
                pe.wait_ge(s["prods_set"], b * CHB + (j + 1))
                for k in range(4):
                    for g in range(2):
                        i = pe.matmul(ps[rows, 4 + q, g * SEG:(g + 1) * SEG], cbd[q][2 * g + k // 2][:, 32 * j:32 * j + 32],
                                      prod[j % 2][k][:, g * SEG:(g + 1) * SEG], start=False, stop=(k == 3), skip_group_check=True)
                i.then_inc(s["pair_done"], 1)

            def main(b, q, turn=None, last=False):
                for j in range(CHB):
                    if j < CHB - 2:
                        bu_of(b, q, j + 2, b * CHB + (j + 2))
                    elif not last:
                        bu_of(b + 1, 1 - q, j - 2, b * CHB + (j + 2))
                    if turn is not None and j < 2:
                        feed(b + 1, 1 - q, turn, j * KC // 2, (j + 1) * KC // 2)
                        if j == 1:
                            turn_b(b + 1, 1 - q)
                    y_of(b, q, j)

            for b in range(2):
                feed(b, b, 0, 0, KC)
                turn_b(b, b)
            for j in range(2):
                bu_of(0, 0, j, j)
            main(0, 0)
            with pe.Fori(0, KC // 2 - 1) as it:
                main(2 * it + 1, 1, it + 1)
                main(2 * it + 2, 0, it + 1)
            main(KC - 1, 1, last=True)

            def tile(key):
                t = TILE[key] = len(TILE)
                if t >= 4:
                    pe.wait_ge(s["lin_free"], t - 3)
                return bank(t % 4)

            def linear(key, mats, cols=HALF):
                o = tile(key)[:, 0:cols]
                for k, (lhs, rhs) in enumerate(mats):
                    i = pe.matmul(o, lhs, rhs, start=(k == 0), stop=(k == len(mats) - 1))
                i.then_inc(s["lin_full"], 1)

            def rows(key, src, width, at, n):
                linear(key, [(src[:, k * width + at:k * width + at + P], w_at(n % WSLOTS, k)) for k in range(KC)])

            def columns(key, src, m, n):
                linear(key, [(w_at(n % WSLOTS, k, m * P, (m + 1) * P), src[:, k * TH:(k + 1) * TH]) for k in range(KC)], TH)

            def have(n):
                pe.wait_ge(s[f"w_in{n % WSLOTS}"], 16 * (n // WSLOTS + 1))

            def used(n):
                FREE_AT[n] = len(TILE)

            def copied():
                pe.wait_ge(s["lin_free"], len(TILE))

            def turn_over(what, hf, src, base, tbs=None):
                for tb in tbs or range(HB * hf, HB * hf + HB):
                    pe.wait_ge(s["h_set"], H[what + (tb,)])
                    for q in range(2):
                        b = tile(("turn", what, tb, q))
                        for k in range(4):
                            o = (tb - base) * D + (4 * q + k) * P
                            i = pe.transpose(b[:, k * P:(k + 1) * P], src[:, o:o + P], ident[:, :])
                        i.then_inc(s["lin_full"], 1)
                    yield

            def column_steps(what, hf, src):
                copied()
                for n0 in range(2):
                    n = W[what, hf][n0]
                    have(n)
                    for m in range(4):
                        columns((what, hf, n0, m), src, m, n)
                        if m == 3:
                            used(n)
                        if m % 2:
                            yield

            def row_steps(what, hf, src):
                copied()
                for n0 in range(2):
                    n = W[what, hf][n0]
                    have(n)
                    for tb in range(HB):
                        rows((what, hf, n0, tb), src, TH, tb * P, n)
                        if tb == HB - 1:
                            used(n)
                        yield

            def route(l, hf):
                copied()
                for hh in range(PH + 1):
                    if hh < PH:
                        n = W["pq", l, hf][hh // 2]
                        have(n)
                        columns(("pq", l, hf, hh, 0), hTh, 2 * (hh % 2), n)
                    yield
                    if hh < PH:
                        columns(("pq", l, hf, hh, 1), hTh, 2 * (hh % 2) + 1, n)
                        if hh % 2:
                            used(n)
                    if hh > 0:
                        g = hh - 1
                        seq = (2 * l + hf) * PH + g
                        pe.wait_ge(s["lin_free"], TILE["pq", l, hf, g, 1] + 1)
                        pe.wait_ge(s["k_in"], 32 * (l + 1))
                        if seq >= 2:
                            pe.wait_ge(s["scores_read"], seq - 1)
                        for sd in range(2):
                            for tb in range(HB):
                                c = (sd * HB + tb) * P
                                i = pe.matmul(ps[:, 4 + g % 2, c:c + P], q_sb[2 * (g % 2) + sd][:, tb * P:(tb + 1) * P],
                                              k12s[:, sd * NKEYS:(sd + 1) * NKEYS], start=True, stop=True)
                        i.then_inc(s["scores_full"], 1)
                    yield
                for _ in range(2 * HB + 2):
                    yield

            def ple(l, hf):
                for _ in range(HB):
                    yield
                yield from turn_over(("ffn", l), hf, h, 0)
                copied()
                pe.wait_ge(s["ple_in"], 32 * (2 * l + hf + 1))
                for n0 in range(2):
                    n = W["pg", l, hf][n0]
                    have(n)
                    for tb in range(HB):
                        rows(("pg", l, hf, n0, tb), hTh, TH, tb * P, n)
                        linear(("pw", l, hf, n0, tb), [(pTs[:, k * TH + tb * P:k * TH + (tb + 1) * P],
                                                        plw[:, k * D + n0 * HALF:k * D + (n0 + 1) * HALF]) for k in range(2)])
                        if tb == HB - 1:
                            used(n)
                        yield

            def ple_block(l, tb):
                yield
                yield from turn_over(("ffn", l), 1, h, 0, [tb])
                copied()
                pe.wait_ge(s["ple_in"], 32 * (2 * l + 2))
                for n0 in range(2):
                    n = W["pg", l, 1][n0]
                    have(n)
                    rows(("pg", l, 1, n0, tb), hTh, TH, (tb - HB) * P, n)
                    linear(("pw", l, 1, n0, tb), [(pTs[:, k * TH + (tb - HB) * P:k * TH + (tb - HB + 1) * P],
                                                   plw[:, k * D + n0 * HALF:k * D + (n0 + 1) * HALF]) for k in range(2)])
                    yield

            def strip(hf, hd, kb, c0=0, c1=None):
                w = TH - first_q(hf, kb)
                o = strip_at(hf, kb) + c0
                return ps[:, 2 * (hd % 2) + o // HALF, :][:, o % HALF:o % HALF + (w if c1 is None else c1) - c0]

            def scores(hf, hd):
                rw = slice(64 * (hd % 2), 64 * (hd % 2) + 64)
                c = hd // 2
                if hf * HEADS + hd >= 2:
                    pe.wait_ge(s["weights_set"], hf * HEADS + hd - 1)
                for kb in hk_blocks(hf):
                    i = pe.matmul(strip(hf, hd, kb), KT[rw, c * T + kb * P:c * T + (kb + 1) * P],
                                  QT[rw, c * TH + first_q(hf, kb):(c + 1) * TH], start=(kb % 2 == 0), stop=True,
                                  skip_group_check=True)
                i.then_inc(s["z_full"], 1)

            def log_weights(hf, hd):
                pe.wait_ge(s["soft_set"], 2 * (hf * HEADS + hd) + 2)
                x = sp_[hd % 2]
                for kb in hk_blocks(hf):
                    for jb in hk_blocks(hf):
                        if jb >= kb:
                            o = strip_at(hf, jb)
                            i = pe.matmul(strip(hf, hd, kb, first_q(hf, jb) - first_q(hf, kb)), ntri[:, :] if jb == kb else nones[:, :],
                                          x[:, o:o + TH - first_q(hf, jb)], start=False, stop=True, skip_group_check=True)
                    if kb >= HB * hf:
                        i = pe.matmul(strip(hf, hd, kb, 0, P), ident[:, :], hide[:, :], start=False, stop=True,
                                      skip_group_check=True)
                i.then_inc(s["sum_full"], 1)

            def values(hf, hd):
                rw = slice(64 * (hd % 2), 64 * (hd % 2) + 64)
                seq = hf * HEADS + hd
                pe.wait_ge(s["weights_set"], seq + 1)
                if seq >= 2:
                    pe.wait_ge(s["o_copied"], seq - 1)
                for kb in hk_blocks(hf):
                    o = strip_at(hf, kb)
                    i = pe.matmul(ps[rw, 4, first_q(hf, kb):TH], V[:, kb * D + hd * HD:kb * D + (hd + 1) * HD],
                                  ez[hd % 2][:, o:o + TH - first_q(hf, kb)], start=(kb == 0), stop=True, skip_group_check=True)
                i.then_inc(s["o_full"], 1)

            def attention(hf):
                copied()
                pe.wait_ge(s["scores_read"], (2 + hf) * PH)
                for hd in range(0, HEADS, 2):
                    for e in range(2):
                        if hd > 0:
                            values(hf, hd - 2 + e)
                    for e in range(2):
                        scores(hf, hd + e)
                    yield
                    yield
                    for e in range(2):
                        log_weights(hf, hd + e)
                    yield
                for e in range(2):
                    values(hf, HEADS - 2 + e)
                yield

            def between_layers(hf):
                yield from ple(0, hf)
                for _ in range(HB):
                    yield
                yield from turn_over(("kv", 1), hf, hk, HB * hf)
                yield from turn_over(("ple", 0), hf, h, 0)
                yield from column_steps("k", hf, hkT)
                yield from row_steps("v", hf, hkT)
                yield from column_steps("q", hf, hTh)
                yield from attention(hf)
                pe.wait_ge(s["o_copied"], (hf + 1) * HEADS)
                yield from row_steps("o", hf, QT)
                for _ in range(HB):
                    yield
                yield from turn_over(("mix", 1), hf, h, 0)
                yield from route(1, hf)

            def block_start(l, tb):
                if l * TB + tb > 0:
                    pe.wait_ge(s["ffn_read"], l * TB + tb)
                for n0 in range(2):
                    pe.matmul(bank(6 + n0), zrow[0:1, 0:P], zrow[0:1, :], start=True, stop=False, skip_group_check=True)

            def block_end(l, tb):
                for n0 in range(2):
                    i = pe.matmul(bank(6 + n0), zrow[0:1, 0:P], zrow[0:1, :], start=False, stop=True, skip_group_check=True)
                i.then_inc(s["ffn_full"], 1)

            def group(l, tb, n, g, j=0):
                pe.wait_ge(s["diag_set"], n + (TURN + 4) + j * TURN)
                for r in range(4):
                    q = (4 * g + r) % RING
                    pe.wait_ge(v_in[q], 16 * ((n + r) // RING + 1) + j * 16 * (TURN // RING))
                    for n0 in range(2):
                        i = pe.matmul(bank(6 + n0), diag[q], v_ring[q][:, n0 * HALF:(n0 + 1) * HALF],
                                      start=False, stop=False, skip_group_check=True)
                    i.then_inc(s["v_used"], 1)

            def block_loop(l, tb):
                n = (l * TB + tb) * SLOTS
                block_start(l, tb)
                for g in range(4):
                    group(l, tb, n + 4 * g, g)
                with pe.Fori(1, SLOTS // TURN) as j:
                    for g in range(4):
                        group(l, tb, n + 4 * g, g, j)
                block_end(l, tb)

            pe.wait_ge(s["y_taken"], KC + 1)
            pe.wait_ge(s["bu_read"], PAIRS)
            for n0 in range(2):
                if n0 == 0:
                    for g in range(2):
                        have(W["glu"][g])
                else:
                    pe.wait_ge(s["glu_w_in1"], 32)
                for tb in range(HB):
                    for g in range(2):
                        o = [yT[:, k * T + tb * P:k * T + (tb + 1) * P] for k in range(KC)]
                        linear(("glu", n0, tb, g), [(o[k], w_at(g, k) if n0 == 0 else glu_w[1][g][:, k * HALF:(k + 1) * HALF])
                                                    for k in range(KC)])
                if n0 == 0:
                    for g in range(2):
                        used(W["glu"][g])

            def side_glu(p, g):
                n0, tb = SIDE[p]
                if p > 0:
                    pe.wait_ge(s["side_free"], p)
                for k in range(KC):
                    i = pe.matmul(bank(6 + g), yT[:, k * T + tb * P:k * T + (tb + 1) * P],
                                  glu_w[n0][g][:, k * HALF:(k + 1) * HALF], start=(k == 0), stop=(k == KC - 1))
                i.then_inc(s["side_full"], 1)

            def beside_route(n):
                if n in SIDE_STEPS:
                    side_glu(*SIDE_STEPS[n])

            pe.wait_ge(s["glu_w_in0"], 32)
            for g in range(2):
                side_glu(0, g)

            def first_route(hf):
                if hf == 1:
                    for _ in range(HB):
                        yield
                yield from turn_over(("mix", 0), hf, h, 0)
                yield from route(0, hf)

            alone(STEPS_FIRST[0], first_route(0), beside_route)
            pe.wait_ge(s["side_free"], len(SIDE))
            pe.sem_inc(s["v_used"], RING)
            weave(0, [0], group, STEPS_FIRST[1], first_route(1), 0, block_start, block_end)
            block_loop(0, 1)
            weave(0, [2, 3], group, STEPS_BETWEEN, between_layers(0), 0, block_start, block_end)
            weave(1, [0, 1], group, STEPS_BETWEEN, between_layers(1), 0, block_start, block_end)
            weave(1, [2], group, STEPS_PLE, ple(1, 0), 0, block_start, block_end)
            weave(1, [HB + 1], group, STEPS_PLE_BLOCK, ple_block(1, HB), 0, block_start, block_end)
            alone(STEPS_PLE_BLOCK, ple_block(1, HB + 1))

        @block.scalar
        def _(act):
            step = Steps(act, s["act_step"])
            act.wait_ge(s["par_in"], 80)
            act.sem_inc(s["y_taken"], 1)
            act.activation(par["dt"], par["dt"], ACT.Exp).then_inc(s["sin_done"], 1)
            act.wait_ge(s["dve_step"], 1)
            act.activation(par["rho"], par["t0"], ACT.Exp).then_inc(s["sin_done"], 1)
            act.wait_ge(s["dve_step"], 7)
            act.activation(par["s"], par["th"], ACT.Sin).then_inc(s["sin_done"], 1)
            act.activation(par["t1"], par["th"], ACT.Sin, scale=0.5).then_inc(s["sin_done"], 1)

            def pre(b, q, turn):
                act.wait_ge(s["u_full"], b + 1)
                if not first(turn):
                    act.wait_ge(s["pair_done"], (b - 1) * CHB)
                act.copy(ub[q], bank(6 + q)).then_inc(s["u_copied"], 1)
                act.wait_ge(s["bt_full"], b + 1)
                for r in range(4):
                    act.copy(bT[q][r], ps[:, 6 + q, r * P:(r + 1) * P]).then_inc(s["bt_copied"], 1)

            def main(b, q):
                act.wait_ge(s["pair_done"], b * CHB + CHB)
                act.activation(yT[:, bass.ds(b * T, T)], bank(4 + q), ACT.Gelu_apprx_tanh).then_inc(s["y_taken"], 1)

            pre(0, 0, 0)
            pre(1, 1, 0)
            with act.Fori(0, KC // 2 - 1) as it:
                main(2 * it, 0)
                pre(2 * it + 2, 0, it + 1)
                main(2 * it + 1, 1)
                pre(2 * it + 3, 1, it + 1)
            main(KC - 2, 0)
            main(KC - 1, 1)

            def store(tb):
                act.wait_ge(s["h_set"], H["ple", 1, tb])
                act.dma_start(out[tb * P:(tb + 1) * P, :], hb(tb)).then_inc(s["out_done"], 16)

            def gate(key, dst, n):
                t = TILE[key]
                act.wait_ge(s["lin_full"], t + 2)
                if n >= 2:
                    act.wait_ge(s["lin_free"], t - 2)
                act.activation(dst, bank(t % 4), ACT.Sigmoid).then_inc(s["gate_sig"], 1)

            lns = [0]

            def root(tbs):
                lns[0] += 1
                act.wait_ge(s["var_set"], lns[0])
                act.activation(rstd[:, tbs], rstd[:, tbs], ACT.Sqrt).then_inc(s["std_set"], 1)

            def evacuate(key, dst, cols=HALF, scale=None, tiles=False):
                t = TILE[key]
                act.wait_ge(s["lin_full"], t + 1)
                src = bank(t % 4)[:, 0:cols]
                if tiles:
                    src = src.rearrange("p (k t) -> p k t", k=4)
                if scale is None:
                    act.copy(dst, src).then_inc(s["lin_free"], 1)
                else:
                    act.mul(dst, src, scale).then_inc(s["lin_free"], 1)

            def turn_over(what, hf, dst, tbs=None):
                for tb in tbs or range(HB * hf, HB * hf + HB):
                    for q in range(2):
                        o = (tb - HB * hf) * P
                        evacuate(("turn", what, tb, q),
                                 dst[:, q * 4 * TH:(q + 1) * 4 * TH].rearrange("p (k t) -> p k t", k=4)[:, :, o:o + P], tiles=True)
                    yield

            def norm_steps(hf):
                for tb in range(HB * hf, HB * hf + HB):
                    root(slice(tb, tb + 1))
                    yield

            def route(l, hf):
                for hh in range(PH + 1):
                    for sd in range(2):
                        if hh < PH:
                            evacuate(("pq", l, hf, hh, sd), q_sb[2 * (hh % 2) + sd], TH)
                        yield
                for n in range(2 * HB + 2):
                    if n == 1:
                        act.wait_ge(s["gap_set"], 2 * l + hf + 1)
                        g = gates[:, HB * hf * SLOTS:HB * (hf + 1) * SLOTS]
                        act.activation(g, g, ACT.Exp).then_inc(s["gap_exp"], 1)
                    yield

            def ple(l, hf):
                yield from norm_steps(hf)
                yield from turn_over(("ffn", l), hf, hTh)
                for n0 in range(2):
                    for tb in range(HB):
                        n = n0 * HB + tb
                        gate(("pg", l, hf, n0, tb), sgp[n % 2], n)
                        yield

            def ple_block(l, tb):
                root(slice(tb, tb + 1))
                yield
                yield from turn_over(("ffn", l), 1, hTh, [tb])
                for n0 in range(2):
                    gate(("pg", l, 1, n0, tb), sgp[n0], n0)
                    yield

            def column_steps(what, hf, place_of, scale=None):
                for n0 in range(2):
                    for m in range(4):
                        evacuate((what, hf, n0, m), place_of(4 * n0 + m), TH, scale)
                        if m % 2:
                            yield

            def strips(hf, hd):
                return ps[:, 2 * (hd % 2):2 * (hd % 2) + 2, :].rearrange("p b n -> p (b n)")[:, 0:ZW[hf]]

            def soft(hf, hd):
                x = ez[hd % 2][:, 0:ZW[hf]]
                seq = 3 * (hf * HEADS + hd)
                act.wait_ge(s["z_full"], hf * HEADS + hd + 1)
                act.activation(x, strips(hf, hd), ACT.Abs).then_inc(s["z_exp"], 1)
                act.wait_ge(s["z_exp"], seq + 1)
                act.activation(x, x, ACT.Exp, scale=-1.0).then_inc(s["z_exp"], 1)
                act.wait_ge(s["z_exp"], seq + 2)
                act.activation(x, x, ACT.Ln, bias=1.0).then_inc(s["z_exp"], 1)

            def outputs(hf, hd):
                rw = slice(64 * (hd % 2), 64 * (hd % 2) + 64)
                act.wait_ge(s["o_full"], hf * HEADS + hd + 1)
                act.copy(QT[rw, (hd // 2) * TH:(hd // 2 + 1) * TH], ps[rw, 4, 0:TH]).then_inc(s["o_copied"], 1)

            def attention(hf):
                for hd in range(0, HEADS, 2):
                    for e in range(2):
                        if hd > 0:
                            outputs(hf, hd - 2 + e)
                    for e in range(2):
                        soft(hf, hd + e)
                    yield
                    yield
                    for e in range(2):
                        act.wait_ge(s["sum_full"], hf * HEADS + hd + e + 1)
                        act.activation(ez[e][:, 0:ZW[hf]], strips(hf, hd + e), ACT.Exp).then_inc(s["weights_set"], 1)
                    yield
                for e in range(2):
                    outputs(hf, HEADS - 2 + e)
                yield

            def between_layers(hf):
                yield from ple(0, hf)
                yield from norm_steps(hf)
                yield from turn_over(("kv", 1), hf, hkT)
                yield from turn_over(("ple", 0), hf, hTh)
                yield from column_steps("k", hf, lambda c: KT[:, c * T + hf * TH:c * T + (hf + 1) * TH])
                for n0 in range(2):
                    for tb in range(HB):
                        o = (HB * hf + tb) * D + n0 * HALF
                        evacuate(("v", hf, n0, tb), V[:, o:o + HALF])
                        yield
                yield from column_steps("q", hf, lambda c: QT[:, c * TH:(c + 1) * TH], HD ** -0.5)
                yield from attention(hf)
                for _ in range(4):
                    yield
                yield from norm_steps(hf)
                yield from turn_over(("mix", 1), hf, hTh)
                yield from route(1, hf)

            def group(l, tb, n, g, j=None):
                loop = 0 if j is None else j * TURN
                c = (4 * g) % TURN
                act.wait_ge(s["u_used"], n + (RING + 4) + loop)
                step.did(act.activation(gelu[:, c:c + 4], actv[:, c:c + 4], ACT.Gelu_apprx_tanh))
                if j is None:
                    step.settle()
                else:
                    reg_wait(act, s["act_step"], step.base + step.n)
                for r in range(4):
                    o = tb * SLOTS + 4 * g + r
                    gt = gates[:, o:o + 1] if j is None else gates[:, bass.ds(j * TURN + o, 1)]
                    step.did(act.activation(gg[:, c + r:c + r + 1], gt, ACT.Copy, scale=gelu[:, c + r:c + r + 1]))
                step.settle()
                act.wait_ge(s["v_used"], n + 4 + loop)
                for r in range(4):
                    act.activation(diag[(4 * g + r) % RING], ident[:, :], ACT.Copy,
                                   scale=gg[:, c + r:c + r + 1]).then_inc(s["diag_set"], 1)

            def block_loop(l, tb):
                n = (l * TB + tb) * SLOTS
                for g in range(4):
                    group(l, tb, n + 4 * g, g)
                with step.loop(SLOTS // TURN - 1, 4 * 5) as i:
                    for g in range(4):
                        group(l, tb, n + 4 * g, g, i + 1)

            for n0 in range(2):
                for tb in range(HB):
                    n = n0 * HB + tb
                    t = TILE["glu", n0, tb, 1]
                    act.wait_ge(s["lin_full"], t + 1)
                    if n >= 2:
                        act.wait_ge(s["lin_free"], t - 3)
                    act.activation(sgm[n % 2], bank(t % 4), ACT.Sigmoid).then_inc(s["gate_sig"], 1)
            act.sem_inc(s["diag_set"], TURN)
            root(slice(0, HB))

            def side_gate(p):
                if p < 2:
                    act.wait_ge(s["lin_free"], TILE["glu", 1, HB - 1, 1] + 1)
                else:
                    act.wait_ge(s["side_free"], p - 1)
                act.wait_ge(s["side_full"], 2 * p + 2)
                act.activation(sgm[p % 2], bank(7), ACT.Sigmoid).then_inc(s["side_sig"], 1)

            def beside_route(n):
                if n in SIDE_STEPS and SIDE_STEPS[n][1] == 1:
                    side_gate(SIDE_STEPS[n][0])

            side_gate(0)

            def first_route(hf):
                if hf == 1:
                    yield from norm_steps(hf)
                yield from turn_over(("mix", 0), hf, hTh)
                yield from route(0, hf)

            alone(STEPS_FIRST[0], first_route(0), beside_route)
            weave(0, [0], group, STEPS_FIRST[1], first_route(1), 1)
            block_loop(0, 1)
            weave(0, [2, 3], group, STEPS_BETWEEN, between_layers(0), 1)
            weave(1, [0, 1], group, STEPS_BETWEEN, between_layers(1), 1)
            weave(1, [2], group, STEPS_PLE, ple(1, 0), 1)
            for tb in range(HB):
                store(tb)
            weave(1, [HB + 1], group, STEPS_PLE_BLOCK, ple_block(1, HB), 1)
            store(HB)
            alone(STEPS_PLE_BLOCK, ple_block(1, HB + 1))
            store(HB + 1)
            act.wait_ge(s["out_done"], 16 * TB)

        @block.vector
        def _(dve):
            step = Steps(dve, s["dve_step"])

            def tt(o_, x, y, op):
                step.did(dve.tensor_tensor(o_, x, y, op))

            def ts(o_, x, c1, c2, op0, op1=None):
                step.did(dve.tensor_scalar(o_, x, c1, c2, op0, op1) if op1 is not None else dve.tensor_scalar(o_, x, c1, None, op0))

            def stt(o_, x, c, y, op0, op1):
                step.did(dve.scalar_tensor_tensor(out=o_, in0=x, scalar=c, in1=y, op0=op0, op1=op1))

            lr, li, dt, t0, t1, t2, rho, th, c, sn, fr, fi = (par[n] for n in (
                "lr", "li", "dt", "t0", "t1", "t2", "rho", "th", "c", "s", "fr", "fi"))
            dve.wait_ge(s["sin_done"], 1)
            tt(t0, lr, dt, ALU.mult)
            tt(th, li, dt, ALU.mult)
            step.settle()
            ts(t2, th, 1.0 / (2 * math.pi), ROUND, ALU.mult, ALU.add)
            step.settle()
            ts(t2, t2, ROUND, None, ALU.subtract)
            step.settle()
            stt(th, t2, -TWO_PI_HI, th, ALU.mult, ALU.add)
            step.settle()
            stt(th, t2, -TWO_PI_LO, th, ALU.mult, ALU.add)
            step.settle()
            ts(th, th, PI_BELOW, -PI_BELOW, ALU.min, ALU.max)
            dve.wait_ge(s["sin_done"], 4)
            tt(c, t1, t1, ALU.mult)
            step.settle()
            ts(c, c, -2.0, 1.0, ALU.mult, ALU.add)
            step.settle()

            def normalise(cc, ss):
                tt(t0, cc, cc, ALU.mult)
                tt(t1, ss, ss, ALU.mult)
                step.settle()
                tt(t0, t0, t1, ALU.add)
                step.settle()
                ts(t0, t0, -0.5, 1.5, ALU.mult, ALU.add)
                step.settle()
                tt(cc, cc, t0, ALU.mult)
                tt(ss, ss, t0, ALU.mult)
                step.settle()

            normalise(c, sn)
            Wp = [(wc[:, lv * PAIRS:(lv + 1) * PAIRS], ws[:, lv * PAIRS:(lv + 1) * PAIRS]) for lv in range(LEVELS + 1)]
            step.did(dve.tensor_copy(Wp[0][0], c))
            step.did(dve.tensor_copy(Wp[0][1], sn))
            step.settle()
            for lv in range(1, LEVELS + 1):
                (pc, ps_), (qc, qs) = Wp[lv - 1], Wp[lv]
                tt(t0, pc, pc, ALU.mult)
                tt(t1, ps_, ps_, ALU.mult)
                stt(qs, pc, 2.0, ps_, ALU.mult, ALU.mult)
                step.settle()
                tt(qc, t0, t1, ALU.subtract)
                step.settle()
                normalise(qc, qs)
            tt(t0, rho, c, ALU.mult)
            tt(t1, rho, sn, ALU.mult)
            tt(t2, lr, lr, ALU.mult)
            tt(th, li, li, ALU.mult)
            step.settle()
            ts(t0, t0, -1.0, None, ALU.add)
            tt(t2, t2, th, ALU.add)
            step.settle()
            step.did(dve.reciprocal(t2, t2))
            tt(fr, t0, lr, ALU.mult)
            tt(th, t1, li, ALU.mult)
            tt(fi, t1, lr, ALU.mult)
            tt(c, t0, li, ALU.mult)
            step.settle()
            tt(fr, fr, th, ALU.add)
            tt(fi, fi, c, ALU.subtract)
            step.settle()
            tt(fr, fr, t2, ALU.mult)
            step.settle()
            dve.tensor_tensor(fi, fi, t2, ALU.mult).then_inc(s["trig_set"], 1)
            dve.wait_ge(s["trig_set"], 1)
            dve.wait_ge(s["const_set"], 9)

            def pre(b, q, turn):
                dve.wait_ge(s[f"bc_in{q}"], turn * 96 + 96)
                if not first(turn):
                    dve.wait_ge(s["pair_done"], (b - 1) * CHB)
                br, bi = (braw[q][r].rearrange("p (j c) -> p j c", j=CHB) for r in range(2))
                m = [bmul[k].rearrange("p (j c) -> p j c", j=CHB) for k in range(4)]
                frb = fr[:, bass.ds(b * CHB, CHB)].unsqueeze(2).to_broadcast([P, CHB, GROUP])
                fib = fi[:, bass.ds(b * CHB, CHB)].unsqueeze(2).to_broadcast([P, CHB, GROUP])
                tt(m[0], br, frb, ALU.mult)
                tt(m[1], bi, fib, ALU.mult)
                tt(m[2], br, fib, ALU.mult)
                tt(m[3], bi, frb, ALU.mult)
                step.settle()
                for r, op in ((0, ALU.subtract), (1, ALU.add)):
                    o4 = bbd[q][r].rearrange("p (j c) -> p j c", j=CHB)
                    for g in range(2):
                        pp = slice(64 * g, 64 * g + 64)
                        dve.tensor_tensor(o4[pp, :, GROUP * g:GROUP * g + GROUP], m[2 * r][pp], m[2 * r + 1][pp],
                                          op).then_inc(s["bbar_set"], 1)
                dve.tensor_scalar(cbd[q][1], cbd[q][1], -1.0, None, ALU.mult).then_inc(s["c_negated"], 1)
                dve.tensor_scalar(dgD[q], ident[:, :], dsk[:, bass.ds(b, 1)], None, ALU.mult).then_inc(s["bbar_set"], 1)
                dve.wait_ge(s["bbar_set"], b * 7 + 5)
                wcb, wsb = (w[:, bass.ds(LEVELS * PAIRS + b * CHB, CHB)].unsqueeze(2).to_broadcast([P, CHB, 2 * GROUP]) for w in (wc, ws))
                x0, x1 = (bbd[q][r].rearrange("p (j c) -> p j c", j=CHB) for r in range(2))
                for k, (x, w) in enumerate(((x0, wcb), (x1, wsb), (x1, wcb), (x0, wsb))):
                    tt(btmp[k].rearrange("p (j c) -> p j c", j=CHB), x, w, ALU.mult)
                step.settle()
                dve.tensor_tensor(bbd[q][2], btmp[0], btmp[1], ALU.add).then_inc(s["bbar_set"], 1)
                dve.tensor_tensor(bbd[q][3], btmp[2], btmp[3], ALU.subtract).then_inc(s["bbar_set"], 1)

            def segments(x):
                return x.rearrange("p (g t) -> p g t", g=2)

            def table(q, r, j):
                return tab[q][r][:, j * SEG:(j + 1) * SEG].unsqueeze(1).to_broadcast([P, 2, SEG])

            def turn_in(b, q, j, behind):
                if j == 0:
                    dve.wait_ge(s["tables_set"], 2 * (b + 1))
                k = 2 * (j % 2)
                dve.wait_ge(s["bu_full"], b * CHB + (j + 1))
                step.settle(behind)
                tt(segments(rot[0]), segments(bank(k)), table(q, 0, j), ALU.mult)
                tt(segments(rot[1]), segments(bank(k + 1)), table(q, 1, j), ALU.mult)
                tt(segments(rot[2]), segments(bank(k + 1)), table(q, 0, j), ALU.mult)
                dve.tensor_tensor(segments(rot[3]), segments(bank(k)), table(q, 1, j), ALU.mult).then_inc(s["bu_read"], 1)

            def add_up(b, q, j, behind):
                step.settle(behind)
                dve.wait_ge(s["bu_read"], b * CHB + (j + 1))
                tt(vin[j % 2][0], rot[0], rot[1], ALU.add)
                tt(vin[j % 2][1], rot[2], rot[3], ALU.subtract)

            def scan(b, j, behind):
                step.settle(behind)
                if not (first(b) and j == 0):
                    dve.wait_ge(s["prods_set"], b * CHB + j)
                decay = rho[:, bass.ds(b * CHB + j, 1)].to_broadcast([P, T])
                for r in range(2):
                    step.did(dve.tensor_tensor_scan(sc_r[r], decay, vin[j % 2][r], 0.0, ALU.mult, ALU.add))

            def turn_out(b, q, j, behind):
                step.settle(behind)
                if not (first(b) and j < 2):
                    dve.wait_ge(s["pair_done"], b * CHB + (j - 1))
                pr = [segments(x) for x in prod[j % 2]]
                x = [segments(sc_r[r]) for r in range(2)]
                tt(pr[0], x[0], table(q, 0, j), ALU.mult)
                stt(pr[1], x[1], -1.0, table(q, 1, j), ALU.mult, ALU.mult)
                tt(pr[2], x[0], table(q, 1, j), ALU.mult)
                dve.tensor_tensor(pr[3], x[1], table(q, 0, j), ALU.mult).then_inc(s["prods_set"], 1)

            def main(b, q, turn=None, last=False):
                for j in range(CHB):
                    nb, nq, nj = (b, q, j + 1) if j < CHB - 1 else (b + 1, 1 - q, 0)
                    more = not (last and j == CHB - 1)
                    if more:
                        turn_in(nb, nq, nj, 0 if first(b) and j == 0 else 3)
                    scan(b, j, 3 if more else 0)
                    if more:
                        add_up(nb, nq, nj, 2)
                    turn_out(b, q, j, 2 if more else 0)
                    if turn is not None and j == 0:
                        pre(b + 1, 1 - q, turn)

            pre(0, 0, 0)
            pre(1, 1, 0)
            turn_in(0, 0, 0, 0)
            add_up(0, 0, 0, 0)
            main(0, 0)
            per_pre, per_main = 4 + 4, 3 + 2 + 2 + 3
            with step.loop(KC // 2 - 1, 2 * (per_pre + CHB * per_main)) as it:
                main(2 * it + 1, 1, it + 1)
                main(2 * it + 2, 0, it + 1)
            main(KC - 1, 1, last=True)

            dve.wait_ge(s["h_in"], 16)
            gates_seen = [0]

            def gated(other, sg, tb, n0, keep):
                gates_seen[0] += 1
                dve.wait_ge(s["gate_sig"], gates_seen[0])
                dve.wait_ge(s["lin_full"], TILE[other] + 1)
                tt(sg, sg, bank(TILE[other] % 4), ALU.mult)
                step.settle()
                dve.scalar_tensor_tensor(out=hb(tb, n0), in0=hb(tb, n0), scalar=keep, in1=sg, op0=ALU.mult,
                                         op1=ALU.add).then_inc(s["lin_free"], 2)

            for n0 in range(2):
                for tb in range(HB):
                    gated(("glu", n0, tb, 0), sgm[tb % 2], tb, n0, ALPHA)
            dve.wait_ge(s["lin_free"], TILE["glu", 1, HB - 1, 1] + 1)

            lns = [0]
            loads = [0]

            def layer_norm(what, tbs, dst, base, last):
                a0, n = tbs[0], len(tbs)
                for tb in tbs:
                    for n0 in range(2):
                        step.did(dve.bn_stats(stat[:, (2 * tb + n0) * 6:(2 * tb + n0 + 1) * 6], hb(tb, n0)))
                step.settle()
                for tb in tbs:
                    step.did(dve.bn_aggr(mv[:, 2 * tb:2 * tb + 2], stat[:, 12 * tb:12 * tb + 12]))
                step.settle()
                rs = rstd[:, a0:a0 + n]
                lns[0] += 1
                dve.tensor_scalar(rs, mv[:, :].rearrange("p (b m) -> p b m", m=2)[:, a0:a0 + n, 1], LN_EPS, None,
                                  ALU.add).then_inc(s["var_set"], 1)
                dve.wait_ge(s["std_set"], lns[0])
                step.did(dve.reciprocal(rs, rs))
                step.settle()
                dve.wait_ge(s["ln_in"], 32 * (loads[0] + 1))

                def d(tb):
                    return dst[:, (tb - base) * D:(tb - base + 1) * D]

                for tb in tbs:
                    ts(d(tb), hb(tb), mv[:, 2 * tb:2 * tb + 1], rstd[:, tb:tb + 1], ALU.subtract, ALU.mult)
                step.settle()
                for tb in tbs:
                    tt(d(tb), d(tb), lnp[:, 0:D], ALU.mult)
                step.settle()
                for tb in tbs:
                    dve.tensor_tensor(d(tb), d(tb), lnp[:, D:2 * D], ALU.add).then_inc(s["h_set"], 1)
                dve.wait_ge(s["h_set"], H[what + (tbs[-1],)])
                if last:
                    loads[0] += 1
                    dve.sem_inc(s["lnp_free"], 1)

            def norm_steps(what, hf, dst, base, last=True):
                for tb in range(HB * hf, HB * hf + HB):
                    layer_norm(what, [tb], dst, base, last and tb % HB == HB - 1)
                    yield

            def nothing(n):
                for _ in range(n):
                    yield

            def route(l, hf):
                seq = 2 * l + hf
                yield from nothing(3)
                for hh in range(PH):
                    e = hh % 2
                    dve.wait_ge(s["scores_full"], seq * PH + hh + 1)
                    todo = [(tb, sd) for tb in range(HB) for sd in range(2)]

                    def S(tb, sd):
                        return ps[:, 4 + e, (sd * HB + tb) * P:(sd * HB + tb + 1) * P]

                    def kv8(tb, sd, c):
                        return val[sd][:, tb * TOPK + 8 * c:tb * TOPK + 8 * c + 8]

                    def ki8(tb, sd, c):
                        o = tb * SLOTS + hh * TOPK + 8 * c
                        return key[sd][:, o:o + 8].bitcast(U32)

                    def bv8(t, tb, c):
                        o = tb * SLOTS + hh * TOPK + 8 * c
                        return t[:, o:o + 8]

                    for tb, sd in todo:
                        step.did(dve.max(kv8(tb, sd, 0), S(tb, sd)))
                    step.settle()
                    for tb, sd in todo:
                        step.did(dve.max_index(ki8(tb, sd, 0), kv8(tb, sd, 0), S(tb, sd)))
                    for tb, sd in todo:
                        i = dve.match_replace(rest[2 * tb + sd], kv8(tb, sd, 0), S(tb, sd), LOWEST)
                        if (tb, sd) != todo[-1]:
                            step.did(i)
                    i.then_inc(s["scores_read"], 1)
                    step.settle()
                    dve.wait_ge(s["scores_read"], seq * PH + hh + 1)
                    for tb, sd in todo:
                        step.did(dve.max(kv8(tb, sd, 1), rest[2 * tb + sd]))
                    step.settle()
                    for tb, sd in todo:
                        step.did(dve.max_index(ki8(tb, sd, 1), kv8(tb, sd, 1), rest[2 * tb + sd]))
                    yield
                    for tb in range(HB):
                        v1 = val[0][:, tb * TOPK:(tb + 1) * TOPK].unsqueeze(2).to_broadcast([P, TOPK, TOPK])
                        v2 = val[1][:, tb * TOPK:(tb + 1) * TOPK].unsqueeze(1).to_broadcast([P, TOPK, TOPK])
                        tt(cand[tb].rearrange("p (i j) -> p i j", i=TOPK), v1, v2, ALU.add)
                    step.settle()
                    for tb in range(HB):
                        step.did(dve.max(bv8(best, tb, 0), cand[tb]))
                    step.settle()
                    for tb in range(HB):
                        step.did(dve.max_index(bv8(bpos, tb, 0).bitcast(U32), bv8(best, tb, 0), cand[tb]))
                        step.did(dve.match_replace(cand2[tb], bv8(best, tb, 0), cand[tb], LOWEST))
                    step.settle()
                    for tb in range(HB):
                        step.did(dve.max(bv8(best, tb, 1), cand2[tb]))
                    step.settle()
                    for tb in range(HB):
                        step.did(dve.max_index(bv8(bpos, tb, 1).bitcast(U32), bv8(best, tb, 1), cand2[tb]))
                    if hh < PH - 1:
                        yield
                step.settle()
                gs = gates[:, HB * hf * SLOTS:HB * (hf + 1) * SLOTS]
                b3 = best.rearrange("p (n k) -> p n k", k=TOPK)
                g3 = gs.rearrange("p (n k) -> p n k", k=TOPK)
                dve.tensor_tensor(g3, b3, b3[:, :, 0:1].to_broadcast([P, HB * PH, TOPK]), ALU.subtract).then_inc(s["gap_set"], 1)
                bu = bpos.bitcast(U32)
                step.did(dve.tensor_scalar(ksel[0].bitcast(U32), bu, 4, None, ALU.logical_shift_right))
                step.did(dve.tensor_scalar(ksel[1].bitcast(U32), bu, 15, None, ALU.bitwise_and))
                for sd in range(2):
                    step.did(dve.tensor_copy(key[sd], key[sd].bitcast(U32)))
                step.settle()
                for sd in range(2):
                    step.did(dve.tensor_copy(ksel[sd], ksel[sd].bitcast(U32)))
                step.settle()
                yield
                for tb in range(HB):
                    cols = slice(tb * SLOTS, (tb + 1) * SLOTS)
                    for sd in range(2):
                        tt(eq.rearrange("p (n j) -> p n j", j=TOPK), ksel[sd][:, cols].unsqueeze(2).to_broadcast([P, SLOTS, TOPK]),
                           iota16[:, :].unsqueeze(1).to_broadcast([P, SLOTS, TOPK]), ALU.is_equal)
                        step.settle()
                        e4 = eq.rearrange("p (h k j) -> p h k j", h=PH, k=TOPK)
                        k4 = key[sd][:, cols].rearrange("p (h j) -> p h j", h=PH).unsqueeze(2).to_broadcast([P, PH, TOPK, TOPK])
                        tt(e4, e4, k4, ALU.mult)
                        step.settle()
                        step.did(dve.tensor_reduce(esel[sd], eq.rearrange("p (n j) -> p n j", j=TOPK), AX_X, ALU.add))
                        step.settle()
                        if sd == 0:
                            yield
                    stt(esel[0], esel[0], float(NKEYS), esel[1], ALU.mult, ALU.add)
                    step.settle()
                    o = (HB * hf + tb) * SLOTS
                    dve.tensor_scalar(idx[:, o:o + SLOTS], esel[0], float(l * EXPERTS), None, ALU.add).then_inc(s["idx_set"], 1)
                    yield
                dve.wait_ge(s["gap_exp"], seq + 1)
                step.did(dve.tensor_reduce(rsum, g3, AX_X, ALU.add))
                step.settle()
                step.did(dve.reciprocal(rinv, rsum))
                step.settle()
                dve.tensor_tensor(g3, g3, rinv.unsqueeze(2).to_broadcast([P, HB * PH, TOPK]), ALU.mult).then_inc(s["routed"], 1)
                yield

            def ple(l, hf):
                yield from norm_steps(("ffn", l), hf, h, 0, last=l == 0)
                yield from nothing(HB)
                for n0 in range(2):
                    for tb in range(HB):
                        gated(("pw", l, hf, n0, tb), sgp[tb % 2], HB * hf + tb, n0, 1.0)
                        if n0 == 1 and tb == HB - 1:
                            dve.wait_ge(s["lin_free"], TILE["pw", l, hf, 1, tb] + 1)
                            dve.sem_inc(s["h_set"], HB)
                        yield

            def ple_block(l, tb):
                layer_norm(("ffn", l), [tb], h, 0, tb == TB - 1)
                yield
                yield
                for n0 in range(2):
                    gated(("pw", l, 1, n0, tb), sgp[n0], tb, n0, 1.0)
                    if n0 == 1:
                        dve.wait_ge(s["lin_free"], TILE["pw", l, 1, n0, tb] + 1)
                        dve.sem_inc(s["h_set"], 1)
                    yield

            def attention(hf):
                for hd in range(0, HEADS, 2):
                    yield
                    for e in range(2):
                        x, w = sp_[e], ZW[hf]
                        zf = ps[:, 2 * e:2 * e + 2, :].rearrange("p b n -> p (b n)")[:, 0:w]
                        dve.wait_ge(s["z_exp"], 3 * (hf * HEADS + hd + e) + 3)
                        stt(x[:, 0:w], zf, 0.0, ez[e][:, 0:w], ALU.max, ALU.add)
                        step.settle()
                        for kb in range(HB * hf, HB * hf + HB):
                            v = x[:, strip_at(hf, kb):strip_at(hf, kb) + P]
                            dve.tensor_tensor(v, v, seen[:, :], ALU.mult).then_inc(s["soft_set"], 1)
                    yield
                    yield
                yield

            def between_layers(hf):
                yield from ple(0, hf)
                yield from norm_steps(("kv", 1), hf, hk, HB * hf)
                yield from nothing(2 * HB + 4 + 4 + 4)
                yield from attention(hf)
                for n0 in range(2):
                    for tb in range(HB):
                        t = TILE["o", hf, n0, tb]
                        dve.wait_ge(s["lin_full"], t + 1)
                        x = hb(HB * hf + tb, n0)
                        dve.scalar_tensor_tensor(out=x, in0=x, scalar=ALPHA, in1=bank(t % 4), op0=ALU.mult,
                                                 op1=ALU.add).then_inc(s["lin_free"], 1)
                        if n0 == 1 and tb == HB - 1:
                            dve.wait_ge(s["lin_free"], t + 1)
                        yield
                yield from norm_steps(("mix", 1), hf, h, 0)
                yield from nothing(HB)
                yield from route(1, hf)

            def ffn_sum(k):
                dve.wait_ge(s["ffn_full"], k + 1)
                dve.scalar_tensor_tensor(out=hb(k % TB), in0=hb(k % TB), scalar=ALPHA,
                                         in1=ps[:, 6:8, :].rearrange("p b n -> p (b n)"), op0=ALU.mult,
                                         op1=ALU.add).then_inc(s["ffn_read"], 1)
                dve.wait_ge(s["ffn_read"], k + 1)

            def group(l, tb, n, g, j=0):
                dve.wait_ge(s["diag_set"], n + 4 + j * TURN)
                for r in range(4):
                    q = (4 * g + r) % RING
                    dve.wait_ge(u_in[q], 16 * ((n + r) // RING + 1) + j * 16 * (TURN // RING))
                    c = (4 * g + r) % TURN
                    dve.tensor_tensor_reduce(u_ring[q], u_ring[q], hb(tb), 1.0, 0.0, ALU.mult, ALU.add,
                                             actv[:, c:c + 1]).then_inc(s["u_used"], 1)
                if isinstance(j, int) and g == 0 and n > 0:
                    ffn_sum(n // SLOTS - 1)

            def block_loop(l, tb):
                n = (l * TB + tb) * SLOTS
                for g in range(4):
                    group(l, tb, n + 4 * g, g)
                with dve.Fori(1, SLOTS // TURN) as j:
                    for g in range(4):
                        group(l, tb, n + 4 * g, g, j)

            def side_gated(p):
                n0, tb = SIDE[p]
                dve.wait_ge(s["side_sig"], p + 1)
                dve.wait_ge(s["side_full"], 2 * p + 2)
                tt(sgm[p % 2], sgm[p % 2], bank(6), ALU.mult)
                step.settle()
                dve.scalar_tensor_tensor(out=hb(tb, n0), in0=hb(tb, n0), scalar=ALPHA, in1=sgm[p % 2], op0=ALU.mult,
                                         op1=ALU.add).then_inc(s["side_free"], 1)

            def beside_route(n):
                if n in SIDE_STEPS and SIDE_STEPS[n][1] == 1:
                    side_gated(SIDE_STEPS[n][0])

            def first_route(hf):
                if hf == 1:
                    dve.wait_ge(s["side_free"], len(SIDE))
                    yield from norm_steps(("mix", 0), hf, h, 0)
                yield from nothing(HB)
                yield from route(0, hf)

            dve.sem_inc(s["u_used"], RING)
            layer_norm(("mix", 0), list(range(HB)), h, 0, False)
            side_gated(0)
            dve.wait_ge(s["tri_set"], 8)
            step.did(dve.tensor_copy(iota16[:, :], iota16[:, :].bitcast(U32)))
            alone(STEPS_FIRST[0], first_route(0), beside_route)
            weave(0, [0], group, STEPS_FIRST[1], first_route(1), 1)
            block_loop(0, 1)
            weave(0, [2, 3], group, STEPS_BETWEEN, between_layers(0), 1)
            weave(1, [0, 1], group, STEPS_BETWEEN, between_layers(1), 1)
            weave(1, [2], group, STEPS_PLE, ple(1, 0), 1)
            weave(1, [HB + 1], group, STEPS_PLE_BLOCK, ple_block(1, HB), 1)
            ffn_sum(DEPTH * TB - 1)
            alone(STEPS_PLE_BLOCK, ple_block(1, HB + 1))

        @block.gpsimd
        def _(pool):
            step = Steps(pool, s["pool_step"])
            step.did(pool.memset(ident[:, :], 0.0))
            for q in range(2):
                for r in range(2):
                    pool.memset(bbd[q][r], 0.0).then_inc(s["const_set"], 1)
                    pool.memset(cbd[q][r], 0.0).then_inc(s["const_set"], 1)
            step.settle()
            pool.affine_select(out=ident[:, :], in_=ident[:, :], compare_op=ALU.not_equal, fill=1.0, base=0,
                               pattern=[[-1, P]], channel_multiplier=1).then_inc(s["const_set"], 1)

            pool.iota(iota16[:, :].bitcast(U32), pattern=[[1, TOPK]], base=0, channel_multiplier=0).then_inc(s["tri_set"], 1)
            pool.memset(zrow[:, :], 0.0).then_inc(s["tri_set"], 1)
            pool.memset(nones[:, :], -1.0).then_inc(s["tri_set"], 1)
            pool.memset(ntri[:, :], -1.0).then_inc(s["tri_set"], 1)
            pool.memset(hide[:, :], 0.0).then_inc(s["tri_set"], 1)
            pool.memset(seen[:, :], 1.0).then_inc(s["tri_set"], 1)
            pool.wait_ge(s["tri_set"], 6)
            pool.affine_select(out=ntri[:, :], in_=ntri[:, :], compare_op=ALU.is_ge, fill=0.0, base=0,
                               pattern=[[-1, P]], channel_multiplier=1).then_inc(s["tri_set"], 1)
            pool.affine_select(out=seen[:, :], in_=seen[:, :], compare_op=ALU.is_gt, fill=0.0, base=0,
                               pattern=[[1, P]], channel_multiplier=-1).then_inc(s["tri_set"], 1)
            pool.affine_select(out=hide[:, :], in_=hide[:, :], compare_op=ALU.is_gt, fill=MASKED, base=0,
                               pattern=[[1, P]], channel_multiplier=-1).then_inc(s["tri_set"], 1)

            def tables(b, q, turn):
                if not first(turn):
                    pool.wait_ge(s["prods_set"], (b - 1) * CHB)
                if not first(b):
                    pool.wait_ge(s["tables_set"], 2 * b)
                c, sn = (tab[q][r].rearrange("p (j t) -> p j t", j=CHB) for r in range(2))
                tm = [ptmp[r].rearrange("p (j t) -> p j t", j=CHB) for r in range(2)]
                for lv in range(LEVELS):
                    n = 1 << lv
                    wcb = wc[:, bass.ds(lv * PAIRS + b * CHB, CHB)].unsqueeze(2).to_broadcast([P, CHB, n])
                    wsb = ws[:, bass.ds(lv * PAIRS + b * CHB, CHB)].unsqueeze(2).to_broadcast([P, CHB, n])
                    step.settle()
                    step.did(pool.tensor_tensor(c[:, :, n:2 * n], c[:, :, 0:n], wcb, ALU.mult))
                    step.did(pool.tensor_tensor(tm[0][:, :, 0:n], sn[:, :, 0:n], wsb, ALU.mult))
                    step.did(pool.tensor_tensor(sn[:, :, n:2 * n], sn[:, :, 0:n], wcb, ALU.mult))
                    step.did(pool.tensor_tensor(tm[1][:, :, 0:n], c[:, :, 0:n], wsb, ALU.mult))
                    step.settle()
                    i0 = pool.tensor_tensor(c[:, :, n:2 * n], c[:, :, n:2 * n], tm[0][:, :, 0:n], ALU.subtract)
                    i1 = pool.tensor_tensor(sn[:, :, n:2 * n], sn[:, :, n:2 * n], tm[1][:, :, 0:n], ALU.add)
                    if lv < LEVELS - 1:
                        step.did(i0)
                        step.did(i1)
                    else:
                        i0.then_inc(s["tables_set"], 1)
                        i1.then_inc(s["tables_set"], 1)

            def turn_c(b, q):
                pool.wait_ge(s["c_negated"], b + 1)
                wcb, wsb = (w[:, bass.ds(LEVELS * PAIRS + b * CHB, CHB)].unsqueeze(2).to_broadcast([P, CHB, 2 * GROUP]) for w in (wc, ws))
                x0, x1 = (cbd[q][r].rearrange("p (j c) -> p j c", j=CHB) for r in range(2))
                if not first(b):
                    pool.wait_ge(s["c_turned"], b * 2)
                for k, (x, w) in enumerate(((x0, wcb), (x1, wsb), (x1, wcb), (x0, wsb))):
                    step.did(pool.tensor_tensor(ctmp[k].rearrange("p (j c) -> p j c", j=CHB), x, w, ALU.mult))
                step.settle()
                pool.tensor_tensor(cbd[q][2], ctmp[0], ctmp[1], ALU.add).then_inc(s["c_turned"], 1)
                pool.tensor_tensor(cbd[q][3], ctmp[2], ctmp[3], ALU.subtract).then_inc(s["c_turned"], 1)

            for q in range(2):
                for r in range(2):
                    step.did(pool.memset(tab[q][r].rearrange("p (j t) -> p j t", j=CHB)[:, :, 0:1], 1.0 - r))
            pool.wait_ge(s["trig_set"], 1)
            tables(0, 0, 0)
            turn_c(0, 0)
            tables(1, 1, 0)
            turn_c(1, 1)
            with step.loop(KC // 2 - 1, 2 * (6 * LEVELS - 2 + 4)) as it:
                tables(2 * it + 2, 0, it + 1)
                turn_c(2 * it + 2, 0)
                tables(2 * it + 3, 1, it + 1)
                turn_c(2 * it + 3, 1)

            def gather(l, tb):
                done = (l * TB + tb) * SLOTS
                pool.wait_ge(s["idx_set"], l * TB + tb + 1)
                if done == 0:
                    pool.wait_ge(s["side_full"], 2 * len(SIDE))
                with step.loop(SLOTS // TURN, 2) as j:
                    for half in range(2):
                        mine = stage_idx[:, half * RING:(half + 1) * RING]
                        step.did(pool.tensor_copy(mine, idx[:, bass.ds(j * TURN + (tb * SLOTS + half * RING), RING)]))
                        reg_wait(pool, s["pool_step"], step.base + step.n)
                        for g in range(RING // 2):
                            n = done + half * RING + 2 * g + 2
                            reg_wait(pool, s["u_used"], j * TURN + n)
                            for r in range(2 * g, 2 * g + 2):
                                pool.indirect_dma_start(u_ring[r], None, a["peer_u"][:, :],
                                                        bass.IndirectOffsetOnAxis(mine[:, r:r + 1], 0)).then_inc(u_in[r], 16)
                            reg_wait(pool, s["v_used"], j * TURN + n)
                            for r in range(2 * g, 2 * g + 2):
                                pool.indirect_dma_start(v_ring[r], None, a["peer_v"][:, :],
                                                        bass.IndirectOffsetOnAxis(mine[:, r:r + 1], 0)).then_inc(v_in[r], 16)

            for l in range(DEPTH):
                for tb in range(TB):
                    gather(l, tb)

        @block.sync
        def _(sp):
            sp.dma_start(xT.rearrange("p (k t) -> p k t", k=KC),
                         a["xT"].rearrange("(k p) t -> p k t", p=P)).then_inc(s["xT_in"], 16)
            for n, key in (("lr", "lam_re"), ("li", "lam_im")):
                sp.dma_start(par[n], a[key]).then_inc(s["par_in"], 16)
            for g in range(2):
                sp.dma_start(par["dt"][64 * g:64 * g + 64, :],
                             a["log_dt"][g:g + 1, :].to_broadcast([64, PAIRS])).then_inc(s["par_in"], 16)
            sp.dma_start(dsk, a["d_skip"]).then_inc(s["par_in"], 16)

            def pre(b, q, turn):
                if not first(turn):
                    sp.wait_ge(s["u_full"], b - 1)
                sp.dma_start(win[q].rearrange("p (k n) -> p k n", k=KC),
                             a["w_in"][:, bass.ds(b * P, P)].rearrange("(k p) n -> p k n", p=P)).then_inc(s[f"win_in{q}"], 16)
                if not first(turn):
                    sp.wait_ge(s["pair_done"], (b - 1) * CHB)
                for r, (bn, cn) in enumerate((("b_re", "c_re"), ("b_im", "c_im"))):
                    sp.dma_start(braw[q][r], a[bn][:, bass.ds(b * CHB * GROUP, CHB * GROUP)]).then_inc(s[f"bc_in{q}"], 16)
                    for g in range(2):
                        sp.dma_start(cbd[q][r][64 * g:64 * g + 64, :].rearrange("p (j c) -> p j c", j=CHB)[:, :, GROUP * g:GROUP * g + GROUP],
                                     a[cn][64 * g:64 * g + 64, bass.ds(b * CHB * GROUP, CHB * GROUP)].rearrange(
                                         "p (j c) -> p j c", j=CHB)).then_inc(s[f"bc_in{q}"], 16)

            sp.wait_ge(s["const_set"], 9)
            pre(0, 0, 0)
            pre(1, 1, 0)
            sp.dma_start(h[:, :].rearrange("p (b d) -> p b d", b=TB),
                         a["x"].rearrange("(b p) d -> p b d", p=P)).then_inc(s["h_in"], 16)
            for n in range(2):
                sp.dma_start(lnp[:, n * D:(n + 1) * D], a[("ln_mix_g", "ln_mix_b")[n]][0:1, :].to_broadcast([P, D])).then_inc(s["ln_in"], 16)

            def load_piece(n):
                if n >= WSLOTS:
                    sp.wait_ge(s["lin_full"], FREE_AT[n - WSLOTS])
                slot = n % WSLOTS
                sp.dma_start(wring[:, slot * KC * HALF:(slot + 1) * KC * HALF].rearrange("p (k n) -> p k n", k=KC),
                             w_plan[n]).then_inc(s[f"w_in{slot}"], 16)

            def load_ln(n):
                name, l = LN_LOADS[n]
                sp.wait_ge(s["lnp_free"], n)
                for m, x in enumerate("gb"):
                    sp.dma_start(lnp[:, m * D:(m + 1) * D],
                                 a[f"{name}_{x}"][l:l + 1, :].to_broadcast([P, D])).then_inc(s["ln_in"], 16)

            def load_keys(l):
                if l > 0:
                    sp.wait_ge(s["scores_full"], 2 * l * PH)
                for m, x in enumerate(("k1T", "k2T")):
                    sp.dma_start(k12s[:, m * NKEYS:(m + 1) * NKEYS], a[x][l * P:(l + 1) * P, :]).then_inc(s["k_in"], 16)

            def load_embedding(l, hf):
                if (l, hf) == (1, 1):
                    sp.wait_ge(s["h_set"], H["ple", 1, HB - 1])
                else:
                    sp.wait_ge(s["routed"], 2 * l + hf + 2)
                sp.dma_start(plw.rearrange("p (k n) -> p k n", k=2),
                             a["ple_w"][l * PLE:(l + 1) * PLE, :].rearrange("(k p) n -> p k n", p=P)).then_inc(s["ple_in"], 16)
                sp.dma_start(pTs.rearrange("p (k n) -> p k n", k=2),
                             a["pT"][l].rearrange("(k p) n -> p k n", p=P)[:, :, hf * TH:(hf + 1) * TH]).then_inc(s["ple_in"], 16)

            for n in range(WSLOTS):
                load_piece(n)
            load_keys(0)
            with sp.Fori(0, KC // 2 - 1) as it:
                pre(2 * it + 2, 0, it + 1)
                pre(2 * it + 3, 1, it + 1)
            sp.wait_ge(s["y_taken"], KC + 1)
            for n0 in (1, 0):
                for g in range(2):
                    c0 = g * D + n0 * HALF
                    sp.dma_start(glu_w[n0][g].rearrange("p (k n) -> p k n", k=KC),
                                 a["w_glu"][:, c0:c0 + HALF].rearrange("(k p) n -> p k n", p=P)).then_inc(s[f"glu_w_in{n0}"], 16)
            also = {W["pq", 0, 1][1]: [(load_ln, 1)]}
            for hf in range(2):
                also[W["pg", 0, hf][1]] = [(load_embedding, 0, hf), (load_ln, 2 + 3 * hf)]
                also[W["v", hf][1]] = [(load_ln, 3 + 3 * hf)]
                also[W["pq", 1, hf][1]] = [(load_keys, 1)] * (1 - hf) + [(load_ln, 4 + 3 * hf)]
                also[W["pg", 1, hf][1]] = [(load_embedding, 1, hf)]
            for n in range(WSLOTS, len(w_plan)):
                load_piece(n)
                for load, *args in also.get(n, ()):
                    load(*args)


def kernel(**inputs):
    import numpy as _np
    import concourse.bacc as _bacc
    from concourse import mybir as _mybir
    from concourse.bass_utils import run_bass_kernel_spmd as _run

    v = {k: _np.asarray(x) for k, x in inputs.items()}

    def by_state(x):
        x = x.reshape((PAIRS, 2, 64) + x.shape[2:])
        x = _np.moveaxis(x, 0, 2)
        return x.reshape(P, -1)

    arrays = {
        "x": v["x"][0], "xT": v["x"][0].T, "pT": v["p"][:, 0].transpose(0, 2, 1),
        "lam_re": by_state(v["ssm_lam_re"][0]), "lam_im": by_state(v["ssm_lam_im"][0]),
        "log_dt": v["ssm_log_dt"][0].reshape(PAIRS, 2).T,
        "b_re": by_state(v["ssm_b_re"][0]), "b_im": by_state(v["ssm_b_im"][0]),
        "c_re": by_state(v["ssm_c_re"][0].transpose(0, 2, 1)), "c_im": by_state(v["ssm_c_im"][0].transpose(0, 2, 1)),
        "d_skip": v["ssm_d"][0].reshape(KC, P).T, "w_in": v["ssm_w_in"][0], "w_glu": v["ssm_w_glu"][0],
        "ln_mix_g": v["ln_mix_g"], "ln_mix_b": v["ln_mix_b"], "ln_ffn_g": v["ln_ffn_g"], "ln_ffn_b": v["ln_ffn_b"],
        "kv_g": v["kv_ln_g"][None], "kv_b": v["kv_ln_b"][None],
        "w_kv": v["w_kv"], "w_q": v["sb_w_q"][0], "w_o": v["sb_w_o"][0],
        "peer_w_q": v["peer_w_q"].reshape(DEPTH * D, PH * 256),
        "k1T": v["peer_k1"].transpose(0, 2, 1).reshape(DEPTH * P, NKEYS),
        "k2T": v["peer_k2"].transpose(0, 2, 1).reshape(DEPTH * P, NKEYS),
        "peer_u": v["peer_u"].reshape(DEPTH * EXPERTS, D), "peer_v": v["peer_v"].reshape(DEPTH * EXPERTS, D),
        "ple_w": v["ple_w"].reshape(DEPTH * PLE, D), "ple_gate": v["ple_gate"].reshape(DEPTH * D, D),
    }
    nc = _bacc.Bacc("TRN2", target_bir_lowering=False, num_devices=1)
    feeds, aps = {}, {}
    for name, x in arrays.items():
        x = _np.ascontiguousarray(x)
        feeds[f"in_{name}"] = x
        aps[name] = nc.dram_tensor(f"in_{name}", x.shape, _mybir.dt.from_np(x.dtype), kind="ExternalInput").ap()
    out = nc.dram_tensor("out", (T, D), _mybir.dt.float32, kind="ExternalOutput").ap()
    build(nc, aps, out)
    r = _run(nc, [feeds], core_ids=[0])
    return r.results[0]["out"].reshape(1, T, D)
```
